# Optimizing a Trainium2 kernel written in Bass

```python
import jax, jax.numpy as jnp
from jax import lax
import numpy as np

D_MODEL = 1024
BATCH = 1
SEQ = 256
DEPTH = 1

N_MIXERS = 2
ATT_HEADS = 8
ATT_HEAD_DIM = D_MODEL // ATT_HEADS
MOBA_BLOCK = 256
MOBA_TOPK = 3
MOBA_QUERY_CHUNK = 32
MLSTM_HEADS = 8
MLSTM_DV = D_MODEL // MLSTM_HEADS
MLSTM_DQK = MLSTM_DV // 2
MLSTM_CHUNK = 64
GATE_SOFTCAP = 15.0
D_FF = 4 * D_MODEL
RMS_EPS = 1e-6
N_ATTN_LAYERS = (DEPTH + N_MIXERS - 1) // N_MIXERS
N_MLSTM_LAYERS = DEPTH // N_MIXERS


def rms_norm(x, gain):
    xf = x.astype(jnp.float32)
    y = xf * lax.rsqrt(jnp.mean(xf * xf, axis=-1, keepdims=True) + RMS_EPS)
    return (y * gain.astype(jnp.float32)).astype(x.dtype)

def alibi_slopes(n_heads):
    return jnp.exp2(-8.0 * jnp.arange(1, n_heads + 1, dtype=jnp.float32) / n_heads)

def soft_cap(z):
    return GATE_SOFTCAP * jnp.tanh(z / GATE_SOFTCAP)

def moba_attention(x, w_qkv, w_o):
    bsz, seq, _ = x.shape
    H, dh, blk, qlen = ATT_HEADS, ATT_HEAD_DIM, MOBA_BLOCK, MOBA_QUERY_CHUNK
    f32 = jnp.float32
    q, k, v = jnp.split(x @ w_qkv, 3, axis=-1)

    def to_heads(t):
        return t.reshape(bsz, seq, H, dh).transpose(0, 2, 1, 3)

    q = to_heads(q) * (dh ** -0.5)
    k = to_heads(k)
    v = to_heads(v)
    n_blk = -(-seq // blk)
    pad = n_blk * blk - seq
    k_blk = jnp.pad(k, ((0, 0), (0, 0), (0, pad), (0, 0))).reshape(bsz, H, n_blk, blk, dh)
    v_blk = jnp.pad(v, ((0, 0), (0, 0), (0, pad), (0, 0))).reshape(bsz, H, n_blk, blk, dh)

    k_mean = jnp.mean(k_blk.astype(f32), axis=3)
    gate = jnp.einsum('bhsd,bhnd->bhsn', q.astype(f32), k_mean)
    n_past = jnp.arange(seq) // blk
    is_past = jnp.arange(n_blk)[None, :] < n_past[:, None]
    gate = jnp.where(is_past, gate, -jnp.inf)
    top = min(MOBA_TOPK, n_blk)
    _, sel = lax.top_k(gate, top)
    sel = sel.astype(jnp.int32)

    n_chunk = seq // qlen
    q_c = jnp.moveaxis(q.reshape(bsz, H, n_chunk, qlen, dh), 2, 0)
    sel_c = jnp.moveaxis(sel.reshape(bsz, H, n_chunk, qlen, top), 2, 0)
    slopes = alibi_slopes(H)
    b_idx = jnp.arange(bsz)[:, None, None, None]
    h_idx = jnp.arange(H)[None, :, None, None]
    offs = jnp.arange(blk)

    def attend_chunk(args):
        c, q_blk, sel_blk = args
        t = c * qlen + jnp.arange(qlen)
        own = (c * qlen) // blk
        k_own = lax.dynamic_index_in_dim(k_blk, own, axis=2, keepdims=False)
        v_own = lax.dynamic_index_in_dim(v_blk, own, axis=2, keepdims=False)
        dist_own = (t[:, None] - (own * blk + offs)[None, :]).astype(f32)
        s_own = jnp.einsum('bhqd,bhkd->bhqk', q_blk, k_own).astype(f32) - slopes[:, None, None] * dist_own
        s_own = jnp.where(dist_own >= 0, s_own, -jnp.inf)
        k_sel = k_blk[b_idx, h_idx, sel_blk]
        v_sel = v_blk[b_idx, h_idx, sel_blk]
        dist_sel = (t[:, None, None] - (sel_blk[..., None] * blk + offs)).astype(f32)
        s_sel = jnp.einsum('bhqd,bhqjkd->bhqjk', q_blk, k_sel).astype(f32) - slopes[:, None, None, None] * dist_sel
        slot_ok = jnp.arange(top)[None, :] < (t // blk)[:, None]
        s_sel = jnp.where(slot_ok[:, :, None], s_sel, -jnp.inf)
        scores = jnp.concatenate([s_own, s_sel.reshape(bsz, H, qlen, top * blk)], axis=-1)
        p = jax.nn.softmax(scores, axis=-1).astype(v_blk.dtype)
        p_own = p[..., :blk]
        p_sel = p[..., blk:].reshape(bsz, H, qlen, top, blk)
        return (jnp.einsum('bhqk,bhkd->bhqd', p_own, v_own)
                + jnp.einsum('bhqjk,bhqjkd->bhqd', p_sel, v_sel))

    o = lax.map(attend_chunk, (jnp.arange(n_chunk), q_c, sel_c))
    o = o.transpose(1, 0, 3, 2, 4).reshape(bsz, seq, H * dh)
    return o @ w_o

def mlstm_chunkwise(q, k, v, log_i, log_f):
    bsz, H, seq, dqk = q.shape
    dv = v.shape[-1]
    L = MLSTM_CHUNK
    n_chunk = seq // L

    def chunks(t):
        return jnp.moveaxis(t.reshape(bsz, H, n_chunk, L, *t.shape[3:]), 2, 0)

    causal = jnp.tril(jnp.ones((L, L), dtype=bool))

    def step(carry, inp):
        C, n, m = carry
        qc, kc, vc, ic, fc = inp
        b = jnp.cumsum(fc, axis=-1)
        log_d = jnp.where(causal, b[..., :, None] - b[..., None, :] + ic[..., None, :], -jnp.inf)
        log_inter = b + m[..., None]
        m_t = jnp.maximum(log_inter, jnp.max(log_d, axis=-1))
        d = jnp.exp(log_d - m_t[..., None])
        w_inter = jnp.exp(log_inter - m_t)
        s = jnp.einsum('bhtd,bhsd->bhts', qc, kc) * d
        num = (w_inter[..., None] * jnp.einsum('bhtd,bhdv->bhtv', qc, C)
               + jnp.einsum('bhts,bhsv->bhtv', s, vc))
        den = w_inter * jnp.einsum('bhtd,bhd->bht', qc, n) + jnp.sum(s, axis=-1)
        h = num / jnp.maximum(jnp.abs(den), jnp.exp(-m_t))[..., None]
        b_end = b[..., -1]
        log_w = b_end[..., None] - b + ic
        m_new = jnp.maximum(b_end + m, jnp.max(log_w, axis=-1))
        decay = jnp.exp(b_end + m - m_new)
        w = jnp.exp(log_w - m_new[..., None])
        C = decay[..., None, None] * C + jnp.einsum('bhs,bhsd,bhsv->bhdv', w, kc, vc)
        n = decay[..., None] * n + jnp.einsum('bhs,bhsd->bhd', w, kc)
        return (C, n, m_new), h

    f32 = jnp.float32
    init = (jnp.zeros((bsz, H, dqk, dv), f32), jnp.zeros((bsz, H, dqk), f32), jnp.zeros((bsz, H), f32))
    _, h = lax.scan(step, init, (chunks(q), chunks(k), chunks(v), chunks(log_i), chunks(log_f)))
    return jnp.moveaxis(h, 0, 2).reshape(bsz, H, seq, dv)

def mlstm_mixer(x, w_in, b_gates, norm_h, w_out):
    bsz, seq, _ = x.shape
    H, dqk, dv = MLSTM_HEADS, MLSTM_DQK, MLSTM_DV
    f32 = jnp.float32
    proj = x @ w_in
    q, k, v, o_pre, gate_pre = jnp.split(
        proj, [H * dqk, 2 * H * dqk, 2 * H * dqk + H * dv, 2 * H * dqk + 2 * H * dv], axis=-1)

    def to_heads(t, dim):
        return t.reshape(bsz, seq, H, dim).transpose(0, 2, 1, 3).astype(f32)

    q = to_heads(q, dqk)
    k = to_heads(k, dqk) * (dqk ** -0.5)
    v = to_heads(v, dv)
    gates = soft_cap(gate_pre.astype(f32) + b_gates.astype(f32)).transpose(0, 2, 1)
    log_i = gates[:, :H]
    log_f = jax.nn.log_sigmoid(gates[:, H:])
    h = mlstm_chunkwise(q, k, v, log_i, log_f)
    h = h * lax.rsqrt(jnp.mean(h * h, axis=-1, keepdims=True) + RMS_EPS)
    h = h.transpose(0, 2, 1, 3).reshape(bsz, seq, H * dv) * norm_h.astype(f32)
    y = (jax.nn.sigmoid(o_pre.astype(f32)) * h).astype(x.dtype)
    return y @ w_out

def squared_relu_mlp(x, w_up, w_down):
    return jnp.square(jax.nn.relu(x @ w_up)) @ w_down

def first_inputs(seed: int = 0) -> dict:
    key = jax.random.key(seed)
    ks = jax.random.split(key, 16)
    f32 = jnp.float32

    def dense(k, shape):
        return jax.random.normal(k, shape, f32) * shape[-2] ** -0.5

    def gain(k, shape):
        return 1.0 + 0.05 * jax.random.normal(k, shape, f32)

    H = MLSTM_HEADS
    mlstm_in = 2 * H * MLSTM_DQK + 2 * H * MLSTM_DV + 2 * H
    i_bias = 0.1 * jax.random.normal(ks[13], (N_MLSTM_LAYERS, H), f32)
    f_bias = 3.0 + 0.5 * jax.random.normal(ks[14], (N_MLSTM_LAYERS, H), f32)
    return {
        "x": jax.random.normal(ks[0], (BATCH, SEQ, D_MODEL), f32),
        "norm_mix_pre": gain(ks[1], (DEPTH, D_MODEL)),
        "norm_mix_post": gain(ks[2], (DEPTH, D_MODEL)),
        "norm_ffn_pre": gain(ks[3], (DEPTH, D_MODEL)),
        "norm_ffn_post": gain(ks[4], (DEPTH, D_MODEL)),
        "w_up": dense(ks[5], (DEPTH, D_MODEL, D_FF)),
        "w_down": dense(ks[6], (DEPTH, D_FF, D_MODEL)),
        "attn_w_qkv": dense(ks[7], (N_ATTN_LAYERS, D_MODEL, 3 * ATT_HEADS * ATT_HEAD_DIM)),
        "attn_w_o": dense(ks[8], (N_ATTN_LAYERS, ATT_HEADS * ATT_HEAD_DIM, D_MODEL)),
        "mlstm_w_in": dense(ks[9], (N_MLSTM_LAYERS, D_MODEL, mlstm_in)),
        "mlstm_b_gates": jnp.concatenate([i_bias, f_bias], axis=-1),
        "mlstm_norm_h": gain(ks[10], (N_MLSTM_LAYERS, H * MLSTM_DV)),
        "mlstm_w_out": dense(ks[11], (N_MLSTM_LAYERS, H * MLSTM_DV, D_MODEL)),
    }

def first_block(x, norm_mix_pre, norm_mix_post, norm_ffn_pre, norm_ffn_post, w_up, w_down,
              attn_w_qkv, attn_w_o, mlstm_w_in, mlstm_b_gates, mlstm_norm_h, mlstm_w_out):
    h = x
    for layer in range(DEPTH):
        j = layer // N_MIXERS
        u = rms_norm(h, norm_mix_pre[layer])
        if layer % N_MIXERS == 0:
            u = moba_attention(u, attn_w_qkv[j], attn_w_o[j])
        else:
            u = mlstm_mixer(u, mlstm_w_in[j], mlstm_b_gates[j], mlstm_norm_h[j], mlstm_w_out[j])
        h = h + rms_norm(u, norm_mix_post[layer])
        u = squared_relu_mlp(rms_norm(h, norm_ffn_pre[layer]), w_up[layer], w_down[layer])
        h = h + rms_norm(u, norm_ffn_post[layer])
    return h


DEPTH_2 = 2

CHUNK = 64
Q_BLOCK = 128
HEAD_DIM = 64
CONV_WIDTH = D_MODEL // 2
LRU_WIDTH = D_MODEL // 2
CONV_GROUPS = CONV_WIDTH // HEAD_DIM
LRU_HEADS = LRU_WIDTH // HEAD_DIM
SHORT_CONV_K = 3
LRU_CONV_K = 4
RG_C = 8.0
SB_HEADS = D_MODEL // HEAD_DIM
D_FF_2 = ((8 * D_MODEL // 3 + 255) // 256) * 256
N_MOD = 6
EPS = 1e-6


def rms_norm_2(x, g):
    x32 = x.astype(jnp.float32)
    y = x32 * lax.rsqrt(jnp.mean(x32 * x32, axis=-1, keepdims=True) + EPS)
    return (y * g.astype(jnp.float32)).astype(x.dtype)

def ada_modulation(c, ada_w, ada_b):
    m = jax.nn.silu(c) @ ada_w + ada_b
    return jnp.split(m, N_MOD, axis=-1)

def modulate(h, shift, scale):
    return h * (1.0 + scale[:, None, :]) + shift[:, None, :]

def causal_depthwise_conv(x, w):
    k_width = w.shape[0]
    seq = x.shape[1]
    xp = jnp.pad(x, ((0, 0), (k_width - 1, 0), (0, 0)))
    y = xp[:, 0:seq] * w[0]
    for k in range(1, k_width):
        y = y + xp[:, k:k + seq] * w[k]
    return y

def rg_lru(xr, w_a, b_a, w_x, b_x, lam):
    bsz, seq, width = xr.shape
    n_blk, blk = w_a.shape[0], w_a.shape[1]
    x32 = xr.astype(jnp.float32)
    xh = x32.reshape(bsz, seq, n_blk, blk)
    r = jax.nn.sigmoid(jnp.einsum('bshi,hij->bshj', xh, w_a.astype(jnp.float32)) + b_a).reshape(bsz, seq, width)
    i = jax.nn.sigmoid(jnp.einsum('bshi,hij->bshj', xh, w_x.astype(jnp.float32)) + b_x).reshape(bsz, seq, width)
    log_a = -RG_C * r * jax.nn.softplus(-lam.astype(jnp.float32))
    a = jnp.exp(log_a)
    b = jnp.sqrt(-jnp.expm1(2.0 * log_a)) * (i * x32)
    n_chunks = seq // CHUNK
    a_c = a.reshape(bsz, n_chunks, CHUNK, width).transpose(1, 0, 2, 3)
    b_c = b.reshape(bsz, n_chunks, CHUNK, width).transpose(1, 0, 2, 3)

    def combine(lhs, rhs):
        al, bl = lhs
        ar, br = rhs
        return al * ar, ar * bl + br

    def chunk_step(h0, ab):
        a_k, b_k = ab
        a_cum, b_cum = lax.associative_scan(combine, (a_k, b_k), axis=1)
        h = a_cum * h0[:, None, :] + b_cum
        return h[:, -1], h

    h_init = jnp.zeros((bsz, width), jnp.float32)
    _, hs = lax.scan(chunk_step, h_init, (a_c, b_c))
    return hs.transpose(1, 0, 2, 3).reshape(bsz, seq, width)

def stick_breaking_attention(q, k, v):
    seq, dh = q.shape[2], q.shape[3]
    scale = dh ** -0.5
    outs = []
    for blk in range(seq // Q_BLOCK):
        q0, q1 = blk * Q_BLOCK, (blk + 1) * Q_BLOCK
        qb = q[:, :, q0:q1].astype(jnp.float32)
        kb = k[:, :, :q1].astype(jnp.float32)
        vb = v[:, :, :q1].astype(jnp.float32)
        z = jnp.einsum('bhqd,bhkd->bhqk', qb, kb) * scale
        q_pos = jnp.arange(q0, q1)[:, None]
        k_pos = jnp.arange(q1)[None, :]
        strict = k_pos < q_pos
        log_keep = jnp.where(strict, jax.nn.log_sigmoid(-z), 0.0)
        prefix = jnp.cumsum(log_keep, axis=-1)
        after = prefix[..., -1:] - prefix
        w = jnp.where(strict, jnp.exp(jax.nn.log_sigmoid(z) + after), 0.0)
        outs.append(jnp.einsum('bhqk,bhkd->bhqd', w, vb))
    return jnp.concatenate(outs, axis=2)

def swiglu(h, w_gate, w_up, w_down):
    return (jax.nn.silu(h @ w_gate) * (h @ w_up)) @ w_down

def even_layer(x, c, ada_w, ada_b, mix_norm, w_in, conv_a_w, conv_b_w, conv_b_b,
               rg_a_w, rg_a_b, rg_x_w, rg_x_b, rg_lambda, w_out,
               ffn_norm, ffn_w_gate, ffn_w_up, ffn_w_down):
    sh_m, sc_m, g_m, sh_f, sc_f, g_f = ada_modulation(c, ada_w, ada_b)
    h = modulate(rms_norm_2(x, mix_norm), sh_m, sc_m)
    u = h @ w_in
    cuts = [CONV_WIDTH, 2 * CONV_WIDTH, 3 * CONV_WIDTH, 3 * CONV_WIDTH + LRU_WIDTH]
    a_b, a_c, a_x, r_gate, r_x = jnp.split(u, cuts, axis=-1)
    y_a = a_b * causal_depthwise_conv(a_c * a_x, conv_a_w)
    xr = causal_depthwise_conv(r_x, conv_b_w) + conv_b_b
    y_b = jax.nn.gelu(r_gate) * rg_lru(xr, rg_a_w, rg_a_b, rg_x_w, rg_x_b, rg_lambda).astype(x.dtype)
    y = jnp.concatenate([y_a, y_b], axis=-1) @ w_out
    x = x + g_m[:, None, :] * y
    hf = modulate(rms_norm_2(x, ffn_norm), sh_f, sc_f)
    return x + g_f[:, None, :] * swiglu(hf, ffn_w_gate, ffn_w_up, ffn_w_down)

def odd_layer(x, c, ada_w, ada_b, mix_norm, w_qkv, q_norm, k_norm, w_out,
              ffn_norm, ffn_w_gate, ffn_w_up, ffn_w_down):
    sh_m, sc_m, g_m, sh_f, sc_f, g_f = ada_modulation(c, ada_w, ada_b)
    h = modulate(rms_norm_2(x, mix_norm), sh_m, sc_m)
    bsz, seq, _ = x.shape
    qkv = (h @ w_qkv).reshape(bsz, seq, 3, SB_HEADS, HEAD_DIM)
    q = rms_norm_2(qkv[:, :, 0], q_norm).transpose(0, 2, 1, 3)
    k = rms_norm_2(qkv[:, :, 1], k_norm).transpose(0, 2, 1, 3)
    v = qkv[:, :, 2].transpose(0, 2, 1, 3)
    o = stick_breaking_attention(q, k, v).astype(x.dtype)
    o = o.transpose(0, 2, 1, 3).reshape(bsz, seq, SB_HEADS * HEAD_DIM)
    x = x + g_m[:, None, :] * (o @ w_out)
    hf = modulate(rms_norm_2(x, ffn_norm), sh_f, sc_f)
    return x + g_f[:, None, :] * swiglu(hf, ffn_w_gate, ffn_w_up, ffn_w_down)

def second_inputs(seed: int = 0) -> dict:
    key = jax.random.key(seed)
    ks = jax.random.split(key, 40)
    f32 = jnp.float32

    def nrm(k, shape, scale):
        return jax.random.normal(k, shape, f32) * scale

    d = D_MODEL
    u = jax.random.uniform(ks[12], (LRU_WIDTH,), f32, 0.9, 0.999)
    a0 = u ** (1.0 / RG_C)
    lam = jnp.log(a0) - jnp.log1p(-a0)
    return {
        'x': nrm(ks[0], (BATCH, SEQ, d), 1.0),
        'c': nrm(ks[1], (BATCH, d), 1.0),
        'l0_ada_w': nrm(ks[2], (d, N_MOD * d), 0.5 * d ** -0.5),
        'l0_ada_b': nrm(ks[3], (N_MOD * d,), 0.02),
        'l0_mix_norm': 1.0 + nrm(ks[4], (d,), 0.02),
        'l0_w_in': nrm(ks[5], (d, 3 * CONV_WIDTH + 2 * LRU_WIDTH), d ** -0.5),
        'l0_conv_a_w': nrm(ks[6], (SHORT_CONV_K, CONV_WIDTH), SHORT_CONV_K ** -0.5),
        'l0_conv_b_w': nrm(ks[7], (LRU_CONV_K, LRU_WIDTH), LRU_CONV_K ** -0.5),
        'l0_conv_b_b': nrm(ks[8], (LRU_WIDTH,), 0.01),
        'l0_rg_a_w': nrm(ks[9], (LRU_HEADS, HEAD_DIM, HEAD_DIM), HEAD_DIM ** -0.5),
        'l0_rg_a_b': nrm(ks[10], (LRU_HEADS, HEAD_DIM), 0.01),
        'l0_rg_x_w': nrm(ks[11], (LRU_HEADS, HEAD_DIM, HEAD_DIM), HEAD_DIM ** -0.5),
        'l0_rg_x_b': nrm(ks[13], (LRU_HEADS, HEAD_DIM), 0.01),
        'l0_rg_lambda': lam,
        'l0_w_out': nrm(ks[14], (CONV_WIDTH + LRU_WIDTH, d), (CONV_WIDTH + LRU_WIDTH) ** -0.5),
        'l0_ffn_norm': 1.0 + nrm(ks[15], (d,), 0.02),
        'l0_ffn_w_gate': nrm(ks[16], (d, D_FF_2), d ** -0.5),
        'l0_ffn_w_up': nrm(ks[17], (d, D_FF_2), d ** -0.5),
        'l0_ffn_w_down': nrm(ks[18], (D_FF_2, d), D_FF_2 ** -0.5),
        'l1_ada_w': nrm(ks[19], (d, N_MOD * d), 0.5 * d ** -0.5),
        'l1_ada_b': nrm(ks[20], (N_MOD * d,), 0.02),
        'l1_mix_norm': 1.0 + nrm(ks[21], (d,), 0.02),
        'l1_w_qkv': nrm(ks[22], (d, 3 * SB_HEADS * HEAD_DIM), d ** -0.5),
        'l1_q_norm': 1.0 + nrm(ks[23], (HEAD_DIM,), 0.02),
        'l1_k_norm': 1.0 + nrm(ks[24], (HEAD_DIM,), 0.02),
        'l1_w_out': nrm(ks[25], (SB_HEADS * HEAD_DIM, d), (SB_HEADS * HEAD_DIM) ** -0.5),
        'l1_ffn_norm': 1.0 + nrm(ks[26], (d,), 0.02),
        'l1_ffn_w_gate': nrm(ks[27], (d, D_FF_2), d ** -0.5),
        'l1_ffn_w_up': nrm(ks[28], (d, D_FF_2), d ** -0.5),
        'l1_ffn_w_down': nrm(ks[29], (D_FF_2, d), D_FF_2 ** -0.5),
    }

def second_block(x, c,
              l0_ada_w, l0_ada_b, l0_mix_norm, l0_w_in, l0_conv_a_w, l0_conv_b_w, l0_conv_b_b,
              l0_rg_a_w, l0_rg_a_b, l0_rg_x_w, l0_rg_x_b, l0_rg_lambda, l0_w_out,
              l0_ffn_norm, l0_ffn_w_gate, l0_ffn_w_up, l0_ffn_w_down,
              l1_ada_w, l1_ada_b, l1_mix_norm, l1_w_qkv, l1_q_norm, l1_k_norm, l1_w_out,
              l1_ffn_norm, l1_ffn_w_gate, l1_ffn_w_up, l1_ffn_w_down):
    even_params = [(l0_ada_w, l0_ada_b, l0_mix_norm, l0_w_in, l0_conv_a_w, l0_conv_b_w, l0_conv_b_b,
                    l0_rg_a_w, l0_rg_a_b, l0_rg_x_w, l0_rg_x_b, l0_rg_lambda, l0_w_out,
                    l0_ffn_norm, l0_ffn_w_gate, l0_ffn_w_up, l0_ffn_w_down)]
    odd_params = [(l1_ada_w, l1_ada_b, l1_mix_norm, l1_w_qkv, l1_q_norm, l1_k_norm, l1_w_out,
                   l1_ffn_norm, l1_ffn_w_gate, l1_ffn_w_up, l1_ffn_w_down)]
    for layer in range(DEPTH_2):
        if layer % 2 == 0:
            x = even_layer(x, c, *even_params[layer // 2])
        else:
            x = odd_layer(x, c, *odd_params[layer // 2])
    return x


def setup_inputs(seed=0):
    out = dict(first_inputs(seed))
    for name, value in second_inputs(seed + 1).items():
        if name != "x":
            out[name + "_2"] = value
    return out


def reference(
    x, norm_mix_pre, norm_mix_post, norm_ffn_pre, norm_ffn_post, w_up, w_down, attn_w_qkv,
    attn_w_o, mlstm_w_in, mlstm_b_gates, mlstm_norm_h, mlstm_w_out, c_2, l0_ada_w_2, l0_ada_b_2,
    l0_mix_norm_2, l0_w_in_2, l0_conv_a_w_2, l0_conv_b_w_2, l0_conv_b_b_2, l0_rg_a_w_2,
    l0_rg_a_b_2, l0_rg_x_w_2, l0_rg_x_b_2, l0_rg_lambda_2, l0_w_out_2, l0_ffn_norm_2,
    l0_ffn_w_gate_2, l0_ffn_w_up_2, l0_ffn_w_down_2, l1_ada_w_2, l1_ada_b_2, l1_mix_norm_2,
    l1_w_qkv_2, l1_q_norm_2, l1_k_norm_2, l1_w_out_2, l1_ffn_norm_2, l1_ffn_w_gate_2,
    l1_ffn_w_up_2, l1_ffn_w_down_2,
):
    x = first_block(
        x, norm_mix_pre, norm_mix_post, norm_ffn_pre, norm_ffn_post, w_up, w_down, attn_w_qkv,
        attn_w_o, mlstm_w_in, mlstm_b_gates, mlstm_norm_h, mlstm_w_out,
    )
    return second_block(
        x, c_2, l0_ada_w_2, l0_ada_b_2, l0_mix_norm_2, l0_w_in_2, l0_conv_a_w_2, l0_conv_b_w_2,
        l0_conv_b_b_2, l0_rg_a_w_2, l0_rg_a_b_2, l0_rg_x_w_2, l0_rg_x_b_2, l0_rg_lambda_2,
        l0_w_out_2, l0_ffn_norm_2, l0_ffn_w_gate_2, l0_ffn_w_up_2, l0_ffn_w_down_2, l1_ada_w_2,
        l1_ada_b_2, l1_mix_norm_2, l1_w_qkv_2, l1_q_norm_2, l1_k_norm_2, l1_w_out_2,
        l1_ffn_norm_2, l1_ffn_w_gate_2, l1_ffn_w_up_2, l1_ffn_w_down_2,
    )


_drawn_inputs = setup_inputs


def setup_inputs(seed=0):
    import zlib

    import numpy as np

    out = dict(_drawn_inputs(seed))
    spreads = {}
    factors = {'l0_ada_b_2': 2.716,
     'l0_mix_norm_2': 8.0,
     'l0_conv_b_b_2': 64.0,
     'l0_rg_a_w_2': 3.487,
     'l0_rg_a_b_2': 64.0,
     'l0_rg_x_b_2': 64.0,
     'l0_ffn_norm_2': 64.0,
     'l1_ada_b_2': 4.141,
     'l1_mix_norm_2': 64.0,
     'l1_q_norm_2': 64.0,
     'l1_k_norm_2': 64.0,
     'l1_ffn_norm_2': 64.0,
     'l1_w_qkv_2': 2.669,
     'l1_w_out_2': 2.672}
    for name, (base, spread) in spreads.items():
        noise = np.random.default_rng([zlib.crc32(name.encode()), seed]).standard_normal(out[name].shape)
        drawn = base * np.exp(spread * noise) if base else spread * noise
        out[name] = __import__('jax').numpy.asarray(drawn.astype(out[name].dtype))
    for name, factor in factors.items():
        out[name] = (out[name] * factor).astype(out[name].dtype)
    return out
```

```python
from contextlib import ExitStack

import concourse.bass as bass
from concourse import mybir

F32 = mybir.dt.float32
F32R = mybir.dt.float32r
ALU = mybir.AluOpType
ACT = mybir.ActivationFunctionType
AX = mybir.AxisListType

P = 128
TOK = 256
NT = TOK // P
D = 1024
KB = D // P
CH = 512
UNIT = 2048
LO_V = 1024
EPS = 1e-6
NEG = -1e30

HEADS = 8
DH = D // HEADS
SB_HEADS = 16
SB_DH = D // SB_HEADS
LRU = 512
LB = LRU // P
LRU_HEAD = 64
RG_C = 8.0
F_MLP = 4096
F_SG = 2816
NJ_MLP = F_MLP // CH
NJ_SG = F_SG // 256
SC = P + TOK

U_QKV1 = 0
U_WO1 = U_QKV1 + 12
U_MLP = U_WO1 + 4
U_WIN = U_MLP + 4 * NJ_MLP
U_WOUT0 = U_WIN + 10
U_SG0 = U_WOUT0 + 4
U_QKV2 = U_SG0 + 3 * NJ_SG
U_WOUT1 = U_QKV2 + 12
U_SG1 = U_WOUT1 + 4
U_END = U_SG1 + 3 * NJ_SG

R_CONV_A, R_CONV_B, R_CONV_BIAS, R_RG_A, R_RG_X, R_LAMBDA, N_ROWS = 0, 3, 7, 8, 9, 10, 11


def plus(base, i, per):
    return base if i is None else i * per + base


def block_program(nc, a, out):
    ctx = ExitStack()
    with ctx:
        def sb(name, shape, dt=F32):
            return ctx.enter_context(nc.sbuf_tensor(name, shape, dt))

        def ps(name, shape):
            return ctx.enter_context(nc.psum_tensor(name, shape, F32))

        def sem(name):
            return ctx.enter_context(nc.semaphore(name))

        w_raw = sb("w_raw", [P, 2, UNIT])
        w_hi = sb("w_hi", [P, 2, UNIT], F32R)
        w_lo = sb("w_lo", [P, 2, UNIT], F32R)
        ada_raw = sb("ada_raw", [P, 3, UNIT])
        mod = sb("mod", [P, 6 * D])
        gate_ffn = sb("gate_ffn", [P, D])
        x = sb("x", [P, NT, D])
        xn = sb("xn", [P, NT, D])
        aT_hi = sb("aT_hi", [P, KB, TOK], F32R)
        aT_lo = sb("aT_lo", [P, KB, TOK], F32R)
        hT_hi = sb("hT_hi", [P, 4, TOK], F32R)
        hT_lo = sb("hT_lo", [P, 4, TOK], F32R)
        gain = sb("gain", [P, 4, D])
        qk_gain = sb("qk_gain", [P, 2, SB_DH])
        scratch = sb("scratch", [P, 10240])
        ident = sb("ident", [P, P])
        ones = sb("ones", [P, P])
        zeros = sb("zeros", [P, CH], F32R)
        neg_dist = sb("neg_dist", [P, SC])
        sb_mask = sb("sb_mask", [P, SC])
        cols = sb("cols", [P, LB, 16])
        silu_c = sb("silu_c", [P, KB])
        rg_w = sb("rg_w", [P, 2, LB, P])
        lam = sb("lam", [P, 10, LB])
        sums = sb("sums", [P, 2])
        var = sb("var", [P, 2])
        rstd = sb("rstd", [P, 2])
        half = sb("half", [P, 16])
        qk_ss = sb("qk_ss", [P, 16])
        qk_var = sb("qk_var", [P, 16])
        qk_rstd = sb("qk_rstd", [P, 16])
        att_max = sb("att_max", [P, 3, 2])
        att_nmax = sb("att_nmax", [P, 3, 2])
        att_sum = sb("att_sum", [P, 3, 2])
        att_rsum = sb("att_rsum", [P, 3, 2])

        tokbuf = scratch[:, 0:2048].rearrange("p (c t n) -> p c t n", c=2, t=NT)
        qkT = scratch[:, 2048:6144].rearrange("p (b n) -> p b n", n=TOK)
        vtok = scratch[:, 6144:8192].rearrange("p (t n) -> p t n", t=NT)
        uT = scratch[:, 2048:7168].rearrange("p (b n) -> p b n", n=TOK)
        prob = scratch[:, 8192:8192 + 3 * SC].rearrange("p (r n) -> p r n", r=3)
        probT = scratch[:, 9344:9344 + 2 * SC].rearrange("p (r n) -> p r n", r=2)
        rows = scratch[0:N_ROWS, 8192:8192 + LRU]
        c_rows = scratch[0:KB, 8192 + LRU:8192 + LRU + P]
        xn_flat = xn[:, :, :].rearrange("p t n -> p (t n)")
        stick_z = scratch[:, 8192:8192 + 3 * SC].rearrange("p (r n) -> p r n", r=3)
        stick_wT = scratch[:, 9344:9344 + 2 * SC].rearrange("p (r n) -> p r n", r=2)
        stick_sp = xn_flat[:, 0:2 * SC].rearrange("p (r n) -> p r n", r=2)
        stick_sum = xn_flat[:, 768:768 + 2 * SC].rearrange("p (r n) -> p r n", r=2)
        qk_sq = xn_flat[:, 0:1024].rearrange("p (h d) -> p h d", d=SB_DH)
        def lru_buf(ap):
            return ap.rearrange("p (b n) -> p b n", n=TOK)
        conv_a = lru_buf(scratch[:, 0:1024])
        xr = lru_buf(scratch[:, 1024:2048])
        gate_r = lru_buf(scratch[:, 7168:8192])
        gate_i = lru_buf(scratch[:, 8192:9216])
        lru_b = lru_buf(scratch[:, 9216:10240])
        lru_a = lru_buf(xn_flat[:, 0:1024])
        lru_h = lru_buf(xn_flat[:, 1024:2048])
        hbuf = scratch[:, 0:1024].rearrange("p (t n) -> p t n", t=NT)
        gbuf = scratch[:, 1024:2048].rearrange("p (t n) -> p t n", t=NT)

        acc = ps("acc", [P, 4, CH])
        ub = ps("ub", [P, 2, CH])
        tp = ps("tp", [P, 2, CH])

        x_loaded = sem("x_loaded")
        small_loaded = sem("small_loaded")
        gain_loaded = [sem(f"gain_loaded{n}") for n in range(8)]
        w_loaded = [sem("w_loaded0"), sem("w_loaded1")]
        hi_done = sem("hi_done")
        lo_v_done = sem("lo_v_done")
        lo_p_done = sem("lo_p_done")
        w_used = sem("w_used")
        ada_loaded = [sem(f"ada_loaded{n}") for n in range(3)]
        ada_bias = sem("ada_bias")
        ada_zero = sem("ada_zero")
        ada_used = sem("ada_used")
        ada_sum = sem("ada_sum")
        ada_out = sem("ada_out")
        ada_gain = sem("ada_gain")
        consts = sem("consts")
        pool_chain = sem("pool_chain")
        dve_chain = sem("dve_chain")
        act_chain = sem("act_chain")
        cols_T = sem("cols_T")
        cols_done = sem("cols_done")
        lam_exp = sem("lam_exp")
        lam_done = sem("lam_done")
        sq_done = sem("sq_done")
        rstd_done = sem("rstd_done")
        xn_done = sem("xn_done")
        nT_done = sem("nT_done")
        n_hi = sem("n_hi")
        n_lo = sem("n_lo")
        x_ready = sem("x_ready")
        chunk_a = sem("chunk_a")
        chunk_v = sem("chunk_v")
        cT0 = sem("cT0")
        cT1 = sem("cT1")
        cT_a = sem("cT_a")
        cT_v = sem("cT_v")
        v_a = sem("v_a")
        v_v = sem("v_v")
        qk_sq_done = sem("qk_sq_done")
        qk_ss_done = sem("qk_ss_done")
        qk_rstd_done = sem("qk_rstd_done")
        s_ready = sem("s_ready")
        s_max = sem("s_max")
        s_exp = sem("s_exp")
        s_norm = sem("s_norm")
        pT_ready = sem("pT_ready")
        pT_copied = sem("pT_copied")
        o_ready = sem("o_ready")
        o_hi = sem("o_hi")
        o_lo = sem("o_lo")
        z_ready = sem("z_ready")
        z_masked = sem("z_masked")
        z_log = sem("z_log")
        z_arg = sem("z_arg")
        z_w = sem("z_w")
        wT_ready = sem("wT_ready")
        wT_copied = sem("wT_copied")
        so_ready = sem("so_ready")
        so_hi = sem("so_hi")
        so_lo = sem("so_lo")
        act_h = sem("act_h")
        h_ready = sem("h_ready")
        hT_ready = sem("hT_ready")
        hT_hi_done = sem("hT_hi_done")
        hT_lo_done = sem("hT_lo_done")
        lru_p = sem("lru_p")
        lru_xr = sem("lru_xr")
        lru_gate = sem("lru_gate")
        lru_gelu = sem("lru_gelu")
        lru_r = sem("lru_r")
        lru_i = sem("lru_i")
        lru_t = sem("lru_t")
        lru_ad = sem("lru_ad")
        lru_ix = sem("lru_ix")
        lru_a2 = sem("lru_a2")
        lru_s2 = sem("lru_s2")
        lru_sqrt = sem("lru_sqrt")
        lru_ya = sem("lru_ya")
        lru_yb = sem("lru_yb")
        y_hi = sem("y_hi")
        y_lo = sem("y_lo")
        stored = sem("stored")

        def blocks(w):
            return w.rearrange("(k p) n -> p k n", p=P)
        qkv1, wo1, up1, down1 = (blocks(a[n][0]) for n in ("attn_w_qkv", "attn_w_o", "w_up", "w_down"))
        w_in, w_out0 = blocks(a["l0_w_in_2"]), blocks(a["l0_w_out_2"])
        qkv2, w_out1 = blocks(a["l1_w_qkv_2"]), blocks(a["l1_w_out_2"])
        sg = [[blocks(a[f"l{n}_ffn_w_{m}_2"]) for m in ("gate", "up", "down")] for n in (0, 1)]
        ada_w = [blocks(a[f"l{n}_ada_w_2"]) for n in (0, 1)]
        ada_b = [a[f"l{n}_ada_b_2"].rearrange("(a n) -> a n", a=1) for n in (0, 1)]
        gains = [a["norm_mix_pre"][0], a["norm_mix_post"][0], a["norm_ffn_pre"][0], a["norm_ffn_post"][0],
                 a["l0_mix_norm_2"], a["l0_ffn_norm_2"], a["l1_mix_norm_2"], a["l1_ffn_norm_2"]]

        H0 = {"mlp": 0, 0: NJ_MLP, 1: NJ_MLP + NJ_SG}
        C0 = {"qkv1": 0, "win": 4, "qkv2": 9}
        SG_U = (U_SG0, U_SG1)

        block = ctx.enter_context(nc.Block())

        @block.sync
        def _(sp):
            def load_unit(u, pieces, i=None, per=0):
                if u >= 2:
                    sp.wait_ge(lo_v_done, plus(u - 1, i, per))
                    sp.wait_ge(lo_p_done, plus(u - 1, i, per))
                for dst, src in pieces:
                    sp.dma_start(dst, src).then_inc(w_loaded[u % 2], 16)

            def proj(u, w, col, i=None, per=0):
                for h in range(2):
                    dst = w_raw[:, (u + h) % 2, :].rearrange("p (k n) -> p k n", n=CH)
                    load_unit(u + h, [(dst[:, 2 * q:2 * q + 2, :],
                                       w[:, 4 * h + 2 * q:4 * h + 2 * q + 2, bass.ds(col, CH)])
                                      for q in range(2)], i, per)

            def down(u, w, row_block, i=None, per=0):
                dst = w_raw[:, u % 2, :].rearrange("p (k n) -> p k n", n=D)
                load_unit(u, [(dst[:, q:q + 1, :], w[:, bass.ds(row_block + q, 1), :]) for q in range(2)], i, per)

            def gate_up(u, layer, col, i=None, per=0):
                for h in range(2):
                    dst = w_raw[:, (u + h) % 2, :].rearrange("p (k n) -> p k n", n=CH)
                    load_unit(u + h, [(dst[:, :, 256 * m:256 * m + 256],
                                       sg[layer][m][:, 4 * h:4 * h + 4, bass.ds(col, 256)])
                                      for m in range(2)], i, per)

            def load_ada(layer, kb, third, i=None, per=0, rb=None):
                n = 24 * layer + 3 * kb + third
                if n >= 3:
                    sp.wait_ge(ada_used, plus(n - 2, i, per))
                src = ada_w[layer][:, bass.ds(kb if rb is None else rb, 1), third * UNIT:(third + 1) * UNIT]
                sp.dma_start(ada_raw[:, third:third + 1, :], src).then_inc(ada_loaded[third], 16)

            def load_gain(n):
                sp.dma_start(gain[:, n % 4, :], gains[n].partition_broadcast(P)).then_inc(gain_loaded[n], 16)

            for t in range(NT):
                sp.dma_start(x[:, t, :], a["x"][0, t * P:(t + 1) * P, :]).then_inc(x_loaded, 16)
            load_gain(0)
            proj(U_QKV1, qkv1, 0)
            small = [(rows[R_CONV_A:R_CONV_A + 3, :], a["l0_conv_a_w_2"]),
                     (rows[R_CONV_B:R_CONV_B + 4, :], a["l0_conv_b_w_2"]),
                     (rows[R_CONV_BIAS:R_CONV_BIAS + 1, :], a["l0_conv_b_b_2"].rearrange("(a n) -> a n", a=1)),
                     (rows[R_RG_A:R_RG_A + 1, :], a["l0_rg_a_b_2"].rearrange("(a h) n -> a (h n)", a=1)),
                     (rows[R_RG_X:R_RG_X + 1, :], a["l0_rg_x_b_2"].rearrange("(a h) n -> a (h n)", a=1)),
                     (rows[R_LAMBDA:R_LAMBDA + 1, :], a["l0_rg_lambda_2"].rearrange("(a n) -> a n", a=1)),
                     (c_rows[:, :], a["c_2"].rearrange("a (k p) -> (a k) p", p=P)),
                     (qk_gain[:, 0, :], a["l1_q_norm_2"].partition_broadcast(P)),
                     (qk_gain[:, 1, :], a["l1_k_norm_2"].partition_broadcast(P))]
            sp.wait_ge(consts, 1)
            for g, name in enumerate(("l0_rg_a_w_2", "l0_rg_x_w_2")):
                for e in range(2):
                    q = slice(LRU_HEAD * e, LRU_HEAD * (e + 1))
                    small.append((rg_w[q, g, :, q], a[name].rearrange("(b e) i j -> e i b j", e=2)[e]))
            for dst, src in small:
                sp.dma_start(dst, src).then_inc(small_loaded, 16)
            load_gain(1)
            sp.wait_ge(ada_zero, 1)
            sp.dma_start(mod[0:1, :], ada_b[0]).then_inc(ada_bias, 16)
            for c in range(1, 6):
                proj(U_QKV1 + 2 * c, qkv1, c * CH)
            load_gain(2)
            load_gain(3)
            for c in range(2):
                proj(U_WO1 + 2 * c, wo1, c * CH)
            proj(U_MLP, up1, 0)
            for third in range(3):
                load_ada(0, 0, third)
            with sp.Fori(0, NJ_MLP - 1) as i:
                u = U_MLP + 2
                proj(u, up1, i * CH + CH, i, 4)
                load_ada(0, 1, 0, i, 3, i + 1)
                down(u + 2, down1, i * 4, i, 4)
                load_ada(0, 1, 1, i, 3, i + 1)
                down(u + 3, down1, i * 4 + 2, i, 4)
                load_ada(0, 1, 2, i, 3, i + 1)
            for h in range(2):
                down(U_WIN - 2 + h, down1, 4 * (NJ_MLP - 1) + 2 * h)
            sp.wait_ge(xn_done, 4)
            load_gain(4)
            load_gain(5)
            load_gain(6)
            for c in range(5):
                proj(U_WIN + 2 * c, w_in, c * CH)
            sp.wait_ge(x_ready, 4)
            load_gain(7)
            for c in range(2):
                proj(U_WOUT0 + 2 * c, w_out0, c * CH)

            def swiglu(layer):
                u = SG_U[layer]
                gate_up(u, layer, 0)
                if layer == 0:
                    sp.wait_ge(ada_zero, 2)
                    sp.dma_start(mod[0:1, :], ada_b[1]).then_inc(ada_bias, 16)

                def pair(i, base, with_ada):
                    for q in range(2):
                        v = u + 2 + 3 * (base - 1 + q)
                        gate_up(v, layer, plus(256 * (base + q), i, 512), i, 6)
                        if with_ada:
                            load_ada(1, q, 0, i, 6, plus(q, i, 2))
                            load_ada(1, q, 1, i, 6, plus(q, i, 2))
                        down(v + 2, sg[layer][2], plus(2 * (base - 1 + q), i, 4), i, 6)
                        if with_ada:
                            load_ada(1, q, 2, i, 6, plus(q, i, 2))

                with sp.Fori(0, 4) as i:
                    pair(i, 1, layer == 0)
                pair(None, 9, False)
                down(u + 3 * NJ_SG - 1, sg[layer][2], 2 * (NJ_SG - 1))

            swiglu(0)
            for c in range(6):
                proj(U_QKV2 + 2 * c, qkv2, c * CH)
            for c in range(2):
                proj(U_WOUT1 + 2 * c, w_out1, c * CH)
            swiglu(1)
            for t in range(NT):
                sp.wait_ge(x_ready, 11 + t)
                sp.dma_start(out[0, t * P:(t + 1) * P, :], x[:, t, :]).then_inc(stored, 16)
            sp.wait_ge(stored, 16 * NT)

        @block.gpsimd
        def _(pool):
            n_chain = [0]

            def chained(ins):
                n_chain[0] += 1
                ins.then_inc(pool_chain, 1)
                pool.wait_ge(pool_chain, n_chain[0])

            def split_lo(u, i=None, per=0):
                if u >= U_END:
                    return
                pool.wait_ge(hi_done, plus(u + 1, i, per))
                s = u % 2
                pool.tensor_tensor(w_lo[:, s, LO_V:], w_raw[:, s, LO_V:], w_hi[:, s, LO_V:].bitcast(F32),
                                   ALU.subtract).then_inc(lo_p_done, 1)

            def splits(u0, u1):
                for u in range(u0, u1):
                    split_lo(u)

            n_rstd = [0]

            def row_rstd():
                n_rstd[0] += 1
                pool.wait_ge(sq_done, 2 * n_rstd[0])
                chained(pool.tensor_scalar(var[:, :], sums[:, :], 1.0 / D, EPS, ALU.mult, ALU.add))
                pool.tensor_tensor(rstd[:, :], var[:, :], half[:, 0:2], ALU.pow).then_inc(rstd_done, 1)

            chained(pool.memset(half[:, :], -0.5))
            chained(pool.memset(ident[:, :], 0.0))
            chained(pool.affine_select(out=ident[:, :], in_=ident[:, :], compare_op=ALU.not_equal, fill=1.0,
                                       base=0, pattern=[[-1, P]], channel_multiplier=1))
            pool.memset(rg_w[:, :, :, :], 0.0).then_inc(consts, 1)
            row_rstd()
            split_lo(0)
            pool.memset(ones[:, :], 1.0).then_inc(consts, 1)
            pool.memset(zeros[:, :].bitcast(F32), 0.0).then_inc(consts, 1)
            chained(pool.iota(neg_dist[:, 0:P], pattern=[[1, P]], base=0, channel_multiplier=-1,
                              allow_small_or_imprecise_dtypes=True))
            chained(pool.iota(neg_dist[:, P:SC], pattern=[[1, TOK]], base=-P, channel_multiplier=-1,
                              allow_small_or_imprecise_dtypes=True))
            chained(pool.memset(sb_mask[:, :], 0.0))
            for m, keep_diag in ((neg_dist, 0), (sb_mask, -1)):
                for lo, n, q0 in ((0, P, 0), (P, TOK, P)):
                    part = m[:, lo:lo + n]
                    pool.affine_select(out=part, in_=part, compare_op=ALU.is_ge, fill=NEG, base=q0 + keep_diag,
                                       pattern=[[-1, n]], channel_multiplier=1).then_inc(consts, 1)
            pool.memset(mod[:, :], 0.0).then_inc(ada_zero, 1)
            splits(1, U_MLP + 1)
            row_rstd()
            row_rstd()
            splits(U_MLP + 1, U_MLP + 3)
            with pool.Fori(0, NJ_MLP - 1) as i:
                for q in range(4):
                    split_lo(U_MLP + 3 + q, i, 4)
            splits(U_MLP + 3 + 4 * (NJ_MLP - 1), U_WIN + 1)
            row_rstd()
            row_rstd()
            splits(U_WIN + 1, U_WOUT0 + 1)
            pool.wait_ge(cT_a, C0["win"] + 3)
            pool.wait_ge(cT_v, C0["win"] + 3)
            pool.tensor_tensor(uT[:, 4:8, :], uT[:, 4:8, :], uT[:, 8:12, :], ALU.mult).then_inc(lru_p, 1)
            pool.wait_ge(lru_i, 1)
            pool.wait_ge(lru_xr, 1)
            pool.tensor_tensor(gate_i, gate_i, xr, ALU.mult).then_inc(lru_ix, 1)
            pool.wait_ge(lru_ad, 1)
            pool.tensor_tensor(gate_r, lru_a, lru_a, ALU.mult).then_inc(lru_a2, 1)
            splits(U_WOUT0 + 1, U_SG0 + 1)
            row_rstd()

            def swiglu(layer):
                u = SG_U[layer]
                if layer == 0:
                    pool.wait_ge(xn_done, 8)
                    pool.memset(mod[:, :], 0.0).then_inc(ada_zero, 1)
                splits(u + 1, u + 3)
                with pool.Fori(0, 4) as i:
                    for q in range(6):
                        split_lo(u + 3 + q, i, 6)
                splits(u + 3 + 24, u + 3 * NJ_SG + 1)

            swiglu(0)
            row_rstd()
            splits(U_QKV2 + 1, U_QKV2 + 2)
            for c in range(4):
                splits(U_QKV2 + 2 + 2 * c, U_QKV2 + 4 + 2 * c)
                pool.wait_ge(qk_ss_done, c + 1)
                chained(pool.tensor_scalar(qk_var[:, :], qk_ss[:, :], 1.0 / SB_DH, EPS, ALU.mult, ALU.add))
                pool.tensor_tensor(qk_rstd[:, :], qk_var[:, :], half[:, :], ALU.pow).then_inc(qk_rstd_done, 1)
            splits(U_QKV2 + 10, U_SG1 + 1)
            row_rstd()
            swiglu(1)

        @block.scalar
        def _(act):
            n_chain = [0]

            def chained(ins):
                n_chain[0] += 1
                ins.then_inc(act_chain, 1)
                act.wait_ge(act_chain, n_chain[0])

            def split_hi(u, i=None, per=0):
                if u >= U_END:
                    return
                act.wait_ge(w_loaded[u % 2], plus(32 * (u // 2 + 1), i, 16 * per))
                if u >= 2:
                    act.wait_ge(w_used, plus(u - 1, i, per))
                act.activation(w_hi[:, u % 2, :], w_raw[:, u % 2, :], ACT.Copy).then_inc(hi_done, 1)

            def splits(u0, u1):
                for u in range(u0, u1):
                    split_hi(u)

            def row_squares(src):
                for t in range(NT):
                    act.activation(xn[:, t, :], src(t), ACT.Square, accum_out=sums[:, t:t + 1]).then_inc(sq_done, 1)

            n_norm = [0]

            def norm(first=False):
                k = n_norm[0]
                n_norm[0] += 1
                if k == 0:
                    act.wait_ge(x_loaded, 32)
                else:
                    act.wait_ge(x_ready, 2 * k)
                row_squares(lambda t: x[:, t, :])
                if first:
                    split_hi(0)
                for g in range(4):
                    act.wait_ge(nT_done, 4 * k + g + 1)
                    act.activation(aT_hi[:, 2 * g:2 * g + 2, :], tp[:, g % 2, :].rearrange("p (b n) -> p b n", n=TOK),
                                   ACT.Copy).then_inc(n_hi, 1)

            def post_norm(u_end):
                act.wait_ge(w_used, u_end)
                row_squares(lambda t: acc[:, 2 * t:2 * t + 2, :].rearrange("p b n -> p (b n)"))

            n_ada = [0]

            def ada_parts():
                for c in range(12):
                    n = 12 * n_ada[0] + c
                    if c == 10 and n_ada[0]:
                        act.wait_ge(x_ready, 8)
                    act.wait_ge(ada_sum, n + 1)
                    dst = mod[:, c * CH:(c + 1) * CH] if c < 10 else gate_ffn[:, (c - 10) * CH:(c - 9) * CH]
                    act.activation(dst, ub[:, c % 2, :], ACT.Copy).then_inc(ada_out, 1)
                n_ada[0] += 1

            n_copied = [0]

            def copy_chunk(u, par, ct, i=None, per=0, step=0):
                act.wait_ge(w_used, plus(u + 2, i, per))
                if ct >= 2:
                    act.wait_ge(cT1, plus(ct - 1, i, step))
                act.activation(tokbuf[:, par, 0, :], acc[:, 2 * par, :], ACT.Copy).then_inc(chunk_a, 1)

            def copy_T(dst, ct, b, i=None, step=0):
                act.wait_ge(cT0, plus(ct + 1, i, step))
                act.activation(dst[:, bass.ds(b, 2), :], tp[:, 0, :].rearrange("p (b n) -> p b n", n=TOK),
                               ACT.Copy).then_inc(cT_a, 1)

            def copy_v(u, n):
                act.wait_ge(w_used, u + 2)
                act.activation(vtok[:, 0, n * CH:(n + 1) * CH], acc[:, 2 * n, :], ACT.Copy).then_inc(v_a, 1)

            def project_pair(u, dst, ct, b, i=None):
                for q in range(1, 4):
                    split_hi(u + q, i, 4)
                copy_chunk(u, 0, ct, i, 4, 2)
                split_hi(u + 4, i, 4)
                copy_chunk(u + 2, 1, ct + 1, i, 4, 2)
                copy_T(dst, ct, b, i, 2)
                copy_T(dst, ct + 1, plus(b + 4, None, 0) if i is None else b + 4, i, 2)

            def project_v(u):
                splits(u + 1, u + 4)
                copy_v(u, 0)
                split_hi(u + 4)
                copy_v(u + 2, 1)

            norm(first=True)
            act.wait_ge(cols_T, 1)
            act.activation(cols[:, :, 0:N_ROWS], ub[:, 0, 0:64].rearrange("p (b r) -> p b r", r=16)[:, :, 0:N_ROWS],
                           ACT.Copy).then_inc(cols_done, 1)
            act.activation(silu_c[:, :], ub[:, 0, 64:64 + KB], ACT.Silu).then_inc(cols_done, 1)
            act.wait_ge(cols_done, 1)
            chained(act.activation(lam[:, 0, :], cols[:, :, R_LAMBDA], ACT.Abs))
            act.activation(lam[:, 1, :], lam[:, 0, :], ACT.Exp, scale=-1.0).then_inc(lam_exp, 1)

            with act.Fori(0, 2) as i:
                project_pair(U_QKV1, qkT, C0["qkv1"], i * 8, i)
            project_v(U_QKV1 + 8)

            def att_exp(h):
                act.wait_ge(s_max, h + 1)
                r = h % 3
                for t, lo, n in ((0, 0, P), (1, P, TOK)):
                    act.activation(prob[:, r, lo:lo + n], prob[:, r, lo:lo + n], ACT.Exp, scale=DH ** -0.5,
                                   bias=att_nmax[:, r, t:t + 1], accum_out=att_sum[:, r, t:t + 1]).then_inc(s_exp, 1)

            att_exp(0)
            for h in range(HEADS):
                if h + 1 < HEADS:
                    att_exp(h + 1)
                act.wait_ge(pT_ready, h + 1)
                if h >= 2:
                    act.wait_ge(o_ready, h - 1)
                act.activation(probT[:, h % 2, :], tp[:, h % 2, 0:SC], ACT.Copy).then_inc(pT_copied, 1)
                act.wait_ge(o_ready, h + 1)
                act.activation(aT_hi[:, h, :], acc[:, h % 2, 0:TOK], ACT.Copy).then_inc(o_hi, 1)
            splits(U_WO1 + 1, U_MLP + 1)
            post_norm(U_MLP)
            norm()

            def mlp_slice(u, j, i=None, first=False):
                split_hi(u + 1, i, 4)
                split_hi(u + 2, i, 4)
                if not first:
                    split_hi(u + 3, i, 4)
                act.wait_ge(w_used, plus(u + 2, i, 4))
                if j >= 1:
                    act.wait_ge(h_ready, plus(j, i, 1))
                act.activation(gbuf, ub[:, :, :], ACT.Relu).then_inc(act_h, 1)
                if not first:
                    split_hi(u + 4, i, 4)
                for g in range(2):
                    act.wait_ge(hT_ready, plus(2 * j + g + 1, i, 2))
                    act.activation(hT_hi[:, 2 * g:2 * g + 2, :], tp[:, g, :].rearrange("p (b n) -> p b n", n=TOK),
                                   ACT.Copy).then_inc(hT_hi_done, 1)

            mlp_slice(U_MLP, 0, first=True)
            with act.Fori(0, NJ_MLP - 1) as i:
                mlp_slice(U_MLP + 2, 1, i)
            splits(U_WIN - 1, U_WIN + 1)
            post_norm(U_WIN)
            ada_parts()
            norm()
            with act.Fori(0, 2) as i:
                project_pair(U_WIN, uT, C0["win"], i * 8, i)
            u = U_WIN + 8
            split_hi(u + 1)
            split_hi(u + 2)
            copy_chunk(u, 0, C0["win"] + 4)
            copy_T(uT, C0["win"] + 4, 16)
            act.wait_ge(cT_a, C0["win"] + 4)
            act.wait_ge(cT_v, C0["win"] + 4)
            act.activation(uT[:, 12:16, :], uT[:, 12:16, :], ACT.Gelu_apprx_tanh).then_inc(lru_gelu, 1)
            for g, (dst, row, done) in enumerate(((gate_r, R_RG_A, lru_r), (gate_i, R_RG_X, lru_i))):
                act.wait_ge(lru_gate, g + 1)
                for b in range(LB):
                    last = act.activation(dst[:, b, :], acc[:, 2 * g + b // 2, (b % 2) * TOK:(b % 2 + 1) * TOK],
                                          ACT.Sigmoid, bias=cols[:, b, row:row + 1])
                last.then_inc(done, 1)
            act.wait_ge(lam_done, 1)
            act.wait_ge(lru_r, 1)
            for b in range(LB):
                last = act.activation(lru_b[:, b, :], gate_r[:, b, :], ACT.Tanh, scale=lam[:, 8, b:b + 1])
            last.then_inc(lru_t, 1)
            for b in range(LB):
                last = act.activation(lru_a[:, b, :], gate_r[:, b, :], ACT.Exp, scale=lam[:, 9, b:b + 1])
            last.then_inc(lru_ad, 1)
            act.wait_ge(lru_ya, 1)
            act.activation(aT_hi[:, 0:LB, :], conv_a, ACT.Copy).then_inc(y_hi, 1)
            act.wait_ge(lru_s2, 1)
            act.activation(lru_b, lru_b, ACT.Sqrt).then_inc(lru_sqrt, 1)
            act.wait_ge(lru_yb, 1)
            act.activation(aT_hi[:, LB:2 * LB, :], lru_h, ACT.Copy).then_inc(y_hi, 1)
            splits(U_WOUT0 + 1, U_SG0 + 1)
            norm()

            def swiglu(layer):
                u, j0 = SG_U[layer], H0[layer]
                hj = 2 * NJ_MLP + NJ_SG * layer

                def one(v, j, i=None, first=False):
                    split_hi(v + 1, i, 6)
                    split_hi(v + 2, i, 6)
                    act.wait_ge(w_used, plus(v + 2, i, 6))
                    act.wait_ge(h_ready, plus(j0 + j, i, 2))
                    act.activation(gbuf[:, :, 0:256], ub[:, :, 0:256], ACT.Silu).then_inc(act_h, 1)
                    if not first:
                        split_hi(v + 3, i, 6)
                    act.wait_ge(hT_ready, plus(hj + j + 1, i, 2))
                    act.activation(hT_hi[:, 0:2, :], tp[:, 0, :].rearrange("p (b n) -> p b n", n=TOK),
                                   ACT.Copy).then_inc(hT_hi_done, 1)

                one(u, 0, first=True)
                with act.Fori(0, 4) as i:
                    for q in range(2):
                        one(u + 2 + 3 * q, 1 + q, i)
                for q in range(2):
                    one(u + 2 + 3 * (8 + q), 9 + q)
                split_hi(u + 3 * NJ_SG)

            swiglu(0)
            ada_parts()
            norm()
            split_hi(U_QKV2 + 1)
            for c in range(4):
                u = U_QKV2 + 2 * c
                split_hi(u + 2)
                act.wait_ge(w_used, u + 2)
                if c >= 1:
                    act.wait_ge(qk_ss_done, c)
                act.activation(qk_sq, acc[:, 2 * (c % 2):2 * (c % 2) + 2, :].rearrange("p t (h d) -> p (t h) d", d=SB_DH),
                               ACT.Square).then_inc(qk_sq_done, 1)
                split_hi(u + 3)
                if c >= 1:
                    copy_T(qkT, C0["qkv2"] + c - 1, 4 * (c - 1))
            u = U_QKV2 + 8
            splits(u + 2, u + 3)
            copy_T(qkT, C0["qkv2"] + 3, 12)
            copy_v(u, 0)
            splits(u + 3, u + 5)
            copy_v(u + 2, 1)

            def stick_log(h):
                act.wait_ge(z_masked, h + 1)
                buf = stick_sp[:, h % 2, :]
                if h >= 2:
                    act.wait_ge(z_arg, h - 1)
                chained(act.activation(buf, stick_z[:, h % 3, :], ACT.Abs))
                chained(act.activation(buf, buf, ACT.Exp, scale=-1.0))
                act.activation(buf, buf, ACT.Ln, bias=1.0).then_inc(z_log, 1)

            def stick_hi(b):
                act.wait_ge(so_ready, 2 * b + 2)
                for e in range(2):
                    q = slice(SB_DH * e, SB_DH * (e + 1))
                    act.activation(aT_hi[q, b, :], acc[q, 2 * (b % 2) + e, 0:TOK], ACT.Copy).then_inc(so_hi, 1)

            stick_log(0)
            for h in range(SB_HEADS):
                if h + 1 < SB_HEADS:
                    stick_log(h + 1)
                act.wait_ge(z_arg, h + 1)
                act.activation(stick_z[:, h % 3, :], stick_z[:, h % 3, :], ACT.Exp).then_inc(z_w, 1)
                if h >= 2 and h % 2 == 0:
                    stick_hi(h // 2 - 1)
            stick_hi(SB_HEADS // 2 - 1)
            splits(U_WOUT1 + 1, U_SG1 + 1)
            norm()
            swiglu(1)

        @block.vector
        def _(dve):
            n_chain = [0]

            def chained(ins):
                n_chain[0] += 1
                ins.then_inc(dve_chain, 1)
                dve.wait_ge(dve_chain, n_chain[0])

            def split_lo(u, i=None, per=0):
                if u >= U_END:
                    return
                dve.wait_ge(hi_done, plus(u + 1, i, per))
                s = u % 2
                dve.tensor_tensor(w_lo[:, s, 0:LO_V], w_raw[:, s, 0:LO_V], w_hi[:, s, 0:LO_V].bitcast(F32),
                                  ALU.subtract).then_inc(lo_v_done, 1)

            def splits(u0, u1):
                for u in range(u0, u1):
                    split_lo(u)

            def bank_lo(dst, hi, bank):
                return dve.tensor_tensor(dst, bank, hi.bitcast(F32), ALU.subtract)

            n_norm, n_rstd = [0], [0]

            def norm(g, shift=None, first=False):
                k = n_norm[0]
                n_norm[0] += 1
                n_rstd[0] += 1
                dve.wait_ge(rstd_done, n_rstd[0])
                for t in range(NT):
                    ins = dve.scalar_tensor_tensor(xn[:, t, :], x[:, t, :], rstd[:, t:t + 1], g, ALU.mult, ALU.mult)
                    if shift is not None:
                        chained(ins)
                        ins = dve.tensor_tensor(xn[:, t, :], xn[:, t, :], shift, ALU.add)
                    ins.then_inc(xn_done, 1)
                if first:
                    split_lo(0)
                for q in range(4):
                    dve.wait_ge(n_hi, 4 * k + q + 1)
                    sl = slice(2 * q, 2 * q + 2)
                    bank_lo(aT_lo[:, sl, :], aT_hi[:, sl, :],
                            tp[:, q % 2, :].rearrange("p (b n) -> p b n", n=TOK)).then_inc(n_lo, 1)

            def acc_tile(t):
                return acc[:, 2 * t:2 * t + 2, :].rearrange("p b n -> p (b n)")

            def post_norm(g):
                n_rstd[0] += 1
                dve.wait_ge(rstd_done, n_rstd[0])
                for t in range(NT):
                    chained(dve.scalar_tensor_tensor(xn[:, t, :], acc_tile(t), rstd[:, t:t + 1], g, ALU.mult, ALU.mult))
                    dve.tensor_tensor(x[:, t, :], x[:, t, :], xn[:, t, :], ALU.add).then_inc(x_ready, 1)

            def gated(u_end, g):
                dve.wait_ge(w_used, u_end)
                for t in range(NT):
                    chained(dve.tensor_tensor(xn[:, t, :], acc_tile(t), g, ALU.mult))
                    dve.tensor_tensor(x[:, t, :], x[:, t, :], xn[:, t, :], ALU.add).then_inc(x_ready, 1)

            def ada(layer, kb, third, i=None, per=0, step=0, col=None):
                n = 24 * layer + 3 * kb + third
                dve.wait_ge(ada_loaded[third], plus(16 * (8 * layer + kb + 1), i, 16 * step))
                if n >= 3:
                    dve.wait_ge(ada_used, plus(n - 2, i, per))
                part = mod[:, third * UNIT:(third + 1) * UNIT]
                dve.scalar_tensor_tensor(part, ada_raw[:, third, :], silu_c[:, bass.ds(kb if col is None else col, 1)],
                                         part, ALU.mult, ALU.add).then_inc(ada_used, 1)

            n_ada = [0]

            def ada_gains():
                for n, c in enumerate((1, 4)):
                    dve.wait_ge(ada_out, 12 * n_ada[0] + 2 * c + 2)
                    g = 4 + 2 * n_ada[0] + n
                    dve.wait_ge(gain_loaded[g], 16)
                    part = mod[:, c * D:(c + 1) * D]
                    dve.scalar_tensor_tensor(part, part, 1.0, gain[:, g % 4, :], ALU.add, ALU.mult).then_inc(ada_gain, 1)
                n_ada[0] += 1
                dve.wait_ge(ada_gain, 2 * n_ada[0])
                dve.wait_ge(ada_out, 12 * n_ada[0])

            SH_M, G_M, GATE_M, SH_F, G_F = (mod[:, c * D:(c + 1) * D] for c in range(5))

            def copy_chunk(u, par, ct, i=None, per=0, step=0):
                dve.wait_ge(w_used, plus(u + 2, i, per))
                if ct >= 2:
                    dve.wait_ge(cT1, plus(ct - 1, i, step))
                dve.tensor_copy(tokbuf[:, par, 1, :], acc[:, 2 * par + 1, :]).then_inc(chunk_v, 1)

            def copy_T(dst, ct, b, i=None, step=0):
                dve.wait_ge(cT1, plus(ct + 1, i, step))
                dve.tensor_copy(dst[:, bass.ds(b, 2), :], tp[:, 1, :].rearrange("p (b n) -> p b n", n=TOK)).then_inc(cT_v, 1)

            def copy_v(u, n):
                dve.wait_ge(w_used, u + 2)
                dve.tensor_copy(vtok[:, 1, n * CH:(n + 1) * CH], acc[:, 2 * n + 1, :]).then_inc(v_v, 1)

            def project_pair(u, dst, ct, b, i=None):
                for q in range(1, 4):
                    split_lo(u + q, i, 4)
                copy_chunk(u, 0, ct, i, 4, 2)
                split_lo(u + 4, i, 4)
                copy_chunk(u + 2, 1, ct + 1, i, 4, 2)
                copy_T(dst, ct, b + 2, i, 2)
                copy_T(dst, ct + 1, b + 6, i, 2)

            dve.wait_ge(gain_loaded[0], 16)
            norm(gain[:, 0, :], first=True)
            dve.wait_ge(lam_exp, 1)
            e, s, s2, q, m = (lam[:, n, :] for n in (1, 3, 4, 5, 6))
            chained(dve.tensor_scalar(lam[:, 2, :], e, 2.0, None, ALU.add))
            chained(dve.reciprocal(lam[:, 2, :], lam[:, 2, :]))
            chained(dve.tensor_tensor(s, e, lam[:, 2, :], ALU.mult))
            chained(dve.tensor_tensor(s2, s, s, ALU.mult))
            chained(dve.tensor_scalar(q, s2, 1.0 / 19.0, None, ALU.mult))
            for n in range(8, 0, -1):
                chained(dve.scalar_tensor_tensor(q, q, 1.0 / (2 * n + 1), s2, ALU.add, ALU.mult))
            chained(dve.scalar_tensor_tensor(q, q, 1.0, s, ALU.add, ALU.mult))
            chained(dve.tensor_scalar(m, cols[:, :, R_LAMBDA], -1.0, 0.0, ALU.mult, ALU.max))
            chained(dve.scalar_tensor_tensor(q, q, 2.0, m, ALU.mult, ALU.add))
            chained(dve.tensor_scalar(lam[:, 8, :], q, RG_C, None, ALU.mult))
            dve.tensor_scalar(lam[:, 9, :], q, -RG_C, None, ALU.mult).then_inc(lam_done, 1)

            with dve.Fori(0, 2) as i:
                project_pair(U_QKV1, qkT, C0["qkv1"], i * 8, i)
            u = U_QKV1 + 8
            splits(u + 1, u + 4)
            copy_v(u, 0)
            split_lo(u + 4)
            copy_v(u + 2, 1)

            def att_max_of(h):
                r = h % 3
                dve.wait_ge(s_ready, h + 1)
                if h >= 3:
                    dve.wait_ge(pT_ready, h - 2)
                slope = 2.0 ** (-8.0 * (h + 1) / HEADS)
                chained(dve.scalar_tensor_tensor(prob[:, r, :], neg_dist[:, :], slope * DH ** 0.5, ub[:, h % 2, 0:SC],
                                                 ALU.mult, ALU.add))
                dve.reduce_max(att_max[:, r, 0:1], prob[:, r, 0:P], AX.X)
                chained(dve.reduce_max(att_max[:, r, 1:2], prob[:, r, P:SC], AX.X))
                dve.tensor_scalar(att_nmax[:, r, :], att_max[:, r, :], -DH ** -0.5, None, ALU.mult).then_inc(s_max, 1)

            def att_norm(h):
                r = h % 3
                dve.wait_ge(s_exp, 2 * h + 2)
                chained(dve.reciprocal(att_rsum[:, r, :], att_sum[:, r, :]))
                for t, lo, n in ((0, 0, P), (1, P, TOK)):
                    dve.tensor_scalar(prob[:, r, lo:lo + n], prob[:, r, lo:lo + n], att_rsum[:, r, t:t + 1], None,
                                      ALU.mult).then_inc(s_norm, 1)

            dve.wait_ge(consts, 7)
            att_max_of(0)
            att_max_of(1)
            att_norm(0)
            for h in range(HEADS):
                if h + 2 < HEADS:
                    att_max_of(h + 2)
                if h + 1 < HEADS:
                    att_norm(h + 1)
                dve.wait_ge(o_hi, h + 1)
                bank_lo(aT_lo[:, h, :], aT_hi[:, h, :], acc[:, h % 2, 0:TOK]).then_inc(o_lo, 1)
            splits(U_WO1 + 1, U_MLP + 1)
            dve.wait_ge(gain_loaded[1], 16)
            post_norm(gain[:, 1, :])
            dve.wait_ge(gain_loaded[2], 16)
            norm(gain[:, 2, :])

            def mlp_slice(u, j, i=None, first=False):
                adas = [(0, j, t, i, 3, 1, None if i is None else i + 1) for t in range(3)]
                split_lo(u + 1, i, 4)
                ada(*adas[0])
                split_lo(u + 2, i, 4)
                ada(*adas[1])
                if not first:
                    split_lo(u + 3, i, 4)
                dve.wait_ge(act_h, plus(j + 1, i, 1))
                if j >= 1:
                    dve.wait_ge(hT_ready, plus(2 * j, i, 2))
                dve.tensor_tensor(hbuf, gbuf, gbuf, ALU.mult).then_inc(h_ready, 1)
                if not first:
                    split_lo(u + 4, i, 4)
                ada(*adas[2])
                for g in range(2):
                    dve.wait_ge(hT_hi_done, plus(2 * j + g + 1, i, 2))
                    sl = slice(2 * g, 2 * g + 2)
                    bank_lo(hT_lo[:, sl, :], hT_hi[:, sl, :],
                            tp[:, g, :].rearrange("p (b n) -> p b n", n=TOK)).then_inc(hT_lo_done, 1)

            dve.wait_ge(cols_done, 2)
            dve.wait_ge(ada_bias, 16)
            mlp_slice(U_MLP, 0, first=True)
            with dve.Fori(0, NJ_MLP - 1) as i:
                mlp_slice(U_MLP + 2, 1, i)
            splits(U_WIN - 1, U_WIN + 1)
            dve.wait_ge(gain_loaded[3], 16)
            post_norm(gain[:, 3, :])
            ada_gains()

            norm(G_M, SH_M)
            with dve.Fori(0, 2) as i:
                project_pair(U_WIN, uT, C0["win"], i * 8, i)
            u = U_WIN + 8
            split_lo(u + 1)
            split_lo(u + 2)
            copy_chunk(u, 0, C0["win"] + 4)
            copy_T(uT, C0["win"] + 4, 18)

            def conv(dst, src, row, width, bias):
                for b in range(LB):
                    w = cols[:, b, row + width - 1:row + width]
                    if bias is None:
                        ins = dve.tensor_scalar(dst[:, b, :], src[:, b, :], w, None, ALU.mult)
                    else:
                        ins = dve.tensor_scalar(dst[:, b, :], src[:, b, :], w, cols[:, b, bias:bias + 1],
                                                ALU.mult, ALU.add)
                for s in range(1, width):
                    chained(ins)
                    for b in range(LB):
                        w = cols[:, b, row + width - 1 - s:row + width - s]
                        ins = dve.scalar_tensor_tensor(dst[:, b, s:], src[:, b, :TOK - s], w, dst[:, b, s:],
                                                       ALU.mult, ALU.add)
                return ins

            dve.wait_ge(cT_a, C0["win"] + 5)
            dve.wait_ge(cT_v, C0["win"] + 5)
            conv(xr, uT[:, 16:20, :], R_CONV_B, 4, R_CONV_BIAS).then_inc(lru_xr, 1)
            dve.wait_ge(lru_p, 1)
            chained(conv(conv_a, uT[:, 4:8, :], R_CONV_A, 3, None))
            dve.tensor_tensor(conv_a, conv_a, uT[:, 0:4, :], ALU.mult).then_inc(lru_ya, 1)
            dve.wait_ge(y_hi, 1)
            dve.tensor_tensor(aT_lo[:, 0:LB, :], conv_a, aT_hi[:, 0:LB, :].bitcast(F32), ALU.subtract).then_inc(y_lo, 1)
            dve.wait_ge(lru_a2, 1)
            dve.wait_ge(lru_t, 1)
            dve.scalar_tensor_tensor(lru_b, gate_r, 1.0, lru_b, ALU.add, ALU.mult).then_inc(lru_s2, 1)
            dve.wait_ge(lru_sqrt, 1)
            dve.wait_ge(lru_ix, 1)
            chained(dve.tensor_tensor(lru_b, lru_b, gate_i, ALU.mult))
            for b in range(LB):
                ins = dve.tensor_tensor_scan(lru_h[:, b, :], lru_a[:, b, :], lru_b[:, b, :], 0.0, ALU.mult, ALU.add)
            chained(ins)
            dve.wait_ge(lru_gelu, 1)
            dve.tensor_tensor(lru_h, lru_h, uT[:, 12:16, :], ALU.mult).then_inc(lru_yb, 1)
            dve.wait_ge(y_hi, 2)
            dve.tensor_tensor(aT_lo[:, LB:2 * LB, :], lru_h, aT_hi[:, LB:2 * LB, :].bitcast(F32),
                              ALU.subtract).then_inc(y_lo, 1)
            splits(U_WOUT0 + 1, U_SG0 + 1)
            gated(U_SG0, GATE_M)
            norm(G_F, SH_F)

            def swiglu(layer):
                u, j0 = SG_U[layer], H0[layer]
                hj = 2 * NJ_MLP + NJ_SG * layer
                hh = 2 * NJ_MLP + NJ_SG * layer

                def one(v, j, i=None, first=False, kb=None):
                    adas = [] if kb is None else [(1, kb, t, i, 6, 2, plus(kb, i, 2)) for t in range(3)]
                    split_lo(v + 1, i, 6)
                    if adas:
                        ada(*adas[0])
                    split_lo(v + 2, i, 6)
                    if adas:
                        ada(*adas[1])
                    dve.wait_ge(act_h, plus(j0 + j + 1, i, 2))
                    dve.wait_ge(hT_ready, plus(hj + j, i, 2))
                    dve.tensor_tensor(hbuf[:, :, 0:256], gbuf[:, :, 0:256], ub[:, :, 256:512],
                                      ALU.mult).then_inc(h_ready, 1)
                    if not first:
                        split_lo(v + 3, i, 6)
                    if adas:
                        ada(*adas[2])
                    dve.wait_ge(hT_hi_done, plus(hh + j + 1, i, 2))
                    bank_lo(hT_lo[:, 0:2, :], hT_hi[:, 0:2, :],
                            tp[:, 0, :].rearrange("p (b n) -> p b n", n=TOK)).then_inc(hT_lo_done, 1)

                one(u, 0, first=True)
                if layer == 0:
                    dve.wait_ge(ada_bias, 32)
                with dve.Fori(0, 4) as i:
                    for q in range(2):
                        one(u + 2 + 3 * q, 1 + q, i, kb=q if layer == 0 else None)
                for q in range(2):
                    one(u + 2 + 3 * (8 + q), 9 + q)
                split_lo(u + 3 * NJ_SG)
                gated(u + 3 * NJ_SG, gate_ffn[:, :])

            swiglu(0)
            ada_gains()

            norm(G_M, SH_M)
            split_lo(U_QKV2 + 1)
            for c in range(4):
                u = U_QKV2 + 2 * c
                split_lo(u + 2)
                src = acc[:, 2 * (c % 2):2 * (c % 2) + 2, :].rearrange("p t (h d) -> p (t h) d", d=SB_DH)
                dst = tokbuf[:, c % 2, :, :].rearrange("p t (h d) -> p (t h) d", d=SB_DH)
                dve.wait_ge(qk_sq_done, c + 1)
                dve.reduce_sum(qk_ss[:, :], qk_sq, AX.X).then_inc(qk_ss_done, 1)
                if c >= 1:
                    copy_T(qkT, C0["qkv2"] + c - 1, 4 * (c - 1) + 2)
                dve.wait_ge(qk_rstd_done, c + 1)
                if c >= 2:
                    dve.wait_ge(cT1, C0["qkv2"] + c - 1)
                chained(dve.tensor_tensor(dst, src, qk_rstd[:, :].unsqueeze(2).broadcast_to([P, 16, SB_DH]), ALU.mult))
                dve.tensor_tensor(dst, dst, qk_gain[:, c // 2:c // 2 + 1, :].broadcast_to([P, 16, SB_DH]),
                                  ALU.mult).then_inc(chunk_v, 1)
                split_lo(u + 3)
            u = U_QKV2 + 8
            splits(u + 2, u + 3)
            copy_T(qkT, C0["qkv2"] + 3, 14)
            copy_v(u, 0)
            splits(u + 3, u + 5)
            copy_v(u + 2, 1)

            def stick_mask(h):
                dve.wait_ge(z_ready, h + 1)
                if h >= 3:
                    dve.wait_ge(wT_ready, h - 2)
                dve.scalar_tensor_tensor(stick_z[:, h % 3, :], ub[:, h % 2, 0:SC], SB_DH ** -0.5, sb_mask[:, :],
                                         ALU.mult, ALU.add).then_inc(z_masked, 1)

            def stick_arg(h):
                z, f, c = stick_z[:, h % 3, :], stick_sp[:, h % 2, :], stick_sum[:, h % 2, :]
                dve.wait_ge(z_log, h + 1)
                chained(dve.scalar_tensor_tensor(f, z, 0.0, f, ALU.max, ALU.add))
                for lo, n in ((0, P), (P, TOK)):
                    fr = f[:, lo:lo + n][:, ::-1]
                    ins = dve.tensor_tensor_scan(c[:, lo:lo + n][:, ::-1], fr, fr, 0.0, ALU.add, ALU.max)
                chained(ins)
                dve.tensor_tensor(z, z, c, ALU.subtract).then_inc(z_arg, 1)

            def stick_wT_copy(h):
                dve.wait_ge(wT_ready, h + 1)
                if h >= 2:
                    dve.wait_ge(so_ready, h - 1)
                dve.tensor_copy(stick_wT[:, h % 2, :], tp[:, h % 2, 0:SC]).then_inc(wT_copied, 1)

            def stick_lo(b):
                dve.wait_ge(so_hi, 2 * b + 2)
                for e in range(2):
                    q = slice(SB_DH * e, SB_DH * (e + 1))
                    bank_lo(aT_lo[q, b, :], aT_hi[q, b, :], acc[q, 2 * (b % 2) + e, 0:TOK]).then_inc(so_lo, 1)

            stick_mask(0)
            stick_mask(1)
            for h in range(SB_HEADS):
                stick_arg(h)
                if h >= 1:
                    stick_wT_copy(h - 1)
                if h + 2 < SB_HEADS:
                    stick_mask(h + 2)
                if h >= 4 and h % 2 == 0:
                    stick_lo(h // 2 - 2)
            stick_wT_copy(SB_HEADS - 1)
            stick_lo(SB_HEADS // 2 - 2)
            stick_lo(SB_HEADS // 2 - 1)
            splits(U_WOUT1 + 1, U_SG1 + 1)
            gated(U_SG1, GATE_M)
            norm(G_F, SH_F)
            swiglu(1)

        @block.tensor
        def _(pe):
            def matmuls(outp, lhs, rhs, start, stop):
                n = len(lhs)
                for k in range(n):
                    (ah, al), (bh, bl) = lhs[k], rhs[k]
                    pe.matmul(outp, ah, bh, start=start and k == 0, stop=False)
                    pe.matmul(outp, ah, bl, start=False, stop=False)
                    last = pe.matmul(outp, al, bh, start=False, stop=stop and k == n - 1)
                return last

            def unit_ready(u, i=None, per=0):
                pe.wait_ge(lo_v_done, plus(u + 1, i, per))
                pe.wait_ge(lo_p_done, plus(u + 1, i, per))

            def project(u, h, bank, i=None, per=0):
                unit_ready(u, i, per)
                s = u % 2
                rhs = [(w_hi[:, s, k * CH:(k + 1) * CH], w_lo[:, s, k * CH:(k + 1) * CH]) for k in range(4)]
                for t in range(NT):
                    q = slice(t * P, (t + 1) * P)
                    lhs = [(aT_hi[:, 4 * h + k, q], aT_lo[:, 4 * h + k, q]) for k in range(4)]
                    last = matmuls(bank(t), lhs, rhs, h == 0, h == 1)
                last.then_inc(w_used, 1)

            def down(u, h, stop, i=None, per=0):
                unit_ready(u, i, per)
                s = u % 2
                for t in range(NT):
                    q = slice(t * P, (t + 1) * P)
                    lhs = [(hT_hi[:, 2 * h + k, q], hT_lo[:, 2 * h + k, q]) for k in range(2)]
                    for n in range(2):
                        rhs = [(w_hi[:, s, k * D + n * CH:k * D + (n + 1) * CH],
                                w_lo[:, s, k * D + n * CH:k * D + (n + 1) * CH]) for k in range(2)]
                        last = matmuls(acc[:, 2 * t + n, :], lhs, rhs, False, stop)
                last.then_inc(w_used, 1)

            n_norm = [0]

            def norm():
                k = n_norm[0]
                n_norm[0] += 1
                pe.wait_ge(xn_done, 2 * k + 2)
                for g in range(4):
                    if g >= 2:
                        pe.wait_ge(n_lo, 4 * k + g - 1)
                    for b in range(2):
                        for t in range(NT):
                            last = pe.transpose(tp[:, g % 2, b * TOK + t * P:b * TOK + (t + 1) * P],
                                                xn[:, t, (2 * g + b) * P:(2 * g + b + 1) * P], ident[:, :])
                    last.then_inc(nT_done, 1)
                pe.wait_ge(n_lo, 4 * k + 4)

            def project_out(u):
                for n in range(2):
                    for h in range(2):
                        project(u + 2 * n + h, h, lambda t: acc[:, 2 * t + n, :])

            def chunk(u, par, i=None, per=0):
                for h in range(2):
                    project(u + h, h, lambda t: acc[:, 2 * par + t, :], i, per)

            def transposed(par, ct, na, nv, i=None, step=0):
                if na:
                    pe.wait_ge(chunk_a, plus(na, i, step))
                pe.wait_ge(chunk_v, plus(nv, i, step))
                if ct:
                    pe.wait_ge(cT_a, plus(ct, i, step))
                    pe.wait_ge(cT_v, plus(ct, i, step))
                for g, done in enumerate((cT0, cT1)):
                    for b in range(2):
                        for t in range(NT):
                            last = pe.transpose(tp[:, g, b * TOK + t * P:b * TOK + (t + 1) * P],
                                                tokbuf[:, par, t, (2 * g + b) * P:(2 * g + b + 1) * P], ident[:, :])
                    last.then_inc(done, 1)

            def project_pair(u, ct, i=None):
                if i is None or ct:
                    pass
                chunk(u, 0, i, 4)
                chunk(u + 2, 1, i, 4)
                transposed(0, ct, ct + 1, ct + 1, i, 2)
                transposed(1, ct + 1, ct + 2, ct + 2, i, 2)

            pe.wait_ge(consts, 1)
            norm()
            pe.wait_ge(small_loaded, 16 * 13)
            for b in range(LB):
                pe.transpose(ub[:, 0, 16 * b:16 * b + N_ROWS], rows[:, b * P:(b + 1) * P], ident[0:N_ROWS, 0:N_ROWS])
            pe.transpose(ub[:, 0, 64:64 + KB], c_rows[:, :], ident[0:KB, 0:KB]).then_inc(cols_T, 1)
            with pe.Fori(0, 2) as i:
                project_pair(U_QKV1, C0["qkv1"], i)
            chunk(U_QKV1 + 8, 0)
            chunk(U_QKV1 + 10, 1)

            def scores(lo_part, h, q, k):
                pe.matmul(ub[:, h % 2, 0:P], q[:, 0:P], k[:, 0:P], start=True, stop=True)
                return pe.matmul(ub[:, h % 2, P:SC], q[:, P:TOK], k[:, :], start=True, stop=True)

            def weights_T(h, w):
                for n in range(3):
                    last = pe.transpose(tp[:, h % 2, n * P:(n + 1) * P], w[:, n * P:(n + 1) * P], ident[:, :])
                return last

            def weighted(o, wT, v0, v1):
                pe.matmul(o[:, 0:P], v0, wT[:, 0:P], start=True, stop=True)
                pe.matmul(o[:, P:TOK], v0, wT[:, P:2 * P], start=True, stop=False)
                return pe.matmul(o[:, P:TOK], v1, wT[:, 2 * P:SC], start=False, stop=True)

            def att_scores(h):
                if h >= 2:
                    pe.wait_ge(s_max, h - 1)
                scores(0, h, qkT[:, h, :], qkT[:, HEADS + h, :]).then_inc(s_ready, 1)

            pe.wait_ge(cT_a, C0["qkv1"] + 4)
            pe.wait_ge(cT_v, C0["qkv1"] + 4)
            pe.wait_ge(v_a, 2)
            pe.wait_ge(v_v, 2)
            pe.wait_ge(cols_done, 2)
            att_scores(0)
            att_scores(1)
            for h in range(HEADS):
                if h + 2 < HEADS:
                    att_scores(h + 2)
                pe.wait_ge(s_norm, 2 * h + 2)
                if h >= 2:
                    pe.wait_ge(pT_copied, h - 1)
                weights_T(h, prob[:, h % 3, :]).then_inc(pT_ready, 1)
                pe.wait_ge(pT_copied, h + 1)
                if h >= 2:
                    pe.wait_ge(o_lo, h - 1)
                f = slice(h * DH, (h + 1) * DH)
                weighted(acc[:, h % 2, 0:TOK], probT[:, h % 2, :], vtok[:, 0, f], vtok[:, 1, f]).then_inc(o_ready, 1)
            pe.wait_ge(o_lo, HEADS)
            project_out(U_WO1)
            norm()

            def clear_acc():
                for n in range(4):
                    pe.matmul(acc[:, n, :], zeros[:, 0:P], zeros[:, :], start=True, stop=False)

            def hidden(u, i=None, per=0):
                for h in range(2):
                    project(u + h, h, lambda t: ub[:, t, :], i, per)

            def hidden_T(nb, ready, base, i=None, step=0):
                pe.wait_ge(h_ready, plus(ready, i, step[0] if step else 0))
                for g in range(nb):
                    for b in range(2):
                        for t in range(NT):
                            last = pe.transpose(tp[:, g, b * TOK + t * P:b * TOK + (t + 1) * P],
                                                hbuf[:, t, (2 * g + b) * P:(2 * g + b + 1) * P], ident[:, :])
                    last.then_inc(hT_ready, 1)

            pe.wait_ge(consts, 3)
            pe.wait_ge(x_ready, 2)
            clear_acc()
            hidden(U_MLP)
            hidden_T(2, 1, 0)
            with pe.Fori(0, NJ_MLP - 1) as i:
                u = U_MLP + 2
                hidden(u, i, 4)
                pe.wait_ge(hT_lo_done, plus(2, i, 2))
                down(u + 2, 0, False, i, 4)
                down(u + 3, 1, False, i, 4)
                hidden_T(2, 2, 0, i, (1,))
            pe.wait_ge(hT_lo_done, 2 * NJ_MLP)
            down(U_WIN - 2, 0, False)
            down(U_WIN - 1, 1, True)

            n_ada = [0]

            def ada_sums():
                pe.wait_ge(ada_used, 24 * (n_ada[0] + 1))
                for c in range(12):
                    n = 12 * n_ada[0] + c
                    if c >= 2:
                        pe.wait_ge(ada_out, n - 1)
                    pe.matmul(ub[:, c % 2, :], ones[:, :], mod[:, c * CH:(c + 1) * CH], start=True,
                              stop=True).then_inc(ada_sum, 1)
                n_ada[0] += 1

            ada_sums()
            norm()
            with pe.Fori(0, 2) as i:
                project_pair(U_WIN, C0["win"], i)
            chunk(U_WIN + 8, 0)
            transposed(0, C0["win"] + 4, C0["win"] + 5, C0["win"] + 5)
            pe.wait_ge(lru_xr, 1)
            for g in range(2):
                for b in range(LB):
                    last = pe.matmul(acc[:, 2 * g + b // 2, (b % 2) * TOK:(b % 2 + 1) * TOK], rg_w[:, g, b, :],
                                     xr[:, b, :], start=True, stop=True)
                last.then_inc(lru_gate, 1)
            pe.wait_ge(lru_i, 1)
            pe.wait_ge(y_lo, 2)
            project_out(U_WOUT0)
            norm()

            def swiglu(layer):
                u, j0 = SG_U[layer], H0[layer]
                hl = 2 * NJ_MLP + NJ_SG * layer
                clear_acc()
                hidden(u)
                hidden_T(1, j0 + 1, 0)

                def one(v, j, i=None):
                    hidden(v, i, 6)
                    pe.wait_ge(hT_lo_done, plus(hl + j, i, 2))
                    down(v + 2, 0, False, i, 6)
                    hidden_T(1, j0 + j + 1, 0, i, (2,))

                with pe.Fori(0, 4) as i:
                    for q in range(2):
                        one(u + 2 + 3 * q, 1 + q, i)
                for q in range(2):
                    one(u + 2 + 3 * (8 + q), 9 + q)
                pe.wait_ge(hT_lo_done, hl + NJ_SG)
                down(u + 3 * NJ_SG - 1, 0, True)

            swiglu(0)
            ada_sums()
            norm()
            for c in range(4):
                if c >= 2:
                    pe.wait_ge(chunk_v, 9 + c - 1)
                chunk(U_QKV2 + 2 * c, c % 2)
                if c >= 1:
                    transposed((c - 1) % 2, C0["qkv2"] + c - 1, 0, 9 + c)
            pe.wait_ge(chunk_v, 9 + 3)
            chunk(U_QKV2 + 8, 0)
            transposed(1, C0["qkv2"] + 3, 0, 9 + 4)
            chunk(U_QKV2 + 10, 1)

            def stick_scores(h):
                if h >= 2:
                    pe.wait_ge(z_masked, h - 1)
                q = slice(SB_DH * (h % 2), SB_DH * (h % 2 + 1))
                scores(0, h, qkT[q, h // 2, :], qkT[q, KB + h // 2, :]).then_inc(z_ready, 1)

            pe.wait_ge(cT_a, C0["qkv2"] + 4)
            pe.wait_ge(cT_v, C0["qkv2"] + 4)
            pe.wait_ge(v_a, 4)
            pe.wait_ge(v_v, 4)
            stick_scores(0)
            stick_scores(1)
            for h in range(SB_HEADS):
                if h + 2 < SB_HEADS:
                    stick_scores(h + 2)
                pe.wait_ge(z_w, h + 1)
                if h >= 2:
                    pe.wait_ge(wT_copied, h - 1)
                weights_T(h, stick_z[:, h % 3, :]).then_inc(wT_ready, 1)
                pe.wait_ge(wT_copied, h + 1)
                b = h // 2
                if b >= 2:
                    pe.wait_ge(so_lo, 2 * (b - 1))
                f = slice(b * P, (b + 1) * P)
                weighted(acc[:, 2 * (b % 2) + h % 2, 0:TOK], stick_wT[:, h % 2, :], vtok[:, 0, f],
                         vtok[:, 1, f]).then_inc(so_ready, 1)
            pe.wait_ge(so_lo, SB_HEADS)
            project_out(U_WOUT1)
            norm()
            swiglu(1)


_INPUTS = [
    "x", "norm_mix_pre", "norm_mix_post", "norm_ffn_pre", "norm_ffn_post", "w_up", "w_down", "attn_w_qkv", "attn_w_o",
    "c_2", "l0_ada_w_2", "l0_ada_b_2", "l0_mix_norm_2", "l0_w_in_2", "l0_conv_a_w_2", "l0_conv_b_w_2",
    "l0_conv_b_b_2", "l0_rg_a_w_2", "l0_rg_a_b_2", "l0_rg_x_w_2", "l0_rg_x_b_2", "l0_rg_lambda_2", "l0_w_out_2",
    "l0_ffn_norm_2", "l0_ffn_w_gate_2", "l0_ffn_w_up_2", "l0_ffn_w_down_2", "l1_ada_w_2", "l1_ada_b_2",
    "l1_mix_norm_2", "l1_w_qkv_2", "l1_q_norm_2", "l1_k_norm_2", "l1_w_out_2", "l1_ffn_norm_2",
    "l1_ffn_w_gate_2", "l1_ffn_w_up_2", "l1_ffn_w_down_2",
]


def kernel(**inputs):
    import numpy as np
    import concourse.bacc as bacc
    from concourse.bass_utils import run_bass_kernel_spmd

    nc = bacc.Bacc("TRN2", target_bir_lowering=False, num_devices=1)
    arrays, args = {}, {}
    for name in _INPUTS:
        arr = np.ascontiguousarray(inputs[name])
        arrays[f"in_{name}"] = arr
        args[name] = nc.dram_tensor(f"in_{name}", arr.shape, mybir.dt.from_np(arr.dtype), kind="ExternalInput").ap()
    out = nc.dram_tensor("out", (1, TOK, D), F32, kind="ExternalOutput").ap()
    block_program(nc, args, out)
    return run_bass_kernel_spmd(nc, [arrays], core_ids=[0]).results[0]["out"]
```

```python
from contextlib import ExitStack

import concourse.bass as bass
from concourse import mybir

F32 = mybir.dt.float32
F32R = mybir.dt.float32r
ALU = mybir.AluOpType
ACT = mybir.ActivationFunctionType
AX = mybir.AxisListType

P = 128
TOK = 256
NT = TOK // P
D = 1024
KB = D // P
CH = 512
UNIT = 2048
LO_V = 1024
EPS = 1e-6
NEG = -1e30

HEADS = 8
DH = D // HEADS
SB_HEADS = 16
SB_DH = D // SB_HEADS
LRU = 512
LB = LRU // P
LRU_HEAD = 64
RG_C = 8.0
F_MLP = 4096
F_SG = 2816
NJ_MLP = F_MLP // CH
NJ_SG = F_SG // 256
SC = P + TOK

U_QKV1 = 0
U_WO1 = U_QKV1 + 12
U_MLP = U_WO1 + 4
U_WIN = U_MLP + 4 * NJ_MLP
U_WOUT0 = U_WIN + 10
U_SG0 = U_WOUT0 + 4
U_QKV2 = U_SG0 + 3 * NJ_SG
U_WOUT1 = U_QKV2 + 12
U_SG1 = U_WOUT1 + 4
U_END = U_SG1 + 3 * NJ_SG

R_CONV_A, R_CONV_B, R_CONV_BIAS, R_RG_A, R_RG_X, R_LAMBDA, N_ROWS = 0, 3, 7, 8, 9, 10, 11


def steps(text):
    return [(s[0], int(s[1:])) for s in text.split()]


ATT_STEPS = steps("""L1 U0 H2 L2 U1 H3 E0 L3 U2 H4 T0 L4 U3 H5 L5 E1 X0 U4 H6 T1 L6 Y0 U5 H7 E2 S0 L7 U6 H8 T2 A0 S1 L8
    U7 H9 E3 L9 W0 A1 S2 U8 H10 T3 W1 L10 A2 S3 U9 H11 E4 W2 L11 A3 S4 U10 H12 W3 L12 A4 S5 A5
    U11 E5 S6 W4 S7 W5 V0 V1 V2 V3 H13 L13 A6 A7 U12 W6 W7 V4 V5 V6 V7 H14 L14 U13 H15 L15
    U14 H16 L16 U15""")
STICK_STEPS = steps("""L1 U0 H2 L2 U1 H3 L3 E0 U2 H4 N0 L4 U3 H5 L5 T0 E1 U4 H6 N1 L6 U5 H7 L7 T1 E2
    U6 H8 S0 S1 L8 N2 A0 A1 U7 H9 W0 W1 T2 S2 S3 L9 A2 A3 E3 U8 H10 W2 W3 S4 S5 L10 N3 A4 A5
    U9 E4 H11 T3 W4 W5 S6 S7 L11 A6 A7 U10 H12 W6 W7 S8 S9 S10 L12 A8 A9 A10
    U11 E5 H13 W8 W9 W10 V0 V1 V2 V3 V4 V5 V6 V7 S11 S12 S13 L13 A11 A12 A13 U12 H14 W11 W12 W13 S14 S15 L14 A14 A15
    U13 H15 W14 W15 L15 V8 V9 V10 V11 V12 V13 V14 V15 U14 H16 U15""")
LRU_STEPS = steps("""B0 B1 L1 U0 H2 L2 U1 H3 E0 L3 M0 U2 H4 T0 L4 C0 B2 U3 H5 E1 L5 M1 U4 H6 G0 T1 L6 B3 M2 U5 H7 G1 D0 E2 L7 M3
    U6 H8 T2 L8 B4 M4 D1 Q0 U7 H9 L9 B5 E3 M5 P0 U8 H10 T3 L10 Y0 B6 U9 E4 H11 L11 K0 B7 U10 H12 T4 L12 Z0 M6
    U11 H13 L13 M7 U12 H14 U13""")
ADA_ORDER = (0, 1, 2, 3, 10, 11, 4, 5, 6, 7, 8, 9), (0, 1, 2, 3, 4, 5, 6, 7, 8, 9, 10, 11)
QKV_CHUNKS = (0, 2, 1, 3, 4, 5)
WIN_CHUNKS = (4, 1, 2, 3, 0)
OUT_LO_FIRST = ((0, 0), (1, 0), (0, 1), (1, 1))
OUT_HI_FIRST = ((0, 1), (1, 1), (0, 0), (1, 0))


def plus(base, i, per):
    return base if i is None else i * per + base


def block_program(nc, a, out):
    ctx = ExitStack()
    with ctx:
        def sb(name, shape, dt=F32):
            return ctx.enter_context(nc.sbuf_tensor(name, shape, dt))

        def ps(name, shape):
            return ctx.enter_context(nc.psum_tensor(name, shape, F32))

        def sem(name):
            return ctx.enter_context(nc.semaphore(name))

        w_raw = sb("w_raw", [P, 2, UNIT])
        w_hi = sb("w_hi", [P, 2, UNIT], F32R)
        w_lo = sb("w_lo", [P, 2, UNIT], F32R)
        ada_raw = sb("ada_raw", [P, 3, UNIT])
        mod = sb("mod", [P, 6 * D])
        gate_ffn = sb("gate_ffn", [P, D])
        x = sb("x", [P, NT, D])
        xn = sb("xn", [P, NT, D])
        aT_hi = sb("aT_hi", [P, KB, TOK], F32R)
        aT_lo = sb("aT_lo", [P, KB, TOK], F32R)
        hT_hi = sb("hT_hi", [P, 4, TOK], F32R)
        hT_lo = sb("hT_lo", [P, 4, TOK], F32R)
        gain = sb("gain", [P, 4, D])
        qk_gain = sb("qk_gain", [P, 2, SB_DH])
        scratch = sb("scratch", [P, 10240])
        ident = sb("ident", [P, P])
        ones = sb("ones", [P, P])
        zeros = sb("zeros", [P, CH], F32R)
        neg_dist = sb("neg_dist", [P, SC])
        sb_mask = sb("sb_mask", [P, SC])
        cols = sb("cols", [P, LB, 16])
        silu_c = sb("silu_c", [P, KB])
        rg_w = sb("rg_w", [P, 2, LB, P])
        lam = sb("lam", [P, 10, LB])
        sums = sb("sums", [P, 2])
        var = sb("var", [P, 2])
        rstd = sb("rstd", [P, 2])
        half = sb("half", [P, 16])
        qk_ss = sb("qk_ss", [P, 16])
        qk_var = sb("qk_var", [P, 16])
        qk_rstd = sb("qk_rstd", [P, 16])
        att_max = sb("att_max", [P, 4, 2])
        att_nmax = sb("att_nmax", [P, 4, 2])
        att_sum = sb("att_sum", [P, 4, 2])
        att_rsum = sb("att_rsum", [P, 4, 2])

        tokbuf = scratch[:, 0:2048].rearrange("p (c t n) -> p c t n", c=2, t=NT)
        qkT = scratch[:, 2048:6144].rearrange("p (b n) -> p b n", n=TOK)
        vtok = scratch[:, 6144:8192].rearrange("p (t n) -> p t n", t=NT)
        uT = scratch[:, 2048:7168].rearrange("p (b n) -> p b n", n=TOK)
        prob = scratch[:, 8192:8192 + 4 * SC].rearrange("p (r n) -> p r n", r=4)
        ada_flat = ada_raw[:, :, :].rearrange("p a n -> p (a n)")
        probT = ada_flat[:, 0:HEADS * SC].rearrange("p (h n) -> p h n", h=HEADS)
        rows = scratch[0:N_ROWS, 8192:8192 + LRU]
        c_rows = scratch[0:KB, 8192 + LRU:8192 + LRU + P]
        xn_flat = xn[:, :, :].rearrange("p t n -> p (t n)")
        stick_z = scratch[:, 8192:8192 + 4 * SC].rearrange("p (r n) -> p r n", r=4)
        stick_wT = ada_flat[:, 0:SB_HEADS * SC].rearrange("p (h n) -> p h n", h=SB_HEADS)
        stick_sp = gain[:, 0, 0:2 * SC].rearrange("p (r n) -> p r n", r=2)
        stick_sum = gain[:, 1, 0:2 * SC].rearrange("p (r n) -> p r n", r=2)
        qk_sq = xn_flat[:, 0:1024].rearrange("p (h d) -> p h d", d=SB_DH)
        def lru_buf(ap):
            return ap.rearrange("p (b n) -> p b n", n=TOK)
        conv_a = lru_buf(ada_raw[:, 2, 0:1024])
        xr = lru_buf(ada_raw[:, 2, 1024:2048])
        gate_r = lru_buf(scratch[:, 7168:8192])
        gate_i = lru_buf(scratch[:, 8192:9216])
        lru_b = lru_buf(scratch[:, 9216:10240])
        lru_a = lru_buf(xn_flat[:, 0:1024])
        lru_h = lru_buf(xn_flat[:, 1024:2048])
        hbuf = scratch[:, 0:1024].rearrange("p (t n) -> p t n", t=NT)
        gbuf = scratch[:, 1024:2048].rearrange("p (t n) -> p t n", t=NT)
        squares = scratch[:, 0:2048].rearrange("p (t n) -> p t n", t=NT)

        acc = ps("acc", [P, 4, CH])
        ub = ps("ub", [P, 2, CH])
        tp = ps("tp", [P, 2, CH])
        o_bank = [acc[:, b, :] for b in range(4)] + [ub[:, 0, :], ub[:, 1, :], tp[:, 0, :], tp[:, 1, :]]

        def acc_tile(t):
            return acc[:, 2 * t:2 * t + 2, :].rearrange("p b n -> p (b n)")

        def norm_banks(k, t):
            if t == 0:
                return [tp[:, 0, :], tp[:, 1, :]]
            return [acc[:, 2, :], acc[:, 3, :]] if k in (1, 3, 5) else [ub[:, 0, :], ub[:, 1, :]]

        x_loaded = [sem("x_loaded0"), sem("x_loaded1")]
        small_loaded = sem("small_loaded")
        gain_loaded = [sem(f"gain_loaded{n}") for n in range(8)]
        w_loaded = [sem("w_loaded0"), sem("w_loaded1")]
        hi_done = sem("hi_done")
        lo_v_done = sem("lo_v_done")
        lo_p_done = sem("lo_p_done")
        w_used = sem("w_used")
        tile0_done = sem("tile0_done")
        ada_loaded = [sem(f"ada_loaded{n}") for n in range(3)]
        ada_bias = sem("ada_bias")
        ada_zero = sem("ada_zero")
        ada_used = sem("ada_used")
        ada_sum = sem("ada_sum")
        ada_out = sem("ada_out")
        ada_gain_done = sem("ada_gain_done")
        consts = sem("consts")
        pool_chain = sem("pool_chain")
        dve_chain = sem("dve_chain")
        act_chain = sem("act_chain")
        cols_T = sem("cols_T")
        cols_done = sem("cols_done")
        lam_exp = sem("lam_exp")
        lam_done = sem("lam_done")
        sq_done = sem("sq_done")
        rstd_done = sem("rstd_done")
        xn_done = sem("xn_done")
        nT_done = sem("nT_done")
        n_hi = sem("n_hi")
        n_lo = sem("n_lo")
        x_ready = sem("x_ready")
        chunk_a = sem("chunk_a")
        chunk_v = sem("chunk_v")
        cT0 = sem("cT0")
        cT1 = sem("cT1")
        cT_a = sem("cT_a")
        cT_v = sem("cT_v")
        v_a = sem("v_a")
        v_v = sem("v_v")
        qk_sq_done = sem("qk_sq_done")
        qk_ss_done = sem("qk_ss_done")
        qk_rstd_done = sem("qk_rstd_done")
        s_ready = sem("s_ready")
        s_max = sem("s_max")
        s_exp = sem("s_exp")
        s_norm = sem("s_norm")
        pT_ready = sem("pT_ready")
        pT_copied = sem("pT_copied")
        o_ready = sem("o_ready")
        o_hi = sem("o_hi")
        o_lo = sem("o_lo")
        z_ready = sem("z_ready")
        z_masked = sem("z_masked")
        z_log = sem("z_log")
        z_cum = sem("z_cum")
        z_arg = sem("z_arg")
        z_w = sem("z_w")
        wT_ready = sem("wT_ready")
        wT_copied = sem("wT_copied")
        so_ready = sem("so_ready")
        so_hi = sem("so_hi")
        so_lo = sem("so_lo")
        act_h = sem("act_h")
        h_ready = sem("h_ready")
        hT_ready = sem("hT_ready")
        hT_hi_done = sem("hT_hi_done")
        hT_lo_done = sem("hT_lo_done")
        lru_p = sem("lru_p")
        lru_conv = sem("lru_conv")
        lru_xr = sem("lru_xr")
        lru_gate = sem("lru_gate")
        lru_r = sem("lru_r")
        lru_i = sem("lru_i")
        lru_t = sem("lru_t")
        lru_ix = sem("lru_ix")
        lru_a2 = sem("lru_a2")
        lru_s2 = sem("lru_s2")
        lru_sqrt = sem("lru_sqrt")
        lru_ya = sem("lru_ya")
        lru_yb = sem("lru_yb")
        y_hi = sem("y_hi")
        y_lo = sem("y_lo")
        stored = sem("stored")

        def blocks(w):
            return w.rearrange("(k p) n -> p k n", p=P)
        qkv1, wo1, up1, down1 = (blocks(a[n][0]) for n in ("attn_w_qkv", "attn_w_o", "w_up", "w_down"))
        w_in, w_out0 = blocks(a["l0_w_in_2"]), blocks(a["l0_w_out_2"])
        qkv2, w_out1 = blocks(a["l1_w_qkv_2"]), blocks(a["l1_w_out_2"])
        sg = [[blocks(a[f"l{n}_ffn_w_{m}_2"]) for m in ("gate", "up", "down")] for n in (0, 1)]
        ada_w = [blocks(a[f"l{n}_ada_w_2"]) for n in (0, 1)]
        ada_b = [a[f"l{n}_ada_b_2"].rearrange("(a n) -> a n", a=1) for n in (0, 1)]
        gains = [a["norm_mix_pre"][0], a["norm_mix_post"][0], a["norm_ffn_pre"][0], a["norm_ffn_post"][0],
                 a["l0_mix_norm_2"], a["l0_ffn_norm_2"], a["l1_mix_norm_2"], a["l1_ffn_norm_2"]]

        H0 = {"mlp": 0, 0: NJ_MLP, 1: NJ_MLP + NJ_SG}
        C0 = {"qkv1": 0, "win": 4, "qkv2": 9}
        SG_U = (U_SG0, U_SG1)

        block = ctx.enter_context(nc.Block())

        @block.sync
        def _(sp):
            def load_unit(u, pieces, i=None, per=0):
                if u >= 2:
                    sp.wait_ge(lo_v_done, plus(u - 1, i, per))
                    sp.wait_ge(lo_p_done, plus(u - 1, i, per))
                for dst, src in pieces:
                    sp.dma_start(dst, src).then_inc(w_loaded[u % 2], 16)

            def proj_half(u, w, col, h, i=None, per=0):
                dst = w_raw[:, u % 2, :].rearrange("p (k n) -> p k n", n=CH)
                load_unit(u, [(dst[:, 2 * q:2 * q + 2, :],
                               w[:, 4 * h + 2 * q:4 * h + 2 * q + 2, bass.ds(col, CH)]) for q in range(2)], i, per)

            def proj(u, w, col, i=None, per=0):
                for h in range(2):
                    proj_half(u + h, w, col, h, i, per)

            def project_out(u, w, order):
                for n, (c, h) in enumerate(order):
                    proj_half(u + n, w, c * CH, h)

            def down(u, w, row_block, i=None, per=0):
                dst = w_raw[:, u % 2, :].rearrange("p (k n) -> p k n", n=D)
                load_unit(u, [(dst[:, q:q + 1, :], w[:, bass.ds(row_block + q, 1), :]) for q in range(2)], i, per)

            def gate_up(u, layer, col, i=None, per=0):
                for h in range(2):
                    dst = w_raw[:, (u + h) % 2, :].rearrange("p (k n) -> p k n", n=CH)
                    load_unit(u + h, [(dst[:, :, 256 * m:256 * m + 256],
                                       sg[layer][m][:, 4 * h:4 * h + 4, bass.ds(col, 256)])
                                      for m in range(2)], i, per)

            def load_ada(slot, rb, cols_of, count, before=None, i=None, per=0):
                if before is not None:
                    sp.wait_ge(ada_used, plus(before, i, per))
                layer, third = cols_of
                src = ada_w[layer][:, bass.ds(rb, 1), third * UNIT:(third + 1) * UNIT]
                sp.dma_start(ada_raw[:, slot:slot + 1, :], src).then_inc(ada_loaded[slot], 16)

            def load_gain(n):
                sp.dma_start(gain[:, n % 4, :], gains[n].partition_broadcast(P)).then_inc(gain_loaded[n], 16)

            def load_x(t):
                sp.dma_start(x[:, t, :], a["x"][0, t * P:(t + 1) * P, :]).then_inc(x_loaded[t], 16)

            load_x(0)
            proj_half(U_QKV1, qkv1, 0, 0)
            load_gain(0)
            load_x(1)
            proj_half(U_QKV1 + 1, qkv1, 0, 1)
            proj_half(U_QKV1 + 2, qkv1, QKV_CHUNKS[1] * CH, 0)
            small = [(rows[R_CONV_A:R_CONV_A + 3, :], a["l0_conv_a_w_2"]),
                     (rows[R_CONV_B:R_CONV_B + 4, :], a["l0_conv_b_w_2"]),
                     (rows[R_CONV_BIAS:R_CONV_BIAS + 1, :], a["l0_conv_b_b_2"].rearrange("(a n) -> a n", a=1)),
                     (rows[R_RG_A:R_RG_A + 1, :], a["l0_rg_a_b_2"].rearrange("(a h) n -> a (h n)", a=1)),
                     (rows[R_RG_X:R_RG_X + 1, :], a["l0_rg_x_b_2"].rearrange("(a h) n -> a (h n)", a=1)),
                     (rows[R_LAMBDA:R_LAMBDA + 1, :], a["l0_rg_lambda_2"].rearrange("(a n) -> a n", a=1)),
                     (c_rows[:, :], a["c_2"].rearrange("a (k p) -> (a k) p", p=P)),
                     (qk_gain[:, 0, :], a["l1_q_norm_2"].partition_broadcast(P)),
                     (qk_gain[:, 1, :], a["l1_k_norm_2"].partition_broadcast(P))]
            sp.wait_ge(consts, 1)
            for g, name in enumerate(("l0_rg_a_w_2", "l0_rg_x_w_2")):
                for e in range(2):
                    q = slice(LRU_HEAD * e, LRU_HEAD * (e + 1))
                    small.append((rg_w[q, g, :, q], a[name].rearrange("(b e) i j -> e i b j", e=2)[e]))
            for dst, src in small:
                sp.dma_start(dst, src).then_inc(small_loaded, 16)
            proj_half(U_QKV1 + 3, qkv1, QKV_CHUNKS[1] * CH, 1)
            load_gain(1)
            for c in range(2, 6):
                proj(U_QKV1 + 2 * c, qkv1, QKV_CHUNKS[c] * CH)
            sp.wait_ge(ada_zero, 1)
            sp.dma_start(mod[0:1, :], ada_b[0]).then_inc(ada_bias, 16)
            load_gain(2)
            load_gain(3)
            project_out(U_WO1, wo1, OUT_LO_FIRST)
            proj(U_MLP, up1, 0)
            sp.wait_ge(o_ready, HEADS)
            for third in range(3):
                load_ada(third, 0, (0, third), third)
            with sp.Fori(0, NJ_MLP - 1) as i:
                u = U_MLP + 2
                proj(u, up1, i * CH + CH, i, 4)
                load_ada(0, i + 1, (0, 0), 3, 1, i, 3)
                down(u + 2, down1, i * 4, i, 4)
                load_ada(1, i + 1, (0, 1), 4, 2, i, 3)
                down(u + 3, down1, i * 4 + 2, i, 4)
                load_ada(2, i + 1, (0, 2), 5, 3, i, 3)
            for h in range(2):
                down(U_WIN - 2 + h, down1, 4 * (NJ_MLP - 1) + 2 * h)
            sp.wait_ge(xn_done, 4)
            load_gain(4)
            load_gain(5)
            load_gain(6)
            for c in range(2):
                proj(U_WIN + 2 * c, w_in, WIN_CHUNKS[c] * CH)
            sp.wait_ge(ada_zero, 2)
            sp.dma_start(mod[0:1, 0:UNIT], ada_b[1][:, 0:UNIT]).then_inc(ada_bias, 16)
            sp.wait_ge(x_ready, 4)
            load_gain(7)

            for c in range(2, 5):
                proj(U_WIN + 2 * c, w_in, WIN_CHUNKS[c] * CH)
            project_out(U_WOUT0, w_out0, OUT_HI_FIRST)

            def swiglu(layer):
                u = SG_U[layer]
                gate_up(u, layer, 0)
                if layer == 0:
                    sp.wait_ge(ada_zero, 3)
                    sp.dma_start(mod[0:1, UNIT:], ada_b[1][:, UNIT:]).then_inc(ada_bias, 16)

                def pair(i, base, with_ada):
                    for q in range(2):
                        v = u + 2 + 3 * (base - 1 + q)
                        gate_up(v, layer, plus(256 * (base + q), i, 512), i, 6)
                        if with_ada:
                            load_ada(0, plus(q, i, 2), (1, 1), 32 + 2 * q, 31 + 2 * q, i, 4)
                        down(v + 2, sg[layer][2], plus(2 * (base - 1 + q), i, 4), i, 6)
                        if with_ada:
                            load_ada(1, plus(q, i, 2), (1, 2), 33 + 2 * q, 32 + 2 * q, i, 4)

                with sp.Fori(0, 4) as i:
                    pair(i, 1, layer == 0)
                pair(None, 9, False)
                down(u + 3 * NJ_SG - 1, sg[layer][2], 2 * (NJ_SG - 1))

            swiglu(0)
            for c in range(6):
                proj(U_QKV2 + 2 * c, qkv2, QKV_CHUNKS[c] * CH)
            project_out(U_WOUT1, w_out1, OUT_LO_FIRST)
            swiglu(1)
            for t in range(NT):
                sp.wait_ge(x_ready, 11 + t)
                sp.dma_start(out[0, t * P:(t + 1) * P, :], x[:, t, :]).then_inc(stored, 16)
            sp.wait_ge(stored, 16 * NT)

        @block.gpsimd
        def _(pool):
            n_chain = [0]

            def chained(ins):
                n_chain[0] += 1
                ins.then_inc(pool_chain, 1)
                pool.wait_ge(pool_chain, n_chain[0])

            def split_lo(u, i=None, per=0):
                if u >= U_END:
                    return
                pool.wait_ge(hi_done, plus(u + 1, i, per))
                s = u % 2
                pool.tensor_tensor(w_lo[:, s, LO_V:], w_raw[:, s, LO_V:], w_hi[:, s, LO_V:].bitcast(F32),
                                   ALU.subtract).then_inc(lo_p_done, 1)

            def splits(u0, u1):
                for u in range(u0, u1):
                    split_lo(u)

            n_rstd = [0]

            def row_rstd(first=False):
                for t in range(NT):
                    if first and t == 1:
                        split_lo(0)
                    n_rstd[0] += 1
                    pool.wait_ge(sq_done, n_rstd[0])
                    chained(pool.tensor_scalar(var[:, t:t + 1], sums[:, t:t + 1], 1.0 / D, EPS, ALU.mult, ALU.add))
                    pool.tensor_tensor(rstd[:, t:t + 1], var[:, t:t + 1], half[:, 0:1], ALU.pow).then_inc(rstd_done, 1)

            chained(pool.memset(half[:, :], -0.5))
            chained(pool.memset(ident[:, :], 0.0))
            chained(pool.affine_select(out=ident[:, :], in_=ident[:, :], compare_op=ALU.not_equal, fill=1.0,
                                       base=0, pattern=[[-1, P]], channel_multiplier=1))
            pool.memset(rg_w[:, :, :, :], 0.0).then_inc(consts, 1)
            row_rstd(first=True)
            splits(1, 2)
            pool.memset(ones[:, :], 1.0).then_inc(consts, 1)
            pool.memset(zeros[:, :].bitcast(F32), 0.0).then_inc(consts, 1)
            chained(pool.iota(neg_dist[:, 0:P], pattern=[[1, P]], base=0, channel_multiplier=-1,
                              allow_small_or_imprecise_dtypes=True))
            chained(pool.iota(neg_dist[:, P:SC], pattern=[[1, TOK]], base=-P, channel_multiplier=-1,
                              allow_small_or_imprecise_dtypes=True))
            chained(pool.memset(sb_mask[:, :], 0.0))
            for m, keep_diag in ((neg_dist, 0), (sb_mask, -1)):
                for lo, n, q0 in ((0, P, 0), (P, TOK, P)):
                    part = m[:, lo:lo + n]
                    pool.affine_select(out=part, in_=part, compare_op=ALU.is_ge, fill=NEG, base=q0 + keep_diag,
                                       pattern=[[-1, n]], channel_multiplier=1).then_inc(consts, 1)
            for step, n in ATT_STEPS:
                if step == "H" and n < 16:
                    split_lo(U_QKV1 + n)
                elif step == "E" and n == 0:
                    pool.memset(mod[:, 0:3 * D], 0.0)
                elif step == "E" and n == 1:
                    pool.memset(mod[:, 3 * D:], 0.0).then_inc(ada_zero, 1)
            row_rstd()
            row_rstd()
            splits(U_MLP, U_MLP + 3)
            with pool.Fori(0, NJ_MLP - 1) as i:
                for q in range(4):
                    split_lo(U_MLP + 3 + q, i, 4)
            splits(U_MLP + 3 + 4 * (NJ_MLP - 1), U_WIN)
            row_rstd()
            row_rstd()
            splits(U_WIN, U_WIN + 2)
            pool.wait_ge(xn_done, 6)
            pool.memset(mod[:, 0:UNIT], 0.0).then_inc(ada_zero, 1)
            for step, n in LRU_STEPS:
                if step == "H" and n < 14:
                    split_lo(U_WIN + n)
                elif step == "P":
                    pool.wait_ge(cT_a, C0["win"] + 3)
                    pool.wait_ge(cT_v, C0["win"] + 3)
                    pool.tensor_tensor(uT[:, 4:8, :], uT[:, 4:8, :], uT[:, 8:12, :], ALU.mult).then_inc(lru_p, 1)
                elif step == "D" and n == 0:
                    pool.wait_ge(lru_i, 1)
                    pool.wait_ge(lru_xr, 1)
                    pool.tensor_tensor(gate_i, gate_i, xr, ALU.mult).then_inc(lru_ix, 1)
            row_rstd()

            def swiglu(layer):
                u = SG_U[layer]
                if layer == 0:
                    splits(u, u + 2)
                    pool.wait_ge(xn_done, 8)
                    pool.memset(mod[:, UNIT:], 0.0).then_inc(ada_zero, 1)
                    split_lo(u + 2)
                else:
                    splits(u, u + 3)
                with pool.Fori(0, 4) as i:
                    for q in range(6):
                        split_lo(u + 3 + q, i, 6)
                splits(u + 3 + 24, u + 3 * NJ_SG)

            swiglu(0)
            row_rstd()
            splits(U_QKV2, U_QKV2 + 2)
            for step, n in STICK_STEPS:
                if step == "H" and n < 16:
                    split_lo(U_QKV2 + n)
                elif step == "E" and n < 4:
                    pool.wait_ge(qk_ss_done, n + 1)
                    chained(pool.tensor_scalar(qk_var[:, :], qk_ss[:, :], 1.0 / SB_DH, EPS, ALU.mult, ALU.add))
                    pool.tensor_tensor(qk_rstd[:, :], qk_var[:, :], half[:, :], ALU.pow).then_inc(qk_rstd_done, 1)
                elif step == "A":
                    pool.wait_ge(z_cum, n + 1)
                    z = stick_z[:, n % 4, :]
                    pool.tensor_tensor(z, z, stick_sum[:, n % 2, :], ALU.subtract).then_inc(z_arg, 1)
            row_rstd()
            swiglu(1)

        @block.scalar
        def _(act):
            n_chain = [0]

            def chained(ins):
                n_chain[0] += 1
                ins.then_inc(act_chain, 1)
                act.wait_ge(act_chain, n_chain[0])

            def split_hi(u, i=None, per=0):
                if u >= U_END:
                    return
                act.wait_ge(w_loaded[u % 2], plus(32 * (u // 2 + 1), i, 16 * per))
                if u >= 2:
                    act.wait_ge(w_used, plus(u - 1, i, per))
                act.activation(w_hi[:, u % 2, :], w_raw[:, u % 2, :], ACT.Copy).then_inc(hi_done, 1)

            def splits(u0, u1):
                for u in range(u0, u1):
                    split_hi(u)

            def row_square(t, src):
                act.activation(squares[:, t, :], src, ACT.Square, accum_out=sums[:, t:t + 1]).then_inc(sq_done, 1)

            n_norm, n_update = [0], [0]

            def norm(u, layer=None, parts=(0, 0, 0, 0)):
                k = n_norm[0]
                n_norm[0] += 1
                ada_parts(layer, parts[0], parts[1])
                for t in range(NT):
                    if k == 0:
                        act.wait_ge(x_loaded[t], 16)
                    else:
                        act.wait_ge(x_ready, 2 * (k - 1) + t + 1)
                    row_square(t, x[:, t, :])
                    if k == 0 and t == 0:
                        split_hi(u)
                        norm_hi(k, 0)
                    ada_parts(layer, parts[1 + t], parts[2 + t])
                if k:
                    norm_hi(k, 0)
                split_hi(u + 1)
                norm_hi(k, 1)

            def norm_hi(k, t):
                for g in range(2):
                    act.wait_ge(nT_done, 4 * k + 2 * t + g + 1)
                    act.activation(aT_hi[:, 4 * g:4 * g + 4, t * P:(t + 1) * P],
                                   norm_banks(k, t)[g].rearrange("p (b n) -> p b n", n=P), ACT.Copy).then_inc(n_hi, 1)

            def post_norm(n, u_end):
                act.wait_ge(tile0_done, n + 1)
                row_square(0, acc_tile(0))
                act.wait_ge(w_used, u_end)
                row_square(1, acc_tile(1))

            def ada_parts(layer, n0, n1):
                for n in range(n0, n1):
                    c = ADA_ORDER[layer][n]
                    if layer and c == 10:
                        act.wait_ge(x_ready, 8)
                    act.wait_ge(ada_sum, 12 * layer + n + 1)
                    dst = mod[:, c * CH:(c + 1) * CH] if c < 10 else gate_ffn[:, (c - 10) * CH:(c - 9) * CH]
                    act.activation(dst, ub[:, n % 2, :], ACT.Copy).then_inc(ada_out, 1)

            def copy_chunk(u, bank, ct):
                act.wait_ge(w_used, u + 2)
                if ct >= 2:
                    act.wait_ge(cT1, ct - 1)
                act.activation(tokbuf[:, ct % 2, 0, :], bank, ACT.Copy).then_inc(chunk_a, 1)

            def copy_T(dst, ct, b):
                act.wait_ge(cT0, ct + 1)
                act.activation(dst[:, b:b + 2, :], tp[:, 0, :].rearrange("p (b n) -> p b n", n=TOK),
                               ACT.Copy).then_inc(cT_a, 1)

            def copy_v(u, n):
                act.wait_ge(w_used, u + 2)
                act.activation(vtok[:, 0, n * CH:(n + 1) * CH], acc[:, 2 * n, :], ACT.Copy).then_inc(v_a, 1)

            norm(U_QKV1)
            for step, n in ATT_STEPS:
                if step == "H":
                    split_hi(U_QKV1 + n)
                elif step == "X":
                    act.wait_ge(cols_T, 1)
                    act.activation(cols[:, :, 0:N_ROWS], ub[:, 0, 0:64].rearrange("p (b r) -> p b r", r=16)[:, :, 0:N_ROWS],
                                   ACT.Copy).then_inc(cols_done, 1)
                    act.activation(silu_c[:, :], ub[:, 0, 64:64 + KB], ACT.Silu).then_inc(cols_done, 1)
                    act.wait_ge(cols_done, 1)
                    chained(act.activation(lam[:, 0, :], cols[:, :, R_LAMBDA], ACT.Abs))
                    act.activation(lam[:, 1, :], lam[:, 0, :], ACT.Exp, scale=-1.0).then_inc(lam_exp, 1)
                elif step == "E" and n < 4:
                    copy_chunk(U_QKV1 + 2 * n, acc[:, 2 * (n % 2), :], C0["qkv1"] + n)
                elif step == "E":
                    copy_v(U_QKV1 + 2 * n, n - 4)
                elif step == "T":
                    copy_T(qkT, C0["qkv1"] + n, 4 * QKV_CHUNKS[n])
                elif step == "A":
                    act.wait_ge(s_max, n + 1)
                    r = n % 4
                    for t, lo, w in ((0, 0, P), (1, P, TOK)):
                        act.activation(prob[:, r, lo:lo + w], prob[:, r, lo:lo + w], ACT.Exp, scale=DH ** -0.5,
                                       bias=att_nmax[:, r, t:t + 1], accum_out=att_sum[:, r, t:t + 1]).then_inc(s_exp, 1)
                elif step == "W":
                    act.wait_ge(pT_ready, n + 1)
                    act.activation(probT[:, n, :], tp[:, n % 2, 0:SC], ACT.Copy).then_inc(pT_copied, 1)
                elif step == "V":
                    act.wait_ge(o_ready, n + 1)
                    act.activation(aT_hi[:, n, :], o_bank[n][:, 0:TOK], ACT.Copy).then_inc(o_hi, 1)
            post_norm(0, U_MLP)
            norm(U_MLP)

            def mlp_slice(u, j, i=None, first=False):
                if not first:
                    split_hi(u + 1, i, 4)
                split_hi(u + 2, i, 4)
                if not first:
                    split_hi(u + 3, i, 4)
                act.wait_ge(w_used, plus(u + 2, i, 4))
                if j >= 1:
                    act.wait_ge(h_ready, plus(j, i, 1))
                act.activation(gbuf, ub[:, :, :], ACT.Relu).then_inc(act_h, 1)
                if not first:
                    split_hi(u + 4, i, 4)
                for g in range(2):
                    act.wait_ge(hT_ready, plus(2 * j + g + 1, i, 2))
                    act.activation(hT_hi[:, 2 * g:2 * g + 2, :], tp[:, g, :].rearrange("p (b n) -> p b n", n=TOK),
                                   ACT.Copy).then_inc(hT_hi_done, 1)

            mlp_slice(U_MLP, 0, first=True)
            with act.Fori(0, NJ_MLP - 1) as i:
                mlp_slice(U_MLP + 2, 1, i)
            ada_parts(0, 0, 6)
            splits(U_WIN - 1, U_WIN + 1)
            post_norm(1, U_WIN)
            norm(U_WIN, 0, (6, 8, 10, 12))
            for step, n in LRU_STEPS:
                if step == "H":
                    split_hi(U_WIN + n)
                elif step == "B":
                    if n >= 2:
                        act.wait_ge(ada_used, 24 + n - 1)
                    act.dma_start(ada_raw[:, n % 2:n % 2 + 1, :], ada_w[1][:, n:n + 1, 0:UNIT]).then_inc(ada_loaded[n % 2], 16)
                elif step == "E" and n == 3:
                    act.wait_ge(w_used, U_WIN + 8)
                    act.wait_ge(cT1, C0["win"] + 2)
                    for t, done in ((0, chunk_a), (1, chunk_v)):
                        act.activation(tokbuf[:, (C0["win"] + 3) % 2, t, :], acc[:, 2 + t, :],
                                       ACT.Gelu_apprx_tanh).then_inc(done, 1)
                elif step == "E":
                    copy_chunk(U_WIN + 2 * n, ub[:, 0, :] if n == 4 else acc[:, 2 * (n % 2), :], C0["win"] + n)
                elif step == "T":
                    copy_T(uT, C0["win"] + n, 4 * WIN_CHUNKS[n])
                elif step == "G":
                    dst, row, done = ((gate_r, R_RG_A, lru_r), (gate_i, R_RG_X, lru_i))[n]
                    act.wait_ge(lru_gate, n + 1)
                    for b in range(LB):
                        last = act.activation(dst[:, b, :], ub[:, b // 2, (b % 2) * TOK:(b % 2 + 1) * TOK],
                                              ACT.Sigmoid, bias=cols[:, b, row:row + 1])
                    last.then_inc(done, 1)
                elif step == "D" and n == 0:
                    act.wait_ge(lam_done, 1)
                    act.wait_ge(lru_r, 1)
                    for b in range(LB):
                        last = act.activation(lru_b[:, b, :], gate_r[:, b, :], ACT.Tanh, scale=lam[:, 8, b:b + 1])
                    last.then_inc(lru_t, 1)
                elif step == "D":
                    for b in range(LB):
                        last = act.activation(lru_a[:, b, :], gate_r[:, b, :], ACT.Exp, scale=lam[:, 9, b:b + 1])
                    chained(last)
                    act.activation(gate_r, lru_a, ACT.Square).then_inc(lru_a2, 1)
                elif step == "Q":
                    act.wait_ge(lru_s2, 1)
                    act.activation(lru_b, lru_b, ACT.Sqrt).then_inc(lru_sqrt, 1)
                elif step == "Y":
                    act.wait_ge(lru_yb, 1)
                    act.activation(hT_hi[:, :, :], lru_h, ACT.Copy).then_inc(y_hi, 1)
                elif step == "Z":
                    act.wait_ge(lru_ya, 1)
                    act.activation(aT_hi[:, 0:LB, :], conv_a, ACT.Copy).then_inc(y_hi, 1)
            norm(U_SG0, 1, (0, 0, 2, 4))

            def swiglu(layer):
                u, j0 = SG_U[layer], H0[layer]
                hj = 2 * NJ_MLP + NJ_SG * layer

                def one(v, j, i=None, first=False):
                    if not first:
                        split_hi(v + 1, i, 6)
                    split_hi(v + 2, i, 6)
                    act.wait_ge(w_used, plus(v + 2, i, 6))
                    act.wait_ge(h_ready, plus(j0 + j, i, 2))
                    act.activation(gbuf[:, :, 0:256], ub[:, :, 0:256], ACT.Silu).then_inc(act_h, 1)
                    if not first:
                        split_hi(v + 3, i, 6)
                    act.wait_ge(hT_ready, plus(hj + j + 1, i, 2))
                    act.activation(hT_hi[:, 0:2, :], tp[:, 0, :].rearrange("p (b n) -> p b n", n=TOK),
                                   ACT.Copy).then_inc(hT_hi_done, 1)

                one(u, 0, first=True)
                with act.Fori(0, 4) as i:
                    for q in range(2):
                        one(u + 2 + 3 * q, 1 + q, i)
                for q in range(2):
                    one(u + 2 + 3 * (8 + q), 9 + q)
                split_hi(u + 3 * NJ_SG)

            swiglu(0)
            norm(U_QKV2, 1, (4, 4, 7, 10))
            act.preload_act_table_set("natural_log_exp_and_others")
            for step, n in STICK_STEPS:
                if step == "H":
                    split_hi(U_QKV2 + n)
                elif step == "E" and n < 4:
                    act.wait_ge(w_used, U_QKV2 + 2 * n + 2)
                    if n >= 1:
                        act.wait_ge(qk_ss_done, n)
                    act.activation(qk_sq, acc[:, 2 * (n % 2):2 * (n % 2) + 2, :].rearrange("p t (h d) -> p (t h) d", d=SB_DH),
                                   ACT.Square).then_inc(qk_sq_done, 1)
                elif step == "E":
                    copy_v(U_QKV2 + 2 * n, n - 4)
                elif step == "T":
                    copy_T(qkT, C0["qkv2"] + n, 4 * QKV_CHUNKS[n])
                elif step == "S":
                    act.wait_ge(z_masked, n + 1)
                    buf = stick_sp[:, n % 2, :]
                    if n >= 2:
                        act.wait_ge(z_cum, n - 1)
                    chained(act.activation(buf, stick_z[:, n % 4, :], ACT.Abs))
                    chained(act.activation(buf, buf, ACT.Exp, scale=-1.0))
                    act.activation(buf, buf, ACT.Ln, bias=1.0).then_inc(z_log, 1)
                elif step == "A":
                    act.wait_ge(z_arg, n + 1)
                    act.activation(stick_z[:, n % 4, :], stick_z[:, n % 4, :], ACT.Exp).then_inc(z_w, 1)
                elif step == "V":
                    act.wait_ge(so_ready, n // 2 * 2 + 2)
                    b, q = n // 2, slice(SB_DH * (n % 2), SB_DH * (n % 2 + 1))
                    act.activation(aT_hi[q, b, :], o_bank[b][q, TOK * (n % 2):TOK * (n % 2 + 1)], ACT.Copy).then_inc(so_hi, 1)
            norm(U_SG1, 1, (10, 10, 12, 12))
            swiglu(1)

        @block.vector
        def _(dve):
            n_chain = [0]

            def chained(ins):
                n_chain[0] += 1
                ins.then_inc(dve_chain, 1)
                dve.wait_ge(dve_chain, n_chain[0])

            def split_lo(u, i=None, per=0):
                if u >= U_END:
                    return
                dve.wait_ge(hi_done, plus(u + 1, i, per))
                s = u % 2
                dve.tensor_tensor(w_lo[:, s, 0:LO_V], w_raw[:, s, 0:LO_V], w_hi[:, s, 0:LO_V].bitcast(F32),
                                  ALU.subtract).then_inc(lo_v_done, 1)

            def splits(u0, u1):
                for u in range(u0, u1):
                    split_lo(u)

            def bank_lo(dst, hi, bank):
                return dve.tensor_tensor(dst, bank, hi.bitcast(F32), ALU.subtract)

            n_norm, n_rstd = [0], [0]

            def norm_scale(t, g):
                chained(dve.tensor_tensor(xn[:, t, :], x[:, t, :], g, ALU.mult))

            def norm_rows(t, g, shift):
                n_rstd[0] += 1
                dve.wait_ge(rstd_done, n_rstd[0])
                src, op, by = (x[:, t, :], ALU.mult, g) if shift is None else (xn[:, t, :], ALU.add, shift)
                dve.scalar_tensor_tensor(xn[:, t, :], src, rstd[:, t:t + 1], by, ALU.mult, op).then_inc(xn_done, 1)

            def norm_lo(t, q):
                k = n_norm[0]
                n_norm[0] += t * q
                dve.wait_ge(n_hi, 4 * k + 2 * t + q + 1)
                part = (slice(None), slice(4 * q, 4 * q + 4), slice(t * P, (t + 1) * P))
                bank_lo(aT_lo[part], aT_hi[part], norm_banks(k, t)[q].rearrange("p (b n) -> p b n", n=P)).then_inc(n_lo, 1)

            def norm_rest(g, shift):
                norm_lo(0, 0)
                norm_rows(1, g, shift)
                norm_lo(0, 1)
                norm_lo(1, 0)
                norm_lo(1, 1)

            def post_norm_scale(t, g):
                n_rstd[0] += 1
                dve.wait_ge(sq_done, n_rstd[0])
                chained(dve.tensor_tensor(xn[:, t, :], acc_tile(t), g, ALU.mult))

            def post_norm_add(t, n):
                dve.wait_ge(rstd_done, n)
                dve.scalar_tensor_tensor(x[:, t, :], xn[:, t, :], rstd[:, t:t + 1], x[:, t, :], ALU.mult,
                                         ALU.add).then_inc(x_ready, 1)

            def post_norm(n, g_post, g, shift):
                post_norm_scale(0, g_post)
                post_norm_add(0, n_rstd[0])
                post_norm_scale(1, g_post)
                n_post = n_rstd[0]
                if shift is None:
                    post_norm_add(1, n_post)
                    norm_rows(0, g, shift)
                else:
                    post_norm_add(1, n_post)
                    dve.wait_ge(x_ready, 2 * n + 1)
                    norm_scale(0, g)
                    norm_rows(0, g, shift)
                    dve.wait_ge(x_ready, 2 * n + 2)
                    norm_scale(1, g)
                norm_rest(g, shift)

            def gated(t, g, n=None):
                part = slice(0, D) if n is None else slice(n * CH, (n + 1) * CH)
                chained(dve.tensor_tensor(xn[:, t, part], acc_tile(t)[:, part], g[:, part], ALU.mult))
                return dve.tensor_tensor(x[:, t, part], x[:, t, part], xn[:, t, part], ALU.add)

            def gated_norm(n, u_end, g_mod, halves, g=None, shift=None):
                if halves:
                    dve.wait_ge(w_used, u_end - 1)
                    for t in range(NT):
                        gated(t, g_mod, 0)
                    split_lo(u_end)
                half_n = 1 if halves else None
                dve.wait_ge(tile0_done, n + 1)
                gated(0, g_mod, half_n).then_inc(x_ready, 1)
                if g is not None:
                    dve.wait_ge(x_ready, 2 * n + 1)
                    norm_scale(0, g)
                dve.wait_ge(w_used, u_end)
                gated(1, g_mod, half_n).then_inc(x_ready, 1)
                if g is not None:
                    norm_rows(0, g, shift)
                    dve.wait_ge(x_ready, 2 * n + 2)
                    norm_scale(1, g)
                    norm_rest(g, shift)

            def ada(slot, loads, third, col, before, i=None, per=0, step=0):
                dve.wait_ge(ada_loaded[slot], plus(16 * loads, i, 16 * step))
                if before:
                    dve.wait_ge(ada_used, plus(before, i, per))
                part = mod[:, third * UNIT:(third + 1) * UNIT]
                dve.scalar_tensor_tensor(part, ada_raw[:, slot, :], silu_c[:, bass.ds(col, 1)], part,
                                         ALU.mult, ALU.add).then_inc(ada_used, 1)

            def ada_gain(layer, c, out):
                dve.wait_ge(ada_out, out)
                g = 4 + 2 * layer + (c == 4)
                dve.wait_ge(gain_loaded[g], 16)
                part = mod[:, c * D:(c + 1) * D]
                dve.scalar_tensor_tensor(part, part, 1.0, gain[:, g % 4, :], ALU.add, ALU.mult).then_inc(ada_gain_done, 1)

            SH_M, G_M, GATE_M, SH_F, G_F = (mod[:, c * D:(c + 1) * D] for c in range(5))

            def copy_chunk(u, bank, ct):
                dve.wait_ge(w_used, u + 2)
                if ct >= 2:
                    dve.wait_ge(cT1, ct - 1)
                dve.tensor_copy(tokbuf[:, ct % 2, 1, :], bank).then_inc(chunk_v, 1)

            def copy_T(dst, ct, b):
                dve.wait_ge(cT1, ct + 1)
                dve.tensor_copy(dst[:, b + 2:b + 4, :], tp[:, 1, :].rearrange("p (b n) -> p b n", n=TOK)).then_inc(cT_v, 1)

            def copy_v(u, n):
                dve.wait_ge(w_used, u + 2)
                dve.tensor_copy(vtok[:, 1, n * CH:(n + 1) * CH], acc[:, 2 * n + 1, :]).then_inc(v_v, 1)

            dve.wait_ge(gain_loaded[0], 16)
            for t in range(NT):
                dve.wait_ge(x_loaded[t], 16)
                norm_rows(t, gain[:, 0, :], None)
                if t == 0:
                    split_lo(U_QKV1)
                norm_lo(t, 0)
                norm_lo(t, 1)
            def lambda_columns():
                dve.wait_ge(lam_exp, 1)
                e, s, s2, q, m = (lam[:, n, :] for n in (1, 3, 4, 5, 6))
                chained(dve.tensor_scalar(lam[:, 2, :], e, 2.0, None, ALU.add))
                chained(dve.reciprocal(lam[:, 2, :], lam[:, 2, :]))
                chained(dve.tensor_tensor(s, e, lam[:, 2, :], ALU.mult))
                chained(dve.tensor_tensor(s2, s, s, ALU.mult))
                chained(dve.tensor_scalar(q, s2, 1.0 / 19.0, None, ALU.mult))
                for n in range(8, 0, -1):
                    chained(dve.scalar_tensor_tensor(q, q, 1.0 / (2 * n + 1), s2, ALU.add, ALU.mult))
                chained(dve.scalar_tensor_tensor(q, q, 1.0, s, ALU.add, ALU.mult))
                chained(dve.tensor_scalar(m, cols[:, :, R_LAMBDA], -1.0, 0.0, ALU.mult, ALU.max))
                chained(dve.scalar_tensor_tensor(q, q, 2.0, m, ALU.mult, ALU.add))
                chained(dve.tensor_scalar(lam[:, 8, :], q, RG_C, None, ALU.mult))
                dve.tensor_scalar(lam[:, 9, :], q, -RG_C, None, ALU.mult).then_inc(lam_done, 1)

            def att_max_of(h):
                r = h % 4
                dve.wait_ge(s_ready, h + 1)
                if h >= 4:
                    dve.wait_ge(pT_ready, h - 3)
                slope = 2.0 ** (-8.0 * (h + 1) / HEADS)
                chained(dve.scalar_tensor_tensor(prob[:, r, :], neg_dist[:, :], slope * DH ** 0.5, ub[:, h % 2, 0:SC],
                                                 ALU.mult, ALU.add))
                dve.reduce_max(att_max[:, r, 0:1], prob[:, r, 0:P], AX.X)
                chained(dve.reduce_max(att_max[:, r, 1:2], prob[:, r, P:SC], AX.X))
                dve.tensor_scalar(att_nmax[:, r, :], att_max[:, r, :], -DH ** -0.5, None, ALU.mult).then_inc(s_max, 1)

            def att_norm(h):
                r = h % 4
                dve.wait_ge(s_exp, 2 * h + 2)
                chained(dve.reciprocal(att_rsum[:, r, :], att_sum[:, r, :]))
                for t, lo, n in ((0, 0, P), (1, P, TOK)):
                    dve.tensor_scalar(prob[:, r, lo:lo + n], prob[:, r, lo:lo + n], att_rsum[:, r, t:t + 1], None,
                                      ALU.mult).then_inc(s_norm, 1)

            dve.wait_ge(consts, 7)
            for step, n in ATT_STEPS:
                if step == "L":
                    split_lo(U_QKV1 + n)
                elif step == "Y":
                    lambda_columns()
                elif step == "E" and n < 4:
                    copy_chunk(U_QKV1 + 2 * n, acc[:, 2 * (n % 2) + 1, :], C0["qkv1"] + n)
                elif step == "E":
                    copy_v(U_QKV1 + 2 * n, n - 4)
                elif step == "T":
                    copy_T(qkT, C0["qkv1"] + n, 4 * QKV_CHUNKS[n])
                elif step == "S":
                    att_max_of(n)
                elif step == "A":
                    att_norm(n)
                elif step == "V":
                    dve.wait_ge(o_hi, n + 1)
                    bank_lo(aT_lo[:, n, :], aT_hi[:, n, :], o_bank[n][:, 0:TOK]).then_inc(o_lo, 1)
            dve.wait_ge(gain_loaded[1], 16)
            dve.wait_ge(gain_loaded[2], 16)
            post_norm(0, gain[:, 1, :], gain[:, 2, :], None)

            def mlp_slice(u, j, i=None, first=False):
                col = j if i is None else i + 1
                adas = [(t, j + 1, t, col, max(3 * j + t - 2, 0), i, 3, 1) for t in range(3)]
                split_lo(u + 1, i, 4)
                ada(*adas[0])
                split_lo(u + 2, i, 4)
                ada(*adas[1])
                if not first:
                    split_lo(u + 3, i, 4)
                dve.wait_ge(act_h, plus(j + 1, i, 1))
                if j >= 1:
                    dve.wait_ge(hT_ready, plus(2 * j, i, 2))
                dve.tensor_tensor(hbuf, gbuf, gbuf, ALU.mult).then_inc(h_ready, 1)
                if not first:
                    split_lo(u + 4, i, 4)
                ada(*adas[2])
                for g in range(2):
                    dve.wait_ge(hT_hi_done, plus(2 * j + g + 1, i, 2))
                    sl = slice(2 * g, 2 * g + 2)
                    bank_lo(hT_lo[:, sl, :], hT_hi[:, sl, :],
                            tp[:, g, :].rearrange("p (b n) -> p b n", n=TOK)).then_inc(hT_lo_done, 1)

            dve.wait_ge(cols_done, 2)
            dve.wait_ge(ada_bias, 16)
            mlp_slice(U_MLP, 0, first=True)
            with dve.Fori(0, NJ_MLP - 1) as i:
                mlp_slice(U_MLP + 2, 1, i)
            splits(U_WIN - 1, U_WIN + 1)
            dve.wait_ge(gain_loaded[3], 16)
            ada_gain(0, 1, 4)
            dve.wait_ge(ada_gain_done, 1)
            post_norm(1, gain[:, 3, :], G_M, SH_M)
            ada_gain(0, 4, 12)

            def conv(dst, src, row, width, bias):
                for b in range(LB):
                    w = cols[:, b, row + width - 1:row + width]
                    if bias is None:
                        ins = dve.tensor_scalar(dst[:, b, :], src[:, b, :], w, None, ALU.mult)
                    else:
                        ins = dve.tensor_scalar(dst[:, b, :], src[:, b, :], w, cols[:, b, bias:bias + 1],
                                                ALU.mult, ALU.add)
                for s in range(1, width):
                    chained(ins)
                    for b in range(LB):
                        w = cols[:, b, row + width - 1 - s:row + width - s]
                        ins = dve.scalar_tensor_tensor(dst[:, b, s:], src[:, b, :TOK - s], w, dst[:, b, s:],
                                                       ALU.mult, ALU.add)
                return ins

            for step, n in LRU_STEPS:
                if step == "L":
                    split_lo(U_WIN + n)
                elif step == "E" and n != 3:
                    copy_chunk(U_WIN + 2 * n, ub[:, 1, :] if n == 4 else acc[:, 2 * (n % 2) + 1, :], C0["win"] + n)
                elif step == "T":
                    copy_T(uT, C0["win"] + n, 4 * WIN_CHUNKS[n])
                elif step == "M":
                    if n == 0:
                        dve.wait_ge(ada_bias, 32)
                    ada(n % 2, 8 + n // 2 + 1, 0, n, 24 + n)
                elif step == "C":
                    dve.wait_ge(cT_a, C0["win"] + 1)
                    dve.wait_ge(cT_v, C0["win"] + 1)
                    conv(xr, uT[:, 16:20, :], R_CONV_B, 4, R_CONV_BIAS).then_inc(lru_xr, 1)
                elif step == "K":
                    dve.wait_ge(lru_p, 1)
                    conv(conv_a, uT[:, 4:8, :], R_CONV_A, 3, None).then_inc(lru_conv, 1)
                elif step == "D" and n == 1:
                    dve.wait_ge(lru_a2, 1)
                    dve.wait_ge(lru_t, 1)
                    dve.scalar_tensor_tensor(lru_b, gate_r, 1.0, lru_b, ALU.add, ALU.mult).then_inc(lru_s2, 1)
                elif step == "Q":
                    dve.wait_ge(lru_sqrt, 1)
                    dve.wait_ge(lru_ix, 1)
                    chained(dve.tensor_tensor(lru_b, lru_b, gate_i, ALU.mult))
                    for b in range(LB):
                        ins = dve.tensor_tensor_scan(lru_h[:, b, :], lru_a[:, b, :], lru_b[:, b, :], 0.0, ALU.mult, ALU.add)
                    chained(ins)
                elif step == "Y":
                    dve.wait_ge(cT_a, C0["win"] + 4)
                    dve.wait_ge(cT_v, C0["win"] + 4)
                    dve.tensor_tensor(lru_h, lru_h, uT[:, 12:16, :], ALU.mult).then_inc(lru_yb, 1)
                    dve.wait_ge(y_hi, 1)
                    dve.tensor_tensor(hT_lo[:, :, :], lru_h, hT_hi[:, :, :].bitcast(F32),
                                      ALU.subtract).then_inc(y_lo, 1)
                elif step == "Z":
                    dve.wait_ge(cT_a, C0["win"] + 5)
                    dve.wait_ge(cT_v, C0["win"] + 5)
                    dve.wait_ge(lru_conv, 1)
                    dve.tensor_tensor(conv_a, conv_a, uT[:, 0:4, :], ALU.mult).then_inc(lru_ya, 1)
                    dve.wait_ge(y_hi, 2)
                    dve.tensor_tensor(aT_lo[:, 0:LB, :], conv_a, aT_hi[:, 0:LB, :].bitcast(F32),
                                      ALU.subtract).then_inc(y_lo, 1)
            dve.wait_ge(ada_gain_done, 2)
            gated_norm(2, U_SG0, GATE_M, True, G_F, SH_F)

            def swiglu(layer):
                u, j0 = SG_U[layer], H0[layer]
                hj = 2 * NJ_MLP + NJ_SG * layer
                hh = 2 * NJ_MLP + NJ_SG * layer

                def one(v, j, i=None, first=False, kb=None):
                    adas = [] if kb is None else [(t, 13 + kb, 1 + t, plus(kb, i, 2),
                                                   32 + 2 * kb + t, i, 4, 2) for t in range(2)]
                    split_lo(v + 1, i, 6)
                    if adas:
                        ada(*adas[0])
                    split_lo(v + 2, i, 6)
                    if adas:
                        ada(*adas[1])
                    dve.wait_ge(act_h, plus(j0 + j + 1, i, 2))
                    dve.wait_ge(hT_ready, plus(hj + j, i, 2))
                    dve.tensor_tensor(hbuf[:, :, 0:256], gbuf[:, :, 0:256], ub[:, :, 256:512],
                                      ALU.mult).then_inc(h_ready, 1)
                    if not first:
                        split_lo(v + 3, i, 6)
                    dve.wait_ge(hT_hi_done, plus(hh + j + 1, i, 2))
                    bank_lo(hT_lo[:, 0:2, :], hT_hi[:, 0:2, :],
                            tp[:, 0, :].rearrange("p (b n) -> p b n", n=TOK)).then_inc(hT_lo_done, 1)

                one(u, 0, first=True)
                if layer == 0:
                    ada_gain(1, 1, 16)
                    dve.wait_ge(ada_bias, 48)
                with dve.Fori(0, 4) as i:
                    for q in range(2):
                        one(u + 2 + 3 * q, 1 + q, i, kb=q if layer == 0 else None)
                for q in range(2):
                    one(u + 2 + 3 * (8 + q), 9 + q)
                split_lo(u + 3 * NJ_SG)

            swiglu(0)
            dve.wait_ge(ada_gain_done, 3)
            gated_norm(3, U_QKV2, gate_ffn, False, G_M, SH_M)
            ada_gain(1, 4, 22)


            def qk_norm(c):
                src = acc[:, 2 * (c % 2):2 * (c % 2) + 2, :].rearrange("p t (h d) -> p (t h) d", d=SB_DH)
                dst = tokbuf[:, (C0["qkv2"] + c) % 2, :, :].rearrange("p t (h d) -> p (t h) d", d=SB_DH)
                dve.wait_ge(qk_rstd_done, c + 1)
                if c >= 2:
                    dve.wait_ge(cT1, C0["qkv2"] + c - 1)
                chained(dve.tensor_tensor(dst, src, qk_rstd[:, :].unsqueeze(2).broadcast_to([P, 16, SB_DH]), ALU.mult))
                dve.tensor_tensor(dst, dst, qk_gain[:, c % 2:c % 2 + 1, :].broadcast_to([P, 16, SB_DH]),
                                  ALU.mult).then_inc(chunk_v, 1)

            def stick_mask(h):
                dve.wait_ge(z_ready, h + 1)
                if h >= 4:
                    dve.wait_ge(wT_ready, h - 3)
                dve.scalar_tensor_tensor(stick_z[:, h % 4, :], ub[:, h % 2, 0:SC], SB_DH ** -0.5, sb_mask[:, :],
                                         ALU.mult, ALU.add).then_inc(z_masked, 1)

            def stick_sum_of(h):
                z, f, c = stick_z[:, h % 4, :], stick_sp[:, h % 2, :], stick_sum[:, h % 2, :]
                dve.wait_ge(z_log, h + 1)
                chained(dve.scalar_tensor_tensor(f, z, 0.0, f, ALU.max, ALU.add))
                if h >= 2:
                    dve.wait_ge(z_arg, h - 1)
                for lo, n in ((0, P), (P, TOK)):
                    fr = f[:, lo:lo + n][:, ::-1]
                    ins = dve.tensor_tensor_scan(c[:, lo:lo + n][:, ::-1], fr, fr, 0.0, ALU.add, ALU.max)
                ins.then_inc(z_cum, 1)

            for step, n in STICK_STEPS:
                if step == "L":
                    split_lo(U_QKV2 + n)
                elif step == "E" and n < 4:
                    dve.wait_ge(qk_sq_done, n + 1)
                    dve.reduce_sum(qk_ss[:, :], qk_sq, AX.X).then_inc(qk_ss_done, 1)
                elif step == "E":
                    copy_v(U_QKV2 + 2 * n, n - 4)
                elif step == "N":
                    qk_norm(n)
                elif step == "T":
                    copy_T(qkT, C0["qkv2"] + n, 4 * QKV_CHUNKS[n])
                elif step == "S":
                    stick_mask(n)
                elif step == "A":
                    stick_sum_of(n)
                elif step == "W":
                    dve.wait_ge(wT_ready, n + 1)
                    dve.tensor_copy(stick_wT[:, n, :], tp[:, n % 2, 0:SC]).then_inc(wT_copied, 1)
                elif step == "V":
                    dve.wait_ge(so_hi, n + 1)
                    b, q = n // 2, slice(SB_DH * (n % 2), SB_DH * (n % 2 + 1))
                    bank_lo(aT_lo[q, b, :], aT_hi[q, b, :], o_bank[b][q, TOK * (n % 2):TOK * (n % 2 + 1)]).then_inc(so_lo, 1)
            dve.wait_ge(ada_gain_done, 4)
            gated_norm(4, U_SG1, GATE_M, True, G_F, SH_F)
            swiglu(1)
            dve.wait_ge(ada_out, 24)
            gated_norm(5, U_END, gate_ffn, False)

        @block.tensor
        def _(pe):
            def matmuls(outp, lhs, rhs, start, stop):
                n = len(lhs)
                for k in range(n):
                    (ah, al), (bh, bl) = lhs[k], rhs[k]
                    pe.matmul(outp, ah, bh, start=start and k == 0, stop=False)
                    pe.matmul(outp, ah, bl, start=False, stop=False)
                    last = pe.matmul(outp, al, bh, start=False, stop=stop and k == n - 1)
                return last

            def unit_ready(u, i=None, per=0):
                pe.wait_ge(lo_v_done, plus(u + 1, i, per))
                pe.wait_ge(lo_p_done, plus(u + 1, i, per))

            def project(u, h, bank, i=None, per=0, first=0, operand=None, tile0=False):
                op_hi, op_lo = operand or (aT_hi[:, 4 * h:4 * h + 4, :], aT_lo[:, 4 * h:4 * h + 4, :])
                unit_ready(u, i, per)
                s = u % 2
                rhs = [(w_hi[:, s, k * CH:(k + 1) * CH], w_lo[:, s, k * CH:(k + 1) * CH]) for k in range(4)]
                for t in range(NT):
                    q = slice(t * P, (t + 1) * P)
                    lhs = [(op_hi[:, k, q], op_lo[:, k, q]) for k in range(4)]
                    last = matmuls(bank(t), lhs, rhs, h == first, h != first)
                    if tile0 and t == 0:
                        last.then_inc(tile0_done, 1)
                last.then_inc(w_used, 1)

            def down(u, h, i=None, per=0, final=0):
                unit_ready(u, i, per)
                s = u % 2
                for t in range(NT):
                    q = slice(t * P, (t + 1) * P)
                    for n in range(2):
                        for part in (0, 1):
                            if final and t == 0 and n == 0 and part == 1:
                                pe.wait_ge(hT_lo_done, final)
                            for k in range(2):
                                c = slice(k * D + n * CH, k * D + (n + 1) * CH)
                                if part == 0:
                                    pe.matmul(acc[:, 2 * t + n, :], hT_hi[:, 2 * h + k, q], w_hi[:, s, c], start=False, stop=False)
                                    pe.matmul(acc[:, 2 * t + n, :], hT_hi[:, 2 * h + k, q], w_lo[:, s, c], start=False, stop=False)
                                else:
                                    last = pe.matmul(acc[:, 2 * t + n, :], hT_lo[:, 2 * h + k, q], w_hi[:, s, c], start=False,
                                                     stop=bool(final) and k == 1)
                    if final and t == 0:
                        last.then_inc(tile0_done, 1)
                last.then_inc(w_used, 1)

            n_norm = [0]

            def norm_T(k, t):
                pe.wait_ge(xn_done, 2 * k + t + 1)
                for g, bank in enumerate(norm_banks(k, t)):
                    for b in range(4):
                        last = pe.transpose(bank[:, b * P:(b + 1) * P], xn[:, t, (4 * g + b) * P:(4 * g + b + 1) * P],
                                            ident[:, :])
                    last.then_inc(nT_done, 1)

            def first_unit(u, bank):
                k = n_norm[0]
                n_norm[0] += 1
                norm_T(k, 0)
                unit_ready(u)
                s = u % 2
                for t in range(NT):
                    q = slice(t * P, (t + 1) * P)
                    pe.wait_ge(n_hi, 4 * k + 2 * t + 1)
                    for b in range(4):
                        pe.matmul(bank(t), aT_hi[:, b, q], w_hi[:, s, b * CH:(b + 1) * CH], start=b == 0, stop=False)
                        pe.matmul(bank(t), aT_hi[:, b, q], w_lo[:, s, b * CH:(b + 1) * CH], start=False, stop=False)
                    if t == 0:
                        norm_T(k, 1)
                    pe.wait_ge(n_lo, 4 * k + 1 if t == 0 else 4 * k + 3)
                    for b in range(4):
                        last = pe.matmul(bank(t), aT_lo[:, b, q], w_hi[:, s, b * CH:(b + 1) * CH], start=False, stop=False)
                last.then_inc(w_used, 1)
                pe.wait_ge(n_lo, 4 * k + 4)

            def keep_warm(n):
                for _ in range(n):
                    pe.matmul(ub[:, 0, :], zeros[:, 0:P], zeros[:, :], start=True, stop=True)

            def out_unit(u, order, n, operand=None):
                c, h = order[n]
                project(u + n, h, lambda t: acc[:, 2 * t + c, :], first=order[0][1], operand=operand, tile0=n == 3)

            def chunk_T(ct):
                if ct:
                    pe.wait_ge(cT_a, ct)
                    pe.wait_ge(cT_v, ct)
                par = ct % 2
                for g, done in enumerate((cT0, cT1)):
                    for b in range(2):
                        for t in range(NT):
                            last = pe.transpose(tp[:, g, b * TOK + t * P:b * TOK + (t + 1) * P],
                                                tokbuf[:, par, t, (2 * g + b) * P:(2 * g + b + 1) * P], ident[:, :])
                    last.then_inc(done, 1)

            pe.wait_ge(consts, 1)
            first_unit(U_QKV1, lambda t: acc[:, t, :])
            def scores(h, q, k):
                pe.matmul(ub[:, h % 2, 0:P], q[:, 0:P], k[:, 0:P], start=True, stop=True)
                return pe.matmul(ub[:, h % 2, P:SC], q[:, P:TOK], k[:, :], start=True, stop=True)

            def weights_T(h, w):
                for n in range(3):
                    last = pe.transpose(tp[:, h % 2, n * P:(n + 1) * P], w[:, n * P:(n + 1) * P], ident[:, :])
                return last

            def weighted(o, wT, v0, v1):
                pe.matmul(o[:, 0:P], v0, wT[:, 0:P], start=True, stop=True)
                pe.matmul(o[:, P:TOK], v0, wT[:, P:2 * P], start=True, stop=False)
                return pe.matmul(o[:, P:TOK], v1, wT[:, 2 * P:SC], start=False, stop=True)

            weights = chunks = 0
            for step, n in ATT_STEPS:
                if step == "U" and 0 < n < 12:
                    c = n // 2
                    if c >= 2 and n % 2 == 0:
                        pe.wait_ge(chunk_a, c - 1)
                        pe.wait_ge(chunk_v, c - 1)
                    project(U_QKV1 + n, n % 2, lambda t: acc[:, 2 * (c % 2) + t, :])
                elif step == "U" and n >= 12:
                    pe.wait_ge(o_lo, 8 if n >= 14 else 4)
                    out_unit(U_WO1, OUT_LO_FIRST, n - 12)
                elif step == "X":
                    pe.wait_ge(small_loaded, 16 * 13)
                    for b in range(LB):
                        pe.transpose(ub[:, 0, 16 * b:16 * b + N_ROWS], rows[:, b * P:(b + 1) * P], ident[0:N_ROWS, 0:N_ROWS])
                    pe.transpose(ub[:, 0, 64:64 + KB], c_rows[:, :], ident[0:KB, 0:KB]).then_inc(cols_T, 1)
                elif step == "T":
                    pe.wait_ge(chunk_a, n + 1)
                    pe.wait_ge(chunk_v, n + 1)
                    if weights:
                        pe.wait_ge(pT_copied, weights)
                    chunk_T(C0["qkv1"] + n)
                    chunks = n + 1
                elif step == "S":
                    if n == 0:
                        pe.wait_ge(cols_done, 2)
                    pe.wait_ge(cT_a, C0["qkv1"] + (4 if n >= HEADS // 2 else 2))
                    pe.wait_ge(cT_v, C0["qkv1"] + (4 if n >= HEADS // 2 else 2))
                    if n >= 2:
                        pe.wait_ge(s_max, n - 1)
                    scores(n, qkT[:, n, :], qkT[:, HEADS + n, :]).then_inc(s_ready, 1)
                elif step == "W":
                    pe.wait_ge(s_norm, 2 * n + 2)
                    pe.wait_ge(cT_a, C0["qkv1"] + chunks)
                    pe.wait_ge(cT_v, C0["qkv1"] + chunks)
                    if n >= 2:
                        pe.wait_ge(pT_copied, n - 1)
                    weights_T(n, prob[:, n % 4, :]).then_inc(pT_ready, 1)
                    weights = n + 1
                elif step == "V":
                    pe.wait_ge(v_a, 2)
                    pe.wait_ge(v_v, 2)
                    pe.wait_ge(pT_copied, HEADS if n >= 4 else n + 1)
                    if n >= 4:
                        pe.wait_ge(s_max, HEADS)
                    f = slice(n * DH, (n + 1) * DH)
                    weighted(o_bank[n][:, 0:TOK], probT[:, n, :], vtok[:, 0, f], vtok[:, 1, f]).then_inc(o_ready, 1)

            def clear_acc():
                for n in range(4):
                    pe.matmul(acc[:, n, :], zeros[:, 0:P], zeros[:, :], start=True, stop=False)

            def hidden(u, i=None, per=0, first=False):
                for h in range(2):
                    if first and h == 0:
                        first_unit(u, lambda t: ub[:, t, :])
                    else:
                        project(u + h, h, lambda t: ub[:, t, :], i, per)

            def hidden_T(nb, ready, base, i=None, step=0):
                pe.wait_ge(h_ready, plus(ready, i, step[0] if step else 0))
                for g in range(nb):
                    for b in range(2):
                        for t in range(NT):
                            last = pe.transpose(tp[:, g, b * TOK + t * P:b * TOK + (t + 1) * P],
                                                hbuf[:, t, (2 * g + b) * P:(2 * g + b + 1) * P], ident[:, :])
                    last.then_inc(hT_ready, 1)

            pe.wait_ge(consts, 3)
            keep_warm(16)
            hidden(U_MLP, first=True)
            clear_acc()
            hidden_T(2, 1, 0)
            with pe.Fori(0, NJ_MLP - 1) as i:
                u = U_MLP + 2
                hidden(u, i, 4)
                pe.wait_ge(hT_lo_done, plus(2, i, 2))
                down(u + 2, 0, i, 4)
                down(u + 3, 1, i, 4)
                hidden_T(2, 2, 0, i, (1,))
            pe.wait_ge(hT_lo_done, 2 * NJ_MLP)
            def ada_sums(layer, n0, n1):
                for n in range(n0, n1):
                    c, m = ADA_ORDER[layer][n], 12 * layer + n
                    if m >= 2:
                        pe.wait_ge(ada_out, m - 1)
                    pe.matmul(ub[:, n % 2, :], ones[:, :], mod[:, c * CH:(c + 1) * CH], start=True,
                              stop=True).then_inc(ada_sum, 1)

            pe.wait_ge(ada_used, 24)
            ada_sums(0, 0, 6)
            down(U_WIN - 2, 0)
            down(U_WIN - 1, 1, final=2 * NJ_MLP)
            ada_sums(0, 6, 12)
            pe.wait_ge(ada_out, 12)
            first_unit(U_WIN, lambda t: acc[:, t, :])
            for step, n in LRU_STEPS:
                if step == "U" and 0 < n < 10:
                    c = n // 2
                    if c == 2 or c == 3:
                        pe.wait_ge(chunk_a, C0["win"] + c - 1)
                        pe.wait_ge(chunk_v, C0["win"] + c - 1)
                    if c == 4:
                        pe.wait_ge(lru_i, 1)
                    project(U_WIN + n, n % 2, lambda t: ub[:, t, :] if c == 4 else acc[:, 2 * (c % 2) + t, :])
                elif step == "U" and n >= 10:
                    if n == 10:
                        pe.wait_ge(chunk_a, C0["win"] + 4)
                        pe.wait_ge(chunk_v, C0["win"] + 4)
                    pe.wait_ge(y_lo, 1 if n < 12 else 2)
                    out_unit(U_WOUT0, OUT_HI_FIRST, n - 10, (hT_hi, hT_lo) if n < 12 else None)
                elif step == "T":
                    pe.wait_ge(chunk_a, C0["win"] + n + 1)
                    pe.wait_ge(chunk_v, C0["win"] + n + 1)
                    chunk_T(C0["win"] + n)
                elif step == "G":
                    pe.wait_ge(lru_xr, 1)
                    if n == 1:
                        pe.wait_ge(lru_r, 1)
                    for b in range(LB):
                        last = pe.matmul(ub[:, b // 2, (b % 2) * TOK:(b % 2 + 1) * TOK], rg_w[:, n, b, :],
                                         xr[:, b, :], start=True, stop=True)
                    last.then_inc(lru_gate, 1)
            pe.wait_ge(ada_used, 32)
            ada_sums(1, 0, 4)
            pe.wait_ge(ada_out, 16)

            def swiglu(layer):
                u, j0 = SG_U[layer], H0[layer]
                hl = 2 * NJ_MLP + NJ_SG * layer
                hidden(u, first=True)
                clear_acc()
                hidden_T(1, j0 + 1, 0)

                def one(v, j, i=None):
                    hidden(v, i, 6)
                    pe.wait_ge(hT_lo_done, plus(hl + j, i, 2))
                    down(v + 2, 0, i, 6)
                    hidden_T(1, j0 + j + 1, 0, i, (2,))

                with pe.Fori(0, 4) as i:
                    for q in range(2):
                        one(u + 2 + 3 * q, 1 + q, i)
                for q in range(2):
                    one(u + 2 + 3 * (8 + q), 9 + q)
                pe.wait_ge(hT_hi_done, hl + NJ_SG)
                down(u + 3 * NJ_SG - 1, 0, final=hl + NJ_SG)

            swiglu(0)
            pe.wait_ge(ada_used, 48)
            ada_sums(1, 4, 10)
            pe.wait_ge(ada_out, 22)
            first_unit(U_QKV2, lambda t: acc[:, t, :])
            weights = chunks = 0
            for step, n in STICK_STEPS:
                if step == "U" and 0 < n < 12:
                    c = n // 2
                    if c >= 2 and n % 2 == 0:
                        pe.wait_ge(chunk_v, C0["qkv2"] + c - 1)
                    project(U_QKV2 + n, n % 2, lambda t: acc[:, 2 * (c % 2) + t, :])
                elif step == "U" and n >= 12:
                    pe.wait_ge(so_lo, 16 if n >= 14 else 8)
                    out_unit(U_WOUT1, OUT_LO_FIRST, n - 12)
                elif step == "T":
                    pe.wait_ge(chunk_v, C0["qkv2"] + n + 1)
                    if weights:
                        pe.wait_ge(wT_copied, weights)
                    chunk_T(C0["qkv2"] + n)
                    chunks = n + 1
                elif step == "S":
                    pe.wait_ge(cT_a, C0["qkv2"] + (4 if n >= SB_HEADS // 2 else 2))
                    pe.wait_ge(cT_v, C0["qkv2"] + (4 if n >= SB_HEADS // 2 else 2))
                    if n >= 2:
                        pe.wait_ge(z_masked, n - 1)
                    q = slice(SB_DH * (n % 2), SB_DH * (n % 2 + 1))
                    scores(n, qkT[q, n // 2, :], qkT[q, KB + n // 2, :]).then_inc(z_ready, 1)
                elif step == "W":
                    pe.wait_ge(z_w, n + 1)
                    pe.wait_ge(cT_a, C0["qkv2"] + chunks)
                    pe.wait_ge(cT_v, C0["qkv2"] + chunks)
                    if n >= 2:
                        pe.wait_ge(wT_copied, n - 1)
                    weights_T(n, stick_z[:, n % 4, :]).then_inc(wT_ready, 1)
                    weights = n + 1
                elif step == "V":
                    pe.wait_ge(v_a, 4)
                    pe.wait_ge(v_v, 4)
                    pe.wait_ge(wT_copied, SB_HEADS if n >= 12 else n + 1)
                    if n >= 8:
                        pe.wait_ge(z_masked, SB_HEADS)
                    f = slice(n // 2 * P, (n // 2 + 1) * P)
                    weighted(o_bank[n // 2][:, TOK * (n % 2):TOK * (n % 2 + 1)], stick_wT[:, n, :], vtok[:, 0, f],
                             vtok[:, 1, f]).then_inc(so_ready, 1)
            ada_sums(1, 10, 12)
            pe.wait_ge(ada_out, 24)
            keep_warm(12)
            swiglu(1)


_INPUTS = [
    "x", "norm_mix_pre", "norm_mix_post", "norm_ffn_pre", "norm_ffn_post", "w_up", "w_down", "attn_w_qkv", "attn_w_o",
    "c_2", "l0_ada_w_2", "l0_ada_b_2", "l0_mix_norm_2", "l0_w_in_2", "l0_conv_a_w_2", "l0_conv_b_w_2",
    "l0_conv_b_b_2", "l0_rg_a_w_2", "l0_rg_a_b_2", "l0_rg_x_w_2", "l0_rg_x_b_2", "l0_rg_lambda_2", "l0_w_out_2",
    "l0_ffn_norm_2", "l0_ffn_w_gate_2", "l0_ffn_w_up_2", "l0_ffn_w_down_2", "l1_ada_w_2", "l1_ada_b_2",
    "l1_mix_norm_2", "l1_w_qkv_2", "l1_q_norm_2", "l1_k_norm_2", "l1_w_out_2", "l1_ffn_norm_2",
    "l1_ffn_w_gate_2", "l1_ffn_w_up_2", "l1_ffn_w_down_2",
]


def kernel(**inputs):
    import numpy as np
    import concourse.bacc as bacc
    from concourse.bass_utils import run_bass_kernel_spmd

    nc = bacc.Bacc("TRN2", target_bir_lowering=False, num_devices=1)
    arrays, args = {}, {}
    for name in _INPUTS:
        arr = np.ascontiguousarray(inputs[name])
        arrays[f"in_{name}"] = arr
        args[name] = nc.dram_tensor(f"in_{name}", arr.shape, mybir.dt.from_np(arr.dtype), kind="ExternalInput").ap()
    out = nc.dram_tensor("out", (1, TOK, D), F32, kind="ExternalOutput").ap()
    block_program(nc, args, out)
    return run_bass_kernel_spmd(nc, [arrays], core_ids=[0]).results[0]["out"]
```

```python
from contextlib import ExitStack

import concourse.bass as bass
from concourse import mybir

F32 = mybir.dt.float32
F32R = mybir.dt.float32r
ALU = mybir.AluOpType
ACT = mybir.ActivationFunctionType
AX = mybir.AxisListType

P = 128
TOK = 256
NT = TOK // P
D = 1024
KB = D // P
CH = 512
HALF = 256
UNIT = 2048
LO_V = 1024
EPS = 1e-6
NEG = -1e30

HEADS = 8
DH = D // HEADS
SB_HEADS = 16
SB_DH = D // SB_HEADS
LRU = 512
LB = LRU // P
LRU_HEAD = 64
RG_C = 8.0
F_MLP = 4096
F_SG = 2816
NJ_MLP = F_MLP // CH
NJ_SG = F_SG // 256
SC = P + TOK

U_QKV1 = 0
U_WO1 = U_QKV1 + 12
U_MLP = U_WO1 + 4
U_WIN = U_MLP + 4 * NJ_MLP
U_WOUT0 = U_WIN + 10
U_SG0 = U_WOUT0 + 4
U_QKV2 = U_SG0 + 3 * NJ_SG
U_WOUT1 = U_QKV2 + 12
U_SG1 = U_WOUT1 + 4
U_END = U_SG1 + 3 * NJ_SG

R_CONV_A, R_CONV_B, R_CONV_BIAS, R_RG_A, R_RG_X, R_LAMBDA, N_ROWS = 0, 3, 7, 8, 9, 10, 11


def steps(text):
    return [(s[0], int(s[1:])) for s in text.split()]


ATT_STEPS = steps("""L1 U0 H2 L2 U1 H3 E0 L3 U2 H4 T0 L4 U3 H5 L5 E1 X0 U4 H6 L6 Y0 U5 H7 E2 S0 L7 U6 H8 A0 S1 L8
    U7 H9 E3 L9 W0 A1 S2 U8 H10 W1 L10 A2 S3 U9 H11 E4 W2 L11 A3 S4 U10 H12 W3 L12 A4 S5
    U11 E5 A5 W4 S6 V0 V1 V2 V3 S7 W5 H13 L13 A6 A7 U12 W6 W7 V4 V5 V6 V7 H14 L14 U13 H15 L15
    U14 H16 L16 U15""")
STICK_STEPS = steps("""U0 H2 L2 U1 E0 H3 L3 N0 U2 H4 L4 T0 U3 E1 H5 L5 N1 U4 H6 L6 T1 U5 E2 H7 S0 S1 L7 A0 A1 N2
    U6 H8 F0 F1 S2 S3 L8 A2 A3 U7 W0 W1 E3 H9 F2 F3 S4 S5 T2 L9 A4 A5 N3 U8 H10 W2 W3 F4 F5 S6 S7 L10 A6 A7 F6
    U9 T3 F7 E4 H11 W4 W5 S8 S9 W6 W7 S10 L11 A8 A9 A10 F8 F9 F10 U10 H12 W8 W9 S11 S12 W10 S13 L12 A11 A12 F11
    U11 E5 A13 F12 H13 W11 W12 V0 V1 V2 V3 V4 V5 V6 V7 F13 W13 S14 S15 L13 A14 A15 F14 F15
    U12 W14 V8 V9 W15 V10 V11 H14 V12 V13 V14 V15 L14 U13 H15 L15 U14 H16 U15""")
LRU_STEPS = steps("""B0 B1 U0 H2 L2 U1 H3 E0 L3 M0 U2 H4 T0 L4 C0 B2 B3 U3 H5 E1 L5 M1 U4 H6 G0 L6 B4 M2 U5 H7 G1 D0 E2 B5 L7 M3
    U6 H8 B6 M4 L8 D1 U7 H9 L9 B7 Q0 E3 P0 U8 H10 Y0 L10 R0 J0 M5 U9 H11 E4 L11 K0 U10 H12 L12 Z0 M6
    U11 H13 L13 M7 U12 H14 U13""")
ADA_ORDER = (0, 1, 2, 3, 10, 11, 4, 5, 6, 7, 8, 9), (0, 1, 2, 3, 4, 5, 6, 7, 8, 9, 10, 11)
QKV_CHUNKS = (0, 2, 1, 3, 4, 5)
WIN_CHUNKS = (4, 3, 1, 2, 0)
OUT_LO_FIRST = ((0, 0), (1, 0), (0, 1), (1, 1))
OUT_HI_FIRST = ((0, 1), (1, 1), (0, 0), (1, 0))


def plus(base, i, per):
    return base if i is None else i * per + base


def block_program(nc, a, out):
    ctx = ExitStack()
    with ctx:
        def sb(name, shape, dt=F32):
            return ctx.enter_context(nc.sbuf_tensor(name, shape, dt))

        def ps(name, shape):
            return ctx.enter_context(nc.psum_tensor(name, shape, F32))

        def sem(name):
            return ctx.enter_context(nc.semaphore(name))

        w_raw = sb("w_raw", [P, 2, UNIT])
        w_hi = sb("w_hi", [P, 2, UNIT], F32R)
        w_lo = sb("w_lo", [P, 2, UNIT], F32R)
        ada_raw = sb("ada_raw", [P, 3, UNIT])
        mod = sb("mod", [P, 6 * D])
        gate_ffn = sb("gate_ffn", [P, D])
        x = sb("x", [P, NT, D])
        xn = sb("xn", [P, NT, D])
        aT_hi = sb("aT_hi", [P, KB, TOK], F32R)
        aT_lo = sb("aT_lo", [P, KB, TOK], F32R)
        hT_hi = sb("hT_hi", [P, 4, TOK], F32R)
        hT_lo = sb("hT_lo", [P, 4, TOK], F32R)
        gain = sb("gain", [P, 4, D])
        qk_gain = sb("qk_gain", [P, 2])
        scratch = sb("scratch", [P, 10240])
        ident = sb("ident", [P, P])
        ones = sb("ones", [P, P])
        zeros = sb("zeros", [P, CH], F32R)
        neg_dist = sb("neg_dist", [P, SC])
        sb_mask = sb("sb_mask", [P, SC])
        cols = sb("cols", [P, LB, 16])
        silu_c = sb("silu_c", [P, KB])
        rg_w = sb("rg_w", [P, 2, LB, P])
        lam = sb("lam", [P, 10, LB])
        sums = sb("sums", [P, 2])
        var = sb("var", [P, 2])
        rstd = sb("rstd", [P, 2])
        half = sb("half", [P, 1])
        eps = sb("eps", [P, 1])
        qk_ss = sb("qk_ss", [P, 16])
        qk_rstd = sb("qk_rstd", [P, 16])
        att_max = sb("att_max", [P, 4, 2])
        att_nmax = sb("att_nmax", [P, 4, 2])
        att_sum = sb("att_sum", [P, 4, 2])
        att_rsum = sb("att_rsum", [P, 4, 2])

        tokbuf = scratch[:, 0:2048].rearrange("p (c t n) -> p c t n", c=2, t=NT)
        qkT = scratch[:, 2048:6144].rearrange("p (b n) -> p b n", n=TOK)
        vtok = scratch[:, 6144:8192].rearrange("p (t n) -> p t n", t=NT)
        uT = scratch[:, 2048:7168].rearrange("p (b n) -> p b n", n=TOK)
        prob = scratch[:, 8192:8192 + 4 * SC].rearrange("p (r n) -> p r n", r=4)
        ada_slot = [ada_raw[:, 0, :], ada_raw[:, 1, :], scratch[:, 0:UNIT]]
        ada_flat = ada_raw[:, :, :].rearrange("p a n -> p (a n)")
        probT = ada_flat[:, 0:HEADS * SC].rearrange("p (h n) -> p h n", h=HEADS)
        rows = scratch[0:N_ROWS, 8192:8192 + LRU]
        c_rows = scratch[0:KB, 8192 + LRU:8192 + LRU + P]
        xn_flat = xn[:, :, :].rearrange("p t n -> p (t n)")
        stick_z = scratch[:, 8192:8192 + 4 * SC].rearrange("p (r n) -> p r n", r=4)
        stick_wT = ada_flat[:, 0:SB_HEADS * SC].rearrange("p (h n) -> p h n", h=SB_HEADS)
        stick_sp = gain[:, 0, 0:2 * SC].rearrange("p (r n) -> p r n", r=2)
        stick_sum = gain[:, 1, 0:2 * SC].rearrange("p (r n) -> p r n", r=2)
        qk_sq = xn_flat[:, 0:1024].rearrange("p (h d) -> p h d", d=SB_DH)
        def lru_buf(ap):
            return ap.rearrange("p (b n) -> p b n", n=TOK)
        conv_a = lru_buf(ada_raw[:, 2, 0:1024])
        xr = lru_buf(ada_raw[:, 2, 1024:2048])
        gate_r = lru_buf(scratch[:, 7168:8192])
        gate_i = lru_buf(scratch[:, 8192:9216])
        lru_b = lru_buf(scratch[:, 9216:10240])
        lru_a = lru_buf(xn_flat[:, 0:1024])
        lru_h = lru_buf(xn_flat[:, 1024:2048])
        hbuf = scratch[:, 0:1024].rearrange("p (b n) -> p b n", n=TOK)
        gbuf = scratch[:, 1024:2048].rearrange("p (b n) -> p b n", n=TOK)
        squares = scratch[:, 0:2048].rearrange("p (t n) -> p t n", t=NT)

        acc = ps("acc", [P, 4, CH])
        ub = ps("ub", [P, 2, CH])
        tp = ps("tp", [P, 2, CH])
        o_bank = [acc[:, b, :] for b in range(4)] + [ub[:, 0, :], ub[:, 1, :], tp[:, 0, :], tp[:, 1, :]]

        def hidden_banks(first):
            return tp[:, :, :] if first else ub[:, :, :]

        def acc_tile(t):
            return acc[:, 2 * t:2 * t + 2, :].rearrange("p b n -> p (b n)")

        def hT_blocks(last):
            return slice(2, 4) if last else slice(0, 2)

        def chunk_banks(ct):
            return acc[:, 2:4, :] if ct == T0["qkv2"] + 3 else tp[:, :, :]

        def blocks_of(banks):
            return banks.rearrange("p a (b n) -> p b a n", n=TOK)

        NORMS_T = 1, 3, 5

        def norm_banks(k, t):
            if k in NORMS_T:
                return [acc[:, 2 * t, :], acc[:, 2 * t + 1, :]]
            return [ub[:, 0, :], ub[:, 1, :]] if t else [tp[:, 0, :], tp[:, 1, :]]

        x_loaded = [sem("x_loaded0"), sem("x_loaded1")]
        rows_loaded = sem("rows_loaded")
        small_loaded = sem("small_loaded")
        gain_loaded = [sem(f"gain_loaded{n}") for n in range(8)]
        w_loaded = [sem("w_loaded0"), sem("w_loaded1")]
        hi_done = sem("hi_done")
        lo_v_done = sem("lo_v_done")
        lo_p_done = sem("lo_p_done")
        w_used = sem("w_used")
        tile0_done = sem("tile0_done")
        ada_loaded = [sem(f"ada_loaded{n}") for n in range(3)]
        ada_bias = sem("ada_bias")
        ada_used = sem("ada_used")
        ada_sum = sem("ada_sum")
        ada_out = sem("ada_out")
        ada_gain_done = sem("ada_gain_done")
        consts = sem("consts")
        pool_chain = sem("pool_chain")
        dve_chain = sem("dve_chain")
        act_chain = sem("act_chain")
        cols_T = sem("cols_T")
        cols_done = sem("cols_done")
        lam_exp = sem("lam_exp")
        lam_done = sem("lam_done")
        hi0_done = sem("hi0_done")
        sq_done = sem("sq_done")
        rstd_done = sem("rstd_done")
        xn_done = sem("xn_done")
        nT_done = sem("nT_done")
        n_hi = sem("n_hi")
        n_lo = sem("n_lo")
        x_ready = sem("x_ready")
        chunk_a = sem("chunk_a")
        chunk_v = sem("chunk_v")
        cT0 = sem("cT0")
        cT1 = sem("cT1")
        cT_a = sem("cT_a")
        cT_v = sem("cT_v")
        v_a = sem("v_a")
        v_v = sem("v_v")
        qk_sq_done = sem("qk_sq_done")
        qk_ss_done = sem("qk_ss_done")
        qk_rstd_done = sem("qk_rstd_done")
        s_ready = sem("s_ready")
        s_max = sem("s_max")
        s_exp = sem("s_exp")
        s_norm = sem("s_norm")
        pT_ready = sem("pT_ready")
        pT_copied = sem("pT_copied")
        o_ready = sem("o_ready")
        o_hi = sem("o_hi")
        o_lo = sem("o_lo")
        z_ready = sem("z_ready")
        z_masked = sem("z_masked")
        z_log = sem("z_log")
        z_cum = sem("z_cum")
        z_arg = sem("z_arg")
        z_w = sem("z_w")
        wT_ready = sem("wT_ready")
        wT_copied = sem("wT_copied")
        so_ready = sem("so_ready")
        so_hi = sem("so_hi")
        so_lo = sem("so_lo")
        act_h = sem("act_h")
        h_ready = sem("h_ready")
        hT_hi_done = sem("hT_hi_done")
        hT_lo_done = sem("hT_lo_done")
        lru_p = sem("lru_p")
        lru_conv = sem("lru_conv")
        lru_xr = sem("lru_xr")
        lru_gate = sem("lru_gate")
        lru_r = sem("lru_r")
        lru_gelu = sem("lru_gelu")
        lru_u = sem("lru_u")
        lru_tap = sem("lru_tap")
        lru_i = sem("lru_i")
        lru_t = sem("lru_t")
        lru_ix = sem("lru_ix")
        lru_a2 = sem("lru_a2")
        lru_s2 = sem("lru_s2")
        lru_sqrt = sem("lru_sqrt")
        lru_ya = sem("lru_ya")
        lru_yb = sem("lru_yb")
        y_hi = sem("y_hi")
        y_lo = sem("y_lo")
        stored = sem("stored")

        def blocks(w):
            return w.rearrange("(k p) n -> p k n", p=P)
        qkv1, wo1, up1, down1 = (blocks(a[n][0]) for n in ("attn_w_qkv", "attn_w_o", "w_up", "w_down"))
        w_in, w_out0 = blocks(a["l0_w_in_2"]), blocks(a["l0_w_out_2"])
        qkv2, w_out1 = blocks(a["l1_w_qkv_2"]), blocks(a["l1_w_out_2"])
        sg = [[blocks(a[f"l{n}_ffn_w_{m}_2"]) for m in ("gate", "up", "down")] for n in (0, 1)]
        ada_w = [blocks(a[f"l{n}_ada_w_2"]) for n in (0, 1)]
        ada_b = [a[f"l{n}_ada_b_2"].rearrange("(a n) -> a n", a=1) for n in (0, 1)]
        gains = [a["norm_mix_pre"][0], a["norm_mix_post"][0], a["norm_ffn_pre"][0], a["norm_ffn_post"][0],
                 a["l0_mix_norm_2"], a["l0_ffn_norm_2"], a["l1_mix_norm_2"], a["l1_ffn_norm_2"]]

        H0 = {"mlp": 0, 0: NJ_MLP, 1: NJ_MLP + NJ_SG}
        C0 = {"qkv1": 0, "win": 4, "qkv2": 5}
        T0 = {"qkv1": 0, "win": 1, "qkv2": 2}
        SG_U = (U_SG0, U_SG1)

        block = ctx.enter_context(nc.Block())

        @block.sync
        def _(sp):
            def load_unit(u, pieces, i=None, per=0):
                if u >= 2:
                    sp.wait_ge(lo_v_done, plus(u - 1, i, per))
                    sp.wait_ge(lo_p_done, plus(u - 1, i, per))
                for dst, src in pieces:
                    sp.dma_start(dst, src).then_inc(w_loaded[u % 2], 16)

            def proj_half(u, w, col, h, i=None, per=0):
                dst = w_raw[:, u % 2, :].rearrange("p (k n) -> p k n", n=CH)
                load_unit(u, [(dst[:, 2 * q:2 * q + 2, :],
                               w[:, 4 * h + 2 * q:4 * h + 2 * q + 2, bass.ds(col, CH)]) for q in range(2)], i, per)

            def proj(u, w, col, i=None, per=0):
                for h in range(2):
                    proj_half(u + h, w, col, h, i, per)

            def project_out(u, w, order):
                for n, (c, h) in enumerate(order):
                    proj_half(u + n, w, c * CH, h)

            def down(u, w, row_block, i=None, per=0):
                dst = w_raw[:, u % 2, :].rearrange("p (k n) -> p k n", n=D)
                load_unit(u, [(dst[:, q:q + 1, :], w[:, bass.ds(row_block + q, 1), :]) for q in range(2)], i, per)

            def proj_T_half(u, w, col, i=None, per=0):
                dst = w_raw[:, u % 2, :].rearrange("p (k n) -> p k n", n=HALF)
                load_unit(u, [(dst[:, 4 * q:4 * q + 4, :], w[:, 4 * q:4 * q + 4, bass.ds(col, HALF)])
                              for q in range(2)], i, per)

            def proj_T(u, w, col, i=None, per=0):
                for h in range(2):
                    proj_T_half(u + h, w, col + HALF * h, i, per)

            def gate_up(u, layer, col, i=None, per=0):
                for m in range(2):
                    proj_T_half(u + m, sg[layer][m], col, i, per)

            def load_ada(slot, rb, cols_of, count, before=None, i=None, per=0):
                if before is not None:
                    sp.wait_ge(ada_used, plus(before, i, per))
                layer, third = cols_of
                src = ada_w[layer][:, bass.ds(rb, 1), third * UNIT:(third + 1) * UNIT]
                sp.dma_start(ada_raw[:, slot:slot + 1, :], src).then_inc(ada_loaded[slot], 16)

            def load_gain(n):
                sp.dma_start(gain[:, n % 4, :], gains[n].partition_broadcast(P)).then_inc(gain_loaded[n], 16)

            def load_x(t):
                sp.dma_start(x[:, t, :], a["x"][0, t * P:(t + 1) * P, :]).then_inc(x_loaded[t], 16)

            load_x(0)
            load_gain(0)
            proj_half(U_QKV1, qkv1, 0, 0)
            load_x(1)
            proj_half(U_QKV1 + 1, qkv1, 0, 1)
            proj_T_half(U_QKV1 + 2, qkv1, QKV_CHUNKS[1] * CH)
            proj_T_half(U_QKV1 + 3, qkv1, QKV_CHUNKS[1] * CH + HALF)
            vectors = [(rows[R_CONV_A:R_CONV_A + 3, :], a["l0_conv_a_w_2"]),
                       (rows[R_CONV_B:R_CONV_B + 4, :], a["l0_conv_b_w_2"]),
                       (rows[R_CONV_BIAS:R_CONV_BIAS + 1, :], a["l0_conv_b_b_2"].rearrange("(a n) -> a n", a=1)),
                       (rows[R_RG_A:R_RG_A + 1, :], a["l0_rg_a_b_2"].rearrange("(a h) n -> a (h n)", a=1)),
                       (rows[R_RG_X:R_RG_X + 1, :], a["l0_rg_x_b_2"].rearrange("(a h) n -> a (h n)", a=1)),
                       (rows[R_LAMBDA:R_LAMBDA + 1, :], a["l0_rg_lambda_2"].rearrange("(a n) -> a n", a=1)),
                       (c_rows[:, :], a["c_2"].rearrange("a (k p) -> (a k) p", p=P))]
            for dst, src in vectors:
                sp.dma_start(dst, src).then_inc(rows_loaded, 16)
            small = []
            for g, name in enumerate(("l1_q_norm_2", "l1_k_norm_2")):
                for e in range(2):
                    small.append((qk_gain[SB_DH * e:SB_DH * (e + 1), g:g + 1], a[name].rearrange("(p a) -> p a", a=1)))
            sp.wait_ge(consts, 1)
            for g, name in enumerate(("l0_rg_a_w_2", "l0_rg_x_w_2")):
                for e in range(2):
                    q = slice(LRU_HEAD * e, LRU_HEAD * (e + 1))
                    small.append((rg_w[q, g, :, q], a[name].rearrange("(b e) i j -> e i b j", e=2)[e]))
            for c in range(2, 6):
                (proj_T if c < 4 else proj)(U_QKV1 + 2 * c, qkv1, QKV_CHUNKS[c] * CH)
                for dst, src in small[4 * (c - 2):4 * (c - 1)]:
                    sp.dma_start(dst, src).then_inc(small_loaded, 16)
            load_gain(1)
            load_gain(2)
            load_gain(3)
            project_out(U_WO1, wo1, OUT_LO_FIRST)
            proj_T(U_MLP, up1, 0)
            sp.wait_ge(o_ready, HEADS)
            for third in range(3):
                load_ada(third, 0, (0, third), third)
            with sp.Fori(0, NJ_MLP - 1) as i:
                u = U_MLP + 2
                proj_T(u, up1, i * CH + CH, i, 4)
                load_ada(0, i + 1, (0, 0), 3, 1, i, 3)
                down(u + 2, down1, i * 4, i, 4)
                load_ada(1, i + 1, (0, 1), 4, 2, i, 3)
                down(u + 3, down1, i * 4 + 2, i, 4)
                load_ada(2, i + 1, (0, 2), 5, 3, i, 3)
            for h in range(2):
                down(U_WIN - 2 + h, down1, 4 * (NJ_MLP - 1) + 2 * h)
            sp.wait_ge(xn_done, 8)
            load_gain(4)
            load_gain(5)
            proj(U_WIN, w_in, WIN_CHUNKS[0] * CH)
            proj_T(U_WIN + 2, w_in, WIN_CHUNKS[1] * CH)
            for c in range(2, 5):
                proj_T(U_WIN + 2 * c, w_in, WIN_CHUNKS[c] * CH)
            project_out(U_WOUT0, w_out0, OUT_HI_FIRST)
            load_gain(6)
            sp.wait_ge(x_ready, 4)
            load_gain(7)

            def swiglu(layer):
                u = SG_U[layer]
                gate_up(u, layer, 0)
                def pair(i, base, with_ada):
                    for q in range(2):
                        v = u + 2 + 3 * (base - 1 + q)
                        gate_up(v, layer, plus(256 * (base + q), i, 512), i, 6)
                        if with_ada:
                            load_ada(0, plus(q, i, 2), (1, 1), 32 + 2 * q, 31 + 2 * q, i, 4)
                        down(v + 2, sg[layer][2], plus(2 * (base - 1 + q), i, 4), i, 6)
                        if with_ada:
                            load_ada(1, plus(q, i, 2), (1, 2), 33 + 2 * q, 32 + 2 * q, i, 4)

                with sp.Fori(0, 4) as i:
                    pair(i, 1, layer == 0)
                pair(None, 9, False)
                down(u + 3 * NJ_SG - 1, sg[layer][2], 2 * (NJ_SG - 1))

            swiglu(0)
            for c in range(6):
                proj(U_QKV2 + 2 * c, qkv2, QKV_CHUNKS[c] * CH)
            project_out(U_WOUT1, w_out1, OUT_LO_FIRST)
            swiglu(1)
            parts = ((0, slice(0, D)), (1, slice(0, CH)), (1, slice(CH, D)))
            for n, (t, c) in enumerate(parts):
                sp.wait_ge(x_ready, 11 + n)
                sp.dma_start(out[0, t * P:(t + 1) * P, c], x[:, t, c]).then_inc(stored, 16)
            sp.wait_ge(stored, 16 * len(parts))

        @block.gpsimd
        def _(pool):
            n_chain = [0]

            def chained(ins):
                n_chain[0] += 1
                ins.then_inc(pool_chain, 1)
                pool.wait_ge(pool_chain, n_chain[0])

            def split_lo(u, i=None, per=0):
                if u >= U_END:
                    return
                pool.wait_ge(hi_done, plus(u + 1, i, per))
                if u == 0:
                    pool.wait_ge(hi0_done, 1)
                s = u % 2
                pool.tensor_tensor(w_lo[:, s, LO_V:], w_raw[:, s, LO_V:], w_hi[:, s, LO_V:].bitcast(F32),
                                   ALU.subtract).then_inc(lo_p_done, 1)

            def splits(u0, u1):
                for u in range(u0, u1):
                    split_lo(u)

            def start_sums(layer, c0, c1):
                chained(pool.memset(mod[:, c0:c1], 0.0))
                pool.dma_start(mod[0:1, c0:c1], ada_b[layer][:, c0:c1]).then_inc(ada_bias, 16)

            n_rstd = [0]

            def row_rstd(u=None):
                for t in range(NT):
                    if u is not None and t == 1:
                        split_lo(u)
                    n_rstd[0] += 1
                    pool.wait_ge(sq_done, n_rstd[0])
                    chained(pool.tensor_scalar(var[:, t:t + 1], sums[:, t:t + 1], 1.0 / D, EPS, ALU.mult, ALU.add))
                    pool.tensor_tensor(rstd[:, t:t + 1], var[:, t:t + 1], half[:, 0:1], ALU.pow).then_inc(rstd_done, 1)

            chained(pool.memset(half[:, :], -0.5))
            pool.memset(eps[:, :], EPS)
            chained(pool.memset(ident[:, :], 0.0))
            chained(pool.affine_select(out=ident[:, :], in_=ident[:, :], compare_op=ALU.not_equal, fill=1.0,
                                       base=0, pattern=[[-1, P]], channel_multiplier=1))
            pool.memset(rg_w[:, :, :, :], 0.0).then_inc(consts, 1)
            row_rstd(U_QKV1)
            splits(1, 2)
            pool.memset(ones[:, :], 1.0).then_inc(consts, 1)
            pool.memset(zeros[:, :].bitcast(F32), 0.0).then_inc(consts, 1)
            chained(pool.iota(neg_dist[:, 0:P], pattern=[[1, P]], base=0, channel_multiplier=-1,
                              allow_small_or_imprecise_dtypes=True))
            chained(pool.iota(neg_dist[:, P:SC], pattern=[[1, TOK]], base=-P, channel_multiplier=-1,
                              allow_small_or_imprecise_dtypes=True))
            chained(pool.memset(sb_mask[:, :], 0.0))
            for m, keep_diag in ((neg_dist, 0), (sb_mask, -1)):
                for lo, n, q0 in ((0, P, 0), (P, TOK, P)):
                    part = m[:, lo:lo + n]
                    pool.affine_select(out=part, in_=part, compare_op=ALU.is_ge, fill=NEG, base=q0 + keep_diag,
                                       pattern=[[-1, n]], channel_multiplier=1).then_inc(consts, 1)
            for step, n in ATT_STEPS:
                if step == "H" and n < 16:
                    split_lo(U_QKV1 + n)
                elif step == "E" and n < 3:
                    start_sums(0, n * UNIT, (n + 1) * UNIT)
            row_rstd(U_MLP)
            row_rstd()
            splits(U_MLP + 1, U_MLP + 3)
            with pool.Fori(0, NJ_MLP - 1) as i:
                for q in range(4):
                    split_lo(U_MLP + 3 + q, i, 4)
            splits(U_MLP + 3 + 4 * (NJ_MLP - 1), U_WIN)
            split_lo(U_WIN)
            row_rstd()
            row_rstd()
            splits(U_WIN + 1, U_WIN + 2)
            pool.wait_ge(xn_done, 12)
            start_sums(1, 0, UNIT)
            for step, n in LRU_STEPS:
                if step == "H" and n < 14:
                    split_lo(U_WIN + n)
                elif step == "P":
                    pool.wait_ge(lru_u, 2)
                    pool.tensor_tensor(uT[:, 4:8, :], uT[:, 4:8, :], uT[:, 8:12, :], ALU.mult).then_inc(lru_p, 1)
                elif step == "D" and n == 0:
                    pool.wait_ge(lru_i, 1)
                    pool.wait_ge(lru_xr, 1)
                    pool.tensor_tensor(gate_i, gate_i, xr, ALU.mult).then_inc(lru_ix, 1)

            def swiglu(layer):
                u = SG_U[layer]
                split_lo(u)
                row_rstd()
                if layer == 0:
                    splits(u + 1, u + 2)
                    pool.wait_ge(xn_done, 16)
                    start_sums(1, UNIT, 3 * UNIT)
                    split_lo(u + 2)
                else:
                    splits(u + 1, u + 3)
                with pool.Fori(0, 4) as i:
                    for q in range(6):
                        split_lo(u + 3 + q, i, 6)
                splits(u + 3 + 24, u + 3 * NJ_SG)

            swiglu(0)
            split_lo(U_QKV2)
            row_rstd()
            splits(U_QKV2 + 1, U_QKV2 + 2)
            for step, n in STICK_STEPS:
                if step == "H" and n < 16:
                    split_lo(U_QKV2 + n)
                elif step == "A":
                    pool.wait_ge(z_cum, n + 1)
                    z = stick_z[:, n % 4, :]
                    pool.tensor_tensor(z, z, stick_sum[:, n % 2, :], ALU.subtract).then_inc(z_arg, 1)
            swiglu(1)

        @block.scalar
        def _(act):
            n_chain = [0]

            def chained(ins):
                n_chain[0] += 1
                ins.then_inc(act_chain, 1)
                act.wait_ge(act_chain, n_chain[0])

            def split_hi(u, i=None, per=0):
                if u >= U_END:
                    return
                act.wait_ge(w_loaded[u % 2], plus(32 * (u // 2 + 1), i, 16 * per))
                if u >= 2:
                    act.wait_ge(w_used, plus(u - 1, i, per))
                c = slice(0, LO_V if u == 0 else UNIT)
                act.activation(w_hi[:, u % 2, c], w_raw[:, u % 2, c], ACT.Copy).then_inc(hi_done, 1)

            def splits(u0, u1):
                for u in range(u0, u1):
                    split_hi(u)

            def row_square(t, src):
                act.activation(squares[:, t, :], src, ACT.Square, accum_out=sums[:, t:t + 1]).then_inc(sq_done, 1)

            n_norm, n_update = [0], [0]

            def norm(u, layer=None, parts=(0, 0, 0, 0)):
                k = n_norm[0]
                n_norm[0] += 1
                ada_parts(layer, parts[0], parts[1])
                for t in range(NT):
                    if k == 0:
                        act.wait_ge(x_loaded[t], 16)
                    else:
                        act.wait_ge(x_ready, 2 * (k - 1) + t + 1)
                    row_square(t, x[:, t, :])
                    ada_parts(layer, parts[1 + t], parts[2 + t])
                    if k in (0, 4) and t == 0:
                        norm_hi(k, 0, u if k == 0 else None)
                if k not in (0, 4):
                    norm_hi(k, 0)
                if k in NORMS_T:
                    norm_hi(k, 1)
                    split_hi(u + 1)
                else:
                    split_hi(u + 1)
                    norm_hi(k, 1)

            def norm_hi(k, t, u=None):
                for g in range(2):
                    if u is not None and g == 1:
                        split_hi(u)
                    act.wait_ge(nT_done, 4 * k + 2 * t + g + 1)
                    act.activation(aT_hi[:, 4 * g:4 * g + 4, t * P:(t + 1) * P],
                                   norm_banks(k, t)[g].rearrange("p (b n) -> p b n", n=P), ACT.Copy).then_inc(n_hi, 1)

            def post_norm(n, u_end):
                act.wait_ge(tile0_done, n + 1)
                row_square(0, acc_tile(0))
                act.wait_ge(w_used, u_end)
                row_square(1, acc_tile(1))

            def ada_parts(layer, n0, n1):
                for n in range(n0, n1):
                    c = ADA_ORDER[layer][n]
                    if layer and c == 10:
                        act.wait_ge(x_ready, 8)
                    act.wait_ge(ada_sum, 12 * layer + n + 1)
                    dst = mod[:, c * CH:(c + 1) * CH] if c < 10 else gate_ffn[:, (c - 10) * CH:(c - 9) * CH]
                    act.activation(dst, ub[:, n % 2, :], ACT.Copy).then_inc(ada_out, 1)

            def copy_chunk(u, bank, ct):
                act.wait_ge(w_used, u + 2)
                if ct >= 2:
                    act.wait_ge(cT1, ct - 1)
                act.activation(tokbuf[:, ct % 2, 0, :], bank, ACT.Copy).then_inc(chunk_a, 1)

            def copy_features(u, bank, dst, b, func=ACT.Copy):
                act.wait_ge(w_used, u + 2)
                act.activation(dst[:, b:b + 3:2, :], bank.rearrange("p (b n) -> p b n", n=TOK), func).then_inc(cT_a, 1)

            def copy_T(dst, ct, b, scale=1.0):
                act.wait_ge(cT0, ct + 1)
                act.activation(dst[:, b:b + 2, :], chunk_banks(ct)[:, 0, :].rearrange("p (b n) -> p b n", n=TOK),
                               ACT.Copy, scale=scale).then_inc(cT_a, 1)

            def copy_v(u, n):
                act.wait_ge(w_used, u + 2)
                act.activation(vtok[:, 0, n * CH:(n + 1) * CH], acc[:, 2 * n, :], ACT.Copy).then_inc(v_a, 1)

            norm(U_QKV1)
            for step, n in ATT_STEPS:
                if step == "H":
                    split_hi(U_QKV1 + n)
                elif step == "X":
                    act.wait_ge(cols_T, 1)
                    act.activation(cols[:, :, 0:N_ROWS], ub[:, 0, 0:64].rearrange("p (b r) -> p b r", r=16)[:, :, 0:N_ROWS],
                                   ACT.Copy).then_inc(cols_done, 1)
                    act.activation(silu_c[:, :], ub[:, 0, 64:64 + KB], ACT.Silu).then_inc(cols_done, 1)
                    act.wait_ge(cols_done, 1)
                    chained(act.activation(lam[:, 0, :], cols[:, :, R_LAMBDA], ACT.Abs))
                    act.activation(lam[:, 1, :], lam[:, 0, :], ACT.Exp, scale=-1.0).then_inc(lam_exp, 1)
                elif step == "E" and n == 0:
                    copy_chunk(U_QKV1, acc[:, 0, :], T0["qkv1"])
                elif step == "E" and n < 4:
                    copy_features(U_QKV1 + 2 * n, acc[:, 2 * (n % 2), :], qkT, 4 * QKV_CHUNKS[n])
                elif step == "E":
                    copy_v(U_QKV1 + 2 * n, n - 4)
                elif step == "T":
                    copy_T(qkT, T0["qkv1"], 4 * QKV_CHUNKS[n])
                elif step == "A":
                    act.wait_ge(s_max, n + 1)
                    r = n % 4
                    for t, lo, w in ((0, 0, P), (1, P, TOK)):
                        act.activation(prob[:, r, lo:lo + w], prob[:, r, lo:lo + w], ACT.Exp, scale=DH ** -0.5,
                                       bias=att_nmax[:, r, t:t + 1], accum_out=att_sum[:, r, t:t + 1]).then_inc(s_exp, 1)
                elif step == "W":
                    act.wait_ge(pT_ready, n + 1)
                    act.activation(probT[:, n, :], tp[:, n % 2, 0:SC], ACT.Copy).then_inc(pT_copied, 1)
                elif step == "V":
                    act.wait_ge(o_ready, n + 1)
                    act.activation(aT_hi[:, n, :], o_bank[n][:, 0:TOK], ACT.Copy).then_inc(o_hi, 1)
            post_norm(0, U_MLP)
            norm(U_MLP)

            def mlp_slice(u, j, i=None, first=False):
                if not first:
                    split_hi(u + 1, i, 4)
                split_hi(u + 2, i, 4)
                if not first:
                    split_hi(u + 3, i, 4)
                act.wait_ge(w_used, plus(u + 2, i, 4))
                if j >= 1:
                    act.wait_ge(h_ready, plus(j, i, 1))
                act.activation(gbuf.rearrange("p (b a) n -> p b a n", a=2), blocks_of(hidden_banks(first)), ACT.Relu).then_inc(act_h, 1)
                if not first:
                    split_hi(u + 4, i, 4)
                    act.wait_ge(w_used, plus(u + 4, i, 4))
                act.wait_ge(act_h, plus(j + 1, i, 1))
                act.activation(hT_hi[:, :, :], gbuf, ACT.Square).then_inc(hT_hi_done, 1)

            mlp_slice(U_MLP, 0, first=True)
            with act.Fori(0, NJ_MLP - 1) as i:
                mlp_slice(U_MLP + 2, 1, i)
            ada_parts(0, 0, 4)
            splits(U_WIN - 1, U_WIN + 1)
            post_norm(1, U_WIN)
            norm(U_WIN, 0, (4, 6, 10, 12))
            for step, n in LRU_STEPS:
                if step == "H":
                    split_hi(U_WIN + n)
                elif step == "B":
                    if n == 2:
                        act.wait_ge(cT1, T0["win"] + 1)
                    if n >= 3:
                        act.wait_ge(ada_used, 24 + n - 2)
                    act.dma_start(ada_slot[n % 3], ada_w[1][:, n, 0:UNIT]).then_inc(ada_loaded[n % 3], 16)
                elif step == "E" and n == 1:
                    act.wait_ge(w_used, U_WIN + 4)
                    b = 4 * WIN_CHUNKS[n]
                    act.activation(uT[:, b:b + 4, :].rearrange("p (b a) n -> p b a n", a=2), blocks_of(acc[:, 2:4, :]),
                                   ACT.Gelu_apprx_tanh).then_inc(lru_gelu, 1)
                    act.preload_act_table_set("sigmoid_and_others")
                elif step == "E" and n == 0:
                    copy_chunk(U_WIN, acc[:, 0, :], T0["win"])
                elif step == "E":
                    act.wait_ge(w_used, U_WIN + 2 * n + 2)
                    b = 4 * WIN_CHUNKS[n]
                    banks = ub[:, :, :] if n == 4 else acc[:, 2 * (n % 2):2 * (n % 2) + 2, :]
                    act.activation(uT[:, b:b + 4, :].rearrange("p (b a) n -> p b a n", a=2), blocks_of(banks),
                                   ACT.Copy).then_inc(lru_u, 1)
                elif step == "J":
                    act.wait_ge(lru_p, 1)
                    for b in range(LB):
                        last = act.activation(conv_a[:, b, :], uT[:, 4 + b, :], ACT.Copy,
                                              scale=cols[:, b, R_CONV_A + 2:R_CONV_A + 3])
                    last.then_inc(lru_tap, 1)
                elif step == "T":
                    copy_T(uT, T0["win"], 4 * WIN_CHUNKS[n])
                elif step == "G":
                    dst, row, done = ((gate_r, R_RG_A, lru_r), (gate_i, R_RG_X, lru_i))[n]
                    act.wait_ge(lru_gate, n + 1)
                    for b in range(LB):
                        last = act.activation(dst[:, b, :], ub[:, b // 2, (b % 2) * TOK:(b % 2 + 1) * TOK],
                                              ACT.Sigmoid, bias=cols[:, b, row:row + 1])
                    last.then_inc(done, 1)
                elif step == "D" and n == 0:
                    act.wait_ge(lam_done, 1)
                    act.wait_ge(lru_r, 1)
                    for b in range(LB):
                        last = act.activation(lru_b[:, b, :], gate_r[:, b, :], ACT.Tanh, scale=lam[:, 8, b:b + 1])
                    last.then_inc(lru_t, 1)
                elif step == "D":
                    for b in range(LB):
                        last = act.activation(lru_a[:, b, :], gate_r[:, b, :], ACT.Exp, scale=lam[:, 9, b:b + 1])
                    chained(last)
                    act.activation(gate_r, lru_a, ACT.Square).then_inc(lru_a2, 1)
                elif step == "Q":
                    act.wait_ge(lru_s2, 1)
                    act.activation(lru_b, lru_b, ACT.Sqrt).then_inc(lru_sqrt, 1)
                elif step == "R":
                    act.wait_ge(lru_yb, 1)
                    act.activation(hT_hi[:, :, :], lru_h, ACT.Copy).then_inc(y_hi, 1)
                elif step == "Z":
                    act.wait_ge(lru_ya, 1)
                    act.activation(aT_hi[:, 0:LB, :], conv_a, ACT.Copy).then_inc(y_hi, 1)
            norm(U_SG0, 1, (0, 0, 2, 4))

            def swiglu(layer):
                u, j0 = SG_U[layer], H0[layer]

                def one(v, j, i=None, first=False, last=False):
                    if not first:
                        split_hi(v + 1, i, 6)
                    split_hi(v + 2, i, 6)
                    act.wait_ge(w_used, plus(v + 2, i, 6))
                    act.wait_ge(hT_lo_done, plus(j0 + j, i, 2))
                    act.activation(gbuf[:, 0:2, :], hidden_banks(first)[:, :, 0:TOK], ACT.Silu).then_inc(act_h, 1)
                    if not first:
                        split_hi(v + 3, i, 6)
                        if not last:
                            act.wait_ge(w_used, plus(v + 3, i, 6))
                    act.wait_ge(h_ready, plus(j0 + j + 1, i, 2))
                    act.activation(hT_hi[:, hT_blocks(last), :], hbuf[:, 0:2, :], ACT.Copy).then_inc(hT_hi_done, 1)

                one(u, 0, first=True)
                with act.Fori(0, 4) as i:
                    for q in range(2):
                        one(u + 2 + 3 * q, 1 + q, i)
                for q in range(2):
                    one(u + 2 + 3 * (8 + q), 9 + q, last=q == 1)
                split_hi(u + 3 * NJ_SG)

            swiglu(0)
            ada_parts(1, 4, 6)
            norm(U_QKV2, 1, (6, 6, 8, 10))
            act.wait_ge(small_loaded, 16 * 8)
            act.preload_act_table_set("natural_log_exp_and_others")
            for step, n in STICK_STEPS:
                if step == "H":
                    split_hi(U_QKV2 + n)
                elif step == "E" and n < 4:
                    act.wait_ge(w_used, U_QKV2 + 2 * n + 2)
                    if n >= 1:
                        act.wait_ge(qk_ss_done, n)
                    act.activation(qk_sq, acc[:, 2 * (n % 2):2 * (n % 2) + 2, :].rearrange("p t (h d) -> p (t h) d", d=SB_DH),
                                   ACT.Square).then_inc(qk_sq_done, 1)
                elif step == "E":
                    copy_v(U_QKV2 + 2 * n, n - 4)
                elif step == "N":
                    act.wait_ge(qk_ss_done, n + 1)
                    chained(act.activation(qk_rstd[:, :], qk_ss[:, :], ACT.Ln, scale=1.0 / SB_DH, bias=eps[:, 0:1]))
                    act.activation(qk_rstd[:, :], qk_rstd[:, :], ACT.Exp, scale=-0.5).then_inc(qk_rstd_done, 1)
                elif step == "T":
                    copy_T(qkT, T0["qkv2"] + n, 4 * QKV_CHUNKS[n], qk_gain[:, n % 2:n % 2 + 1])
                elif step == "S":
                    act.wait_ge(z_masked, n + 1)
                    buf = stick_sp[:, n % 2, :]
                    if n >= 2:
                        act.wait_ge(z_cum, n - 1)
                    chained(act.activation(buf, stick_z[:, n % 4, :], ACT.Abs))
                    chained(act.activation(buf, buf, ACT.Exp, scale=-1.0))
                    act.activation(buf, buf, ACT.Ln, bias=1.0).then_inc(z_log, 1)
                elif step == "F":
                    act.wait_ge(z_arg, n + 1)
                    act.activation(stick_z[:, n % 4, :], stick_z[:, n % 4, :], ACT.Exp).then_inc(z_w, 1)
                elif step == "V":
                    act.wait_ge(so_ready, n // 2 * 2 + 2)
                    b, q = n // 2, slice(SB_DH * (n % 2), SB_DH * (n % 2 + 1))
                    act.activation(aT_hi[q, b, :], o_bank[b][q, TOK * (n % 2):TOK * (n % 2 + 1)], ACT.Copy).then_inc(so_hi, 1)
            norm(U_SG1, 1, (10, 10, 12, 12))
            swiglu(1)

        @block.vector
        def _(dve):
            n_chain = [0]

            def chained(ins):
                n_chain[0] += 1
                ins.then_inc(dve_chain, 1)
                dve.wait_ge(dve_chain, n_chain[0])

            def split_lo(u, i=None, per=0):
                if u >= U_END:
                    return
                dve.wait_ge(hi_done, plus(u + 1, i, per))
                s = u % 2
                dve.tensor_tensor(w_lo[:, s, 0:LO_V], w_raw[:, s, 0:LO_V], w_hi[:, s, 0:LO_V].bitcast(F32),
                                  ALU.subtract).then_inc(lo_v_done, 1)

            def splits(u0, u1):
                for u in range(u0, u1):
                    split_lo(u)

            def bank_lo(dst, hi, bank):
                return dve.tensor_tensor(dst, bank, hi.bitcast(F32), ALU.subtract)

            n_norm, n_rstd = [0], [0]

            def norm_scale(t, g):
                chained(dve.tensor_tensor(xn[:, t, :], x[:, t, :], g, ALU.mult))

            def norm_rows(t, g, shift):
                n_rstd[0] += 1
                dve.wait_ge(rstd_done, n_rstd[0])
                src, op, by = (x[:, t, :], ALU.mult, g) if shift is None else (xn[:, t, :], ALU.add, shift)
                for g in range(2):
                    c = slice(g * CH, (g + 1) * CH)
                    dve.scalar_tensor_tensor(xn[:, t, c], src[:, c], rstd[:, t:t + 1], by[:, c], ALU.mult,
                                             op).then_inc(xn_done, 1)

            def norm_lo(t, q):
                k = n_norm[0]
                n_norm[0] += t * q
                dve.wait_ge(n_hi, 4 * k + 2 * t + q + 1)
                part = (slice(None), slice(4 * q, 4 * q + 4), slice(t * P, (t + 1) * P))
                bank_lo(aT_lo[part], aT_hi[part], norm_banks(k, t)[q].rearrange("p (b n) -> p b n", n=P)).then_inc(n_lo, 1)

            def norm_rest(g, shift):
                if n_norm[0] in NORMS_T:
                    norm_rows(1, g, shift)
                    norm_lo(0, 0)
                else:
                    norm_lo(0, 0)
                    norm_rows(1, g, shift)
                norm_lo(0, 1)
                norm_lo(1, 0)
                norm_lo(1, 1)

            def post_norm_scale(t, g):
                n_rstd[0] += 1
                dve.wait_ge(sq_done, n_rstd[0])
                chained(dve.tensor_tensor(xn[:, t, :], acc_tile(t), g, ALU.mult))

            def post_norm_add(t, n):
                dve.wait_ge(rstd_done, n)
                dve.scalar_tensor_tensor(x[:, t, :], xn[:, t, :], rstd[:, t:t + 1], x[:, t, :], ALU.mult,
                                         ALU.add).then_inc(x_ready, 1)

            def post_norm(n, g_post, g, shift):
                post_norm_scale(0, g_post)
                post_norm_add(0, n_rstd[0])
                if shift is not None:
                    dve.wait_ge(x_ready, 2 * n + 1)
                    norm_scale(0, g)
                post_norm_scale(1, g_post)
                post_norm_add(1, n_rstd[0])
                norm_rows(0, g, shift)
                if shift is not None:
                    dve.wait_ge(x_ready, 2 * n + 2)
                    norm_scale(1, g)
                norm_rest(g, shift)

            def columns(n):
                return slice(0, D) if n is None else slice(n * CH, (n + 1) * CH)

            def gate(t, g, n=None):
                part = columns(n)
                chained(dve.tensor_tensor(xn[:, t, part], acc_tile(t)[:, part], g[:, part], ALU.mult))

            def add_gated(t, n=None):
                part = columns(n)
                return dve.tensor_tensor(x[:, t, part], x[:, t, part], xn[:, t, part], ALU.add)

            def gated(t, g, n=None):
                gate(t, g, n)
                return add_gated(t, n)

            def gated_norm(n, u_end, g_mod, halves, g=None, shift=None):
                if halves:
                    dve.wait_ge(w_used, u_end - 1)
                    for t in range(NT):
                        gated(t, g_mod, 0)
                    split_lo(u_end)
                half_n = 1 if halves else None
                dve.wait_ge(tile0_done, n + 1)
                gated(0, g_mod, half_n).then_inc(x_ready, 1)
                if g is not None:
                    dve.wait_ge(x_ready, 2 * n + 1)
                    norm_scale(0, g)
                dve.wait_ge(w_used, u_end)
                if g is None:
                    for c in range(2):
                        gated(1, g_mod, c).then_inc(x_ready, 1)
                    return
                gate(1, g_mod, half_n)
                if n_norm[0] in NORMS_T:
                    add_gated(1, half_n).then_inc(x_ready, 1)
                norm_rows(0, g, shift)
                if n_norm[0] not in NORMS_T:
                    add_gated(1, half_n).then_inc(x_ready, 1)
                dve.wait_ge(x_ready, 2 * n + 2)
                norm_scale(1, g)
                norm_rest(g, shift)

            def ada(slot, loads, third, col, before, i=None, per=0, step=0, src=None):
                dve.wait_ge(ada_loaded[slot], plus(16 * loads, i, 16 * step))
                if before:
                    dve.wait_ge(ada_used, plus(before, i, per))
                part = mod[:, third * UNIT:(third + 1) * UNIT]
                dve.scalar_tensor_tensor(part, ada_raw[:, slot, :] if src is None else src, silu_c[:, bass.ds(col, 1)], part,
                                         ALU.mult, ALU.add).then_inc(ada_used, 1)

            def ada_gain(layer, c, out):
                dve.wait_ge(ada_out, out)
                g = 4 + 2 * layer + (c == 4)
                dve.wait_ge(gain_loaded[g], 16)
                part = mod[:, c * D:(c + 1) * D]
                dve.scalar_tensor_tensor(part, part, 1.0, gain[:, g % 4, :], ALU.add, ALU.mult).then_inc(ada_gain_done, 1)

            SH_M, G_M, GATE_M, SH_F, G_F = (mod[:, c * D:(c + 1) * D] for c in range(5))

            def copy_chunk(u, bank, ct):
                dve.wait_ge(w_used, u + 2)
                if ct >= 2:
                    dve.wait_ge(cT1, ct - 1)
                dve.tensor_copy(tokbuf[:, ct % 2, 1, :], bank).then_inc(chunk_v, 1)

            def copy_features(u, bank, dst, b):
                dve.wait_ge(w_used, u + 2)
                dve.tensor_copy(dst[:, b + 1:b + 4:2, :], bank.rearrange("p (b n) -> p b n", n=TOK)).then_inc(cT_v, 1)

            def copy_T(dst, ct, b, scale=1.0):
                dve.wait_ge(cT1, ct + 1)
                dve.tensor_scalar(dst[:, b + 2:b + 4, :], chunk_banks(ct)[:, 1, :].rearrange("p (b n) -> p b n", n=TOK), scale, None,
                                  ALU.mult).then_inc(cT_v, 1)

            def copy_v(u, n):
                dve.wait_ge(w_used, u + 2)
                dve.tensor_copy(vtok[:, 1, n * CH:(n + 1) * CH], acc[:, 2 * n + 1, :]).then_inc(v_v, 1)

            dve.wait_ge(gain_loaded[0], 16)
            for t in range(NT):
                dve.wait_ge(x_loaded[t], 16)
                norm_rows(t, gain[:, 0, :], None)
                if t == 0:
                    dve.wait_ge(w_loaded[0], 32)
                    dve.tensor_copy(w_hi[:, 0, LO_V:], w_raw[:, 0, LO_V:]).then_inc(hi0_done, 1)
                    split_lo(U_QKV1)
                norm_lo(t, 0)
                norm_lo(t, 1)
            def lambda_columns():
                dve.wait_ge(lam_exp, 1)
                e, s, s2, q, m = (lam[:, n, :] for n in (1, 3, 4, 5, 6))
                chained(dve.tensor_scalar(lam[:, 2, :], e, 2.0, None, ALU.add))
                chained(dve.reciprocal(lam[:, 2, :], lam[:, 2, :]))
                chained(dve.tensor_tensor(s, e, lam[:, 2, :], ALU.mult))
                chained(dve.tensor_tensor(s2, s, s, ALU.mult))
                chained(dve.tensor_scalar(q, s2, 1.0 / 19.0, None, ALU.mult))
                for n in range(8, 0, -1):
                    chained(dve.scalar_tensor_tensor(q, q, 1.0 / (2 * n + 1), s2, ALU.add, ALU.mult))
                chained(dve.scalar_tensor_tensor(q, q, 1.0, s, ALU.add, ALU.mult))
                chained(dve.tensor_scalar(m, cols[:, :, R_LAMBDA], -1.0, 0.0, ALU.mult, ALU.max))
                chained(dve.scalar_tensor_tensor(q, q, 2.0, m, ALU.mult, ALU.add))
                chained(dve.tensor_scalar(lam[:, 8, :], q, RG_C, None, ALU.mult))
                dve.tensor_scalar(lam[:, 9, :], q, -RG_C, None, ALU.mult).then_inc(lam_done, 1)

            def att_max_of(h):
                r = h % 4
                dve.wait_ge(s_ready, h + 1)
                if h >= 4:
                    dve.wait_ge(pT_ready, h - 3)
                slope = 2.0 ** (-8.0 * (h + 1) / HEADS)
                chained(dve.scalar_tensor_tensor(prob[:, r, :], neg_dist[:, :], slope * DH ** 0.5, ub[:, h % 2, 0:SC],
                                                 ALU.mult, ALU.add))
                dve.reduce_max(att_max[:, r, 0:1], prob[:, r, 0:P], AX.X)
                chained(dve.reduce_max(att_max[:, r, 1:2], prob[:, r, P:SC], AX.X))
                dve.tensor_scalar(att_nmax[:, r, :], att_max[:, r, :], -DH ** -0.5, None, ALU.mult).then_inc(s_max, 1)

            def att_norm(h):
                r = h % 4
                dve.wait_ge(s_exp, 2 * h + 2)
                chained(dve.reciprocal(att_rsum[:, r, :], att_sum[:, r, :]))
                for t, lo, n in ((0, 0, P), (1, P, TOK)):
                    dve.tensor_scalar(prob[:, r, lo:lo + n], prob[:, r, lo:lo + n], att_rsum[:, r, t:t + 1], None,
                                      ALU.mult).then_inc(s_norm, 1)

            for step, n in ATT_STEPS:
                if step == "L":
                    split_lo(U_QKV1 + n)
                elif step == "Y":
                    lambda_columns()
                elif step == "E" and n == 0:
                    copy_chunk(U_QKV1, acc[:, 1, :], T0["qkv1"])
                elif step == "E" and n < 4:
                    copy_features(U_QKV1 + 2 * n, acc[:, 2 * (n % 2) + 1, :], qkT, 4 * QKV_CHUNKS[n])
                elif step == "E":
                    copy_v(U_QKV1 + 2 * n, n - 4)
                elif step == "T":
                    copy_T(qkT, T0["qkv1"], 4 * QKV_CHUNKS[n])
                elif step == "S":
                    if n == 0:
                        dve.wait_ge(consts, 7)
                    att_max_of(n)
                elif step == "A":
                    att_norm(n)
                elif step == "V":
                    dve.wait_ge(o_hi, n + 1)
                    bank_lo(aT_lo[:, n, :], aT_hi[:, n, :], o_bank[n][:, 0:TOK]).then_inc(o_lo, 1)
            dve.wait_ge(gain_loaded[1], 16)
            dve.wait_ge(gain_loaded[2], 16)
            post_norm(0, gain[:, 1, :], gain[:, 2, :], None)

            def mlp_slice(u, j, i=None, first=False):
                col = j if i is None else i + 1
                adas = [(t, j + 1, t, col, max(3 * j + t - 2, 0), i, 3, 1) for t in range(3)]
                split_lo(u + 1, i, 4)
                ada(*adas[0])
                split_lo(u + 2, i, 4)
                ada(*adas[1])
                if not first:
                    split_lo(u + 3, i, 4)
                else:
                    ada(*adas[2])
                dve.wait_ge(act_h, plus(j + 1, i, 1))
                dve.tensor_tensor(hbuf, gbuf, gbuf, ALU.mult).then_inc(h_ready, 1)
                if not first:
                    split_lo(u + 4, i, 4)
                    ada(*adas[2])
                dve.wait_ge(h_ready, plus(j + 1, i, 1))
                dve.wait_ge(hT_hi_done, plus(j + 1, i, 1))
                bank_lo(hT_lo[:, :, :], hT_hi[:, :, :], hbuf).then_inc(hT_lo_done, 1)

            dve.wait_ge(cols_done, 2)
            dve.wait_ge(ada_bias, 48)
            mlp_slice(U_MLP, 0, first=True)
            with dve.Fori(0, NJ_MLP - 1) as i:
                mlp_slice(U_MLP + 2, 1, i)
            splits(U_WIN - 1, U_WIN + 1)
            dve.wait_ge(gain_loaded[3], 16)
            ada_gain(0, 1, 4)
            dve.wait_ge(ada_gain_done, 1)
            post_norm(1, gain[:, 3, :], G_M, SH_M)
            split_lo(U_WIN + 1)
            ada_gain(0, 4, 12)

            def conv_last(dst, src, row, width, bias):
                for b in range(LB):
                    ins = dve.tensor_scalar(dst[:, b, :], src[:, b, :], cols[:, b, row + width - 1:row + width],
                                            cols[:, b, bias:bias + 1], ALU.mult, ALU.add)
                chained(ins)

            def conv_taps(dst, src, row, width):
                for s in range(1, width):
                    if s > 1:
                        chained(ins)
                    for b in range(LB):
                        w = cols[:, b, row + width - 1 - s:row + width - s]
                        ins = dve.scalar_tensor_tensor(dst[:, b, s:], src[:, b, :TOK - s], w, dst[:, b, s:],
                                                       ALU.mult, ALU.add)
                return ins

            for step, n in LRU_STEPS:
                if step == "L":
                    split_lo(U_WIN + n)
                elif step == "E" and n == 0:
                    copy_chunk(U_WIN, acc[:, 1, :], T0["win"])
                elif step == "T":
                    copy_T(uT, T0["win"], 4 * WIN_CHUNKS[n])
                elif step == "M":
                    if n == 0:
                        dve.wait_ge(ada_bias, 64)
                    ada(n % 3, 8 + n // 3 + 1, 0, n, 24 + n, src=ada_slot[n % 3])
                elif step == "C":
                    dve.wait_ge(cT_a, C0["win"] + 1)
                    dve.wait_ge(cT_v, C0["win"] + 1)
                    conv_last(xr, uT[:, 16:20, :], R_CONV_B, 4, R_CONV_BIAS)
                    conv_taps(xr, uT[:, 16:20, :], R_CONV_B, 4).then_inc(lru_xr, 1)
                elif step == "K":
                    dve.wait_ge(lru_tap, 1)
                    conv_taps(conv_a, uT[:, 4:8, :], R_CONV_A, 3).then_inc(lru_conv, 1)
                elif step == "D" and n == 1:
                    dve.wait_ge(lru_a2, 1)
                    dve.wait_ge(lru_t, 1)
                    dve.scalar_tensor_tensor(lru_b, gate_r, 1.0, lru_b, ALU.add, ALU.mult).then_inc(lru_s2, 1)
                elif step == "Q":
                    dve.wait_ge(lru_sqrt, 1)
                    dve.wait_ge(lru_ix, 1)
                    chained(dve.tensor_tensor(lru_b, lru_b, gate_i, ALU.mult))
                    for b in range(LB):
                        ins = dve.tensor_tensor_scan(lru_h[:, b, :], lru_a[:, b, :], lru_b[:, b, :], 0.0, ALU.mult, ALU.add)
                    chained(ins)
                elif step == "Y":
                    dve.wait_ge(lru_gelu, 1)
                    dve.tensor_tensor(lru_h, lru_h, uT[:, 12:16, :], ALU.mult).then_inc(lru_yb, 1)
                elif step == "R":
                    dve.wait_ge(lru_yb, 1)
                    dve.wait_ge(y_hi, 1)
                    dve.tensor_tensor(hT_lo[:, :, :], lru_h, hT_hi[:, :, :].bitcast(F32),
                                      ALU.subtract).then_inc(y_lo, 1)
                elif step == "Z":
                    dve.wait_ge(lru_u, 3)
                    dve.wait_ge(lru_conv, 1)
                    dve.tensor_tensor(conv_a, conv_a, uT[:, 0:4, :], ALU.mult).then_inc(lru_ya, 1)
                    dve.wait_ge(y_hi, 2)
                    dve.tensor_tensor(aT_lo[:, 0:LB, :], conv_a, aT_hi[:, 0:LB, :].bitcast(F32),
                                      ALU.subtract).then_inc(y_lo, 1)
            dve.wait_ge(ada_gain_done, 2)
            gated_norm(2, U_SG0, GATE_M, True, G_F, SH_F)

            def swiglu(layer):
                u, j0 = SG_U[layer], H0[layer]

                def one(v, j, i=None, first=False, last=False, kb=None):
                    adas = [] if kb is None else [(t, 12 + kb, 1 + t, plus(kb, i, 2),
                                                   32 + 2 * kb + t, i, 4, 2) for t in range(2)]
                    split_lo(v + 1, i, 6)
                    if adas:
                        ada(*adas[0])
                    split_lo(v + 2, i, 6)
                    if adas:
                        ada(*adas[1])
                    dve.wait_ge(act_h, plus(j0 + j + 1, i, 2))
                    dve.tensor_tensor(hbuf[:, 0:2, :], gbuf[:, 0:2, :], hidden_banks(first)[:, :, TOK:], ALU.mult).then_inc(h_ready, 1)
                    if not first:
                        split_lo(v + 3, i, 6)
                    dve.wait_ge(hT_hi_done, plus(j0 + j + 1, i, 2))
                    b = hT_blocks(last)
                    bank_lo(hT_lo[:, b, :], hT_hi[:, b, :], hbuf[:, 0:2, :]).then_inc(hT_lo_done, 1)

                one(u, 0, first=True)
                if layer == 0:
                    ada_gain(1, 1, 16)
                    dve.wait_ge(ada_bias, 80)
                with dve.Fori(0, 4) as i:
                    for q in range(2):
                        one(u + 2 + 3 * q, 1 + q, i, kb=q if layer == 0 else None)
                for q in range(2):
                    one(u + 2 + 3 * (8 + q), 9 + q, last=q == 1)
                split_lo(u + 3 * NJ_SG)

            swiglu(0)
            dve.wait_ge(ada_gain_done, 3)
            gated_norm(3, U_QKV2, gate_ffn, False, G_M, SH_M)
            split_lo(U_QKV2 + 1)
            ada_gain(1, 4, 22)

            dve.wait_ge(small_loaded, 16 * 8)

            def qk_norm(c):
                src = acc[:, 2 * (c % 2):2 * (c % 2) + 2, :].rearrange("p t (h d) -> p (t h) d", d=SB_DH)
                dst = tokbuf[:, (T0["qkv2"] + c) % 2, :, :].rearrange("p t (h d) -> p (t h) d", d=SB_DH)
                dve.wait_ge(qk_rstd_done, c + 1)
                if c >= 2:
                    dve.wait_ge(cT1, T0["qkv2"] + c - 1)
                dve.tensor_tensor(dst, src, qk_rstd[:, :].unsqueeze(2).broadcast_to([P, 16, SB_DH]),
                                  ALU.mult).then_inc(chunk_v, 1)

            def stick_mask(h):
                dve.wait_ge(z_ready, h + 1)
                if h >= 4:
                    dve.wait_ge(wT_ready, h - 3)
                dve.scalar_tensor_tensor(stick_z[:, h % 4, :], ub[:, h % 2, 0:SC], SB_DH ** -0.5, sb_mask[:, :],
                                         ALU.mult, ALU.add).then_inc(z_masked, 1)

            def stick_sum_of(h):
                z, f, c = stick_z[:, h % 4, :], stick_sp[:, h % 2, :], stick_sum[:, h % 2, :]
                dve.wait_ge(z_log, h + 1)
                chained(dve.scalar_tensor_tensor(f, z, 0.0, f, ALU.max, ALU.add))
                if h >= 2:
                    dve.wait_ge(z_arg, h - 1)
                for lo, n in ((0, P), (P, TOK)):
                    fr = f[:, lo:lo + n][:, ::-1]
                    ins = dve.tensor_tensor_scan(c[:, lo:lo + n][:, ::-1], fr, fr, 0.0, ALU.add, ALU.max)
                ins.then_inc(z_cum, 1)

            for step, n in STICK_STEPS:
                if step == "L":
                    split_lo(U_QKV2 + n)
                elif step == "E" and n < 4:
                    dve.wait_ge(qk_sq_done, n + 1)
                    dve.reduce_sum(qk_ss[:, :], qk_sq, AX.X).then_inc(qk_ss_done, 1)
                elif step == "E":
                    copy_v(U_QKV2 + 2 * n, n - 4)
                elif step == "N":
                    qk_norm(n)
                elif step == "T":
                    copy_T(qkT, T0["qkv2"] + n, 4 * QKV_CHUNKS[n], qk_gain[:, n % 2:n % 2 + 1])
                elif step == "S":
                    stick_mask(n)
                elif step == "A":
                    stick_sum_of(n)
                elif step == "W":
                    dve.wait_ge(wT_ready, n + 1)
                    dve.tensor_copy(stick_wT[:, n, :], tp[:, n % 2, 0:SC]).then_inc(wT_copied, 1)
                elif step == "V":
                    dve.wait_ge(so_hi, n + 1)
                    b, q = n // 2, slice(SB_DH * (n % 2), SB_DH * (n % 2 + 1))
                    bank_lo(aT_lo[q, b, :], aT_hi[q, b, :], o_bank[b][q, TOK * (n % 2):TOK * (n % 2 + 1)]).then_inc(so_lo, 1)
            dve.wait_ge(ada_gain_done, 4)
            gated_norm(4, U_SG1, GATE_M, True, G_F, SH_F)
            swiglu(1)
            dve.wait_ge(ada_out, 24)
            gated_norm(5, U_END, gate_ffn, False)

        @block.tensor
        def _(pe):
            def matmuls(outp, lhs, rhs, start, stop):
                n = len(lhs)
                for k in range(n):
                    (ah, al), (bh, bl) = lhs[k], rhs[k]
                    pe.matmul(outp, ah, bh, start=start and k == 0, stop=False)
                    pe.matmul(outp, ah, bl, start=False, stop=False)
                    last = pe.matmul(outp, al, bh, start=False, stop=stop and k == n - 1)
                return last

            def unit_ready(u, i=None, per=0):
                pe.wait_ge(lo_v_done, plus(u + 1, i, per))
                pe.wait_ge(lo_p_done, plus(u + 1, i, per))

            def project(u, h, bank, i=None, per=0, first=0, operand=None, tile0=False, lo_count=0):
                op_hi, op_lo = operand or (aT_hi[:, 4 * h:4 * h + 4, :], aT_lo[:, 4 * h:4 * h + 4, :])
                unit_ready(u, i, per)
                s = u % 2
                rhs = [(w_hi[:, s, k * CH:(k + 1) * CH], w_lo[:, s, k * CH:(k + 1) * CH]) for k in range(4)]
                if lo_count:
                    for t in range(NT):
                        for k in range(4):
                            for part in range(2):
                                pe.matmul(bank(t), op_hi[:, k, t * P:(t + 1) * P], rhs[k][part],
                                          start=h == first and k == 0 and part == 0, stop=False)
                    pe.wait_ge(y_lo, lo_count)
                    for t in range(NT):
                        for k in range(4):
                            last = pe.matmul(bank(t), op_lo[:, k, t * P:(t + 1) * P], rhs[k][0], start=False,
                                             stop=h != first and k == 3)
                    last.then_inc(w_used, 1)
                    return
                for t in range(NT):
                    q = slice(t * P, (t + 1) * P)
                    lhs = [(op_hi[:, k, q], op_lo[:, k, q]) for k in range(4)]
                    last = matmuls(bank(t), lhs, rhs, h == first, h != first)
                    if tile0 and t == 0:
                        last.then_inc(tile0_done, 1)
                last.then_inc(w_used, 1)

            def down(u, h, i=None, per=0, final=0):
                unit_ready(u, i, per)
                s = u % 2
                for t in range(NT):
                    q = slice(t * P, (t + 1) * P)
                    for n in range(2):
                        for part in (0, 1):
                            if final and t == 0 and n == 0 and part == 1:
                                pe.wait_ge(hT_lo_done, final)
                            for k in range(2):
                                c = slice(k * D + n * CH, k * D + (n + 1) * CH)
                                if part == 0:
                                    pe.matmul(acc[:, 2 * t + n, :], hT_hi[:, 2 * h + k, q], w_hi[:, s, c], start=False, stop=False)
                                    pe.matmul(acc[:, 2 * t + n, :], hT_hi[:, 2 * h + k, q], w_lo[:, s, c], start=False, stop=False)
                                else:
                                    last = pe.matmul(acc[:, 2 * t + n, :], hT_lo[:, 2 * h + k, q], w_hi[:, s, c], start=False,
                                                     stop=bool(final) and k == 1)
                    if final and t == 0:
                        last.then_inc(tile0_done, 1)
                last.then_inc(w_used, 1)

            n_norm = [0]

            def norm_T(k, t):
                for g, bank in enumerate(norm_banks(k, t)):
                    pe.wait_ge(xn_done, 4 * k + 2 * t + g + 1)
                    for b in range(4):
                        last = pe.transpose(bank[:, b * P:(b + 1) * P], xn[:, t, (4 * g + b) * P:(4 * g + b + 1) * P],
                                            ident[:, :])
                    last.then_inc(nT_done, 1)

            def project_T(u, h, banks, i=None, per=0):
                unit_ready(u, i, per)
                s = u % 2
                for f in range(2):
                    lhs = [(w_hi[:, s, c:c + P], w_lo[:, s, c:c + P]) for c in range(f * P, UNIT, HALF)]
                    rhs = [(aT_hi[:, k, :], aT_lo[:, k, :]) for k in range(KB)]
                    last = matmuls(banks[f][:, h * TOK:(h + 1) * TOK], lhs, rhs, True, True)
                last.then_inc(w_used, 1)

            def first_unit(u, banks, ada_parts=0):
                k = n_norm[0]
                n_norm[0] += 1
                norm_T(k, 0)
                pe.wait_ge(hi_done, u + 1)
                s = u % 2
                for t in range(NT):
                    q = slice(t * P, (t + 1) * P)
                    pe.wait_ge(n_hi, 4 * k + 2 * t + 1)
                    for b in range(4):
                        if u == 0 and t == 0 and b == 2:
                            pe.wait_ge(hi0_done, 1)
                        pe.matmul(banks[t], aT_hi[:, b, q], w_hi[:, s, b * CH:(b + 1) * CH], start=b == 0, stop=False)
                    if t == 0:
                        unit_ready(u)
                    for b in range(4):
                        pe.matmul(banks[t], aT_hi[:, b, q], w_lo[:, s, b * CH:(b + 1) * CH], start=False, stop=False)
                    if t == 0:
                        if ada_parts:
                            pe.wait_ge(ada_out, ada_parts)
                        norm_T(k, 1)
                    pe.wait_ge(n_lo, 4 * k + 1 if t == 0 else 4 * k + 3)
                    for b in range(4):
                        last = pe.matmul(banks[t], aT_lo[:, b, q], w_hi[:, s, b * CH:(b + 1) * CH], start=False, stop=False)
                last.then_inc(w_used, 1)
                pe.wait_ge(n_lo, 4 * k + 4)

            def first_unit_T(u, banks):
                k = n_norm[0]
                n_norm[0] += 1
                for t in range(NT):
                    norm_T(k, t)
                unit_ready(u)
                s = u % 2
                for part, done in ((0, n_hi), (1, n_lo)):
                    for g in range(2):
                        pe.wait_ge(done, 4 * k + 3 + g)
                        for f in range(2):
                            outp = banks[f][:, 0:TOK]
                            for b in range(4 * g, 4 * g + 4):
                                c = slice(b * HALF + f * P, b * HALF + (f + 1) * P)
                                if part == 0:
                                    pe.matmul(outp, w_hi[:, s, c], aT_hi[:, b, :], start=b == 0, stop=False)
                                    pe.matmul(outp, w_lo[:, s, c], aT_hi[:, b, :], start=False, stop=False)
                                else:
                                    last = pe.matmul(outp, w_hi[:, s, c], aT_lo[:, b, :], start=False, stop=b == KB - 1)
                last.then_inc(w_used, 1)

            def keep_warm(n):
                for _ in range(n):
                    pe.matmul(ub[:, 0, :], zeros[:, 0:P], zeros[:, :], start=True, stop=True)

            def out_unit(u, order, n, operand=None, lo_count=0):
                c, h = order[n]
                project(u + n, h, lambda t: acc[:, 2 * t + c, :], first=order[0][1], operand=operand, tile0=n == 3,
                        lo_count=lo_count)

            def chunk_T(ct, before):
                if before:
                    pe.wait_ge(cT_a, before)
                    pe.wait_ge(cT_v, before)
                par = ct % 2
                for g, done in enumerate((cT0, cT1)):
                    for b in range(2):
                        for t in range(NT):
                            last = pe.transpose(chunk_banks(ct)[:, g, b * TOK + t * P:b * TOK + (t + 1) * P],
                                                tokbuf[:, par, t, (2 * g + b) * P:(2 * g + b + 1) * P], ident[:, :])
                    last.then_inc(done, 1)

            pe.wait_ge(consts, 1)
            first_unit(U_QKV1, (acc[:, 0, :], acc[:, 1, :]))
            def scores(h, q, k):
                pe.matmul(ub[:, h % 2, 0:P], q[:, 0:P], k[:, 0:P], start=True, stop=True)
                return pe.matmul(ub[:, h % 2, P:SC], q[:, P:TOK], k[:, :], start=True, stop=True)

            def weights_T(h, w):
                for n in range(3):
                    last = pe.transpose(tp[:, h % 2, n * P:(n + 1) * P], w[:, n * P:(n + 1) * P], ident[:, :])
                return last

            def weighted(o, wT, v0, v1):
                pe.matmul(o[:, 0:P], v0, wT[:, 0:P], start=True, stop=True)
                pe.matmul(o[:, P:TOK], v0, wT[:, P:2 * P], start=True, stop=False)
                return pe.matmul(o[:, P:TOK], v1, wT[:, 2 * P:SC], start=False, stop=True)

            weights = chunks = 0
            for step, n in ATT_STEPS:
                if step == "U" and 0 < n < 12:
                    c = n // 2
                    if c >= 2 and n % 2 == 0:
                        pe.wait_ge(cT_a, C0["qkv1"] + c - 1)
                        pe.wait_ge(cT_v, C0["qkv1"] + c - 1)
                    if 1 <= c < 4:
                        project_T(U_QKV1 + n, n % 2, [acc[:, 2 * (c % 2) + p, :] for p in range(2)])
                    else:
                        project(U_QKV1 + n, n % 2, lambda t: acc[:, 2 * (c % 2) + t, :])
                elif step == "U" and n >= 12:
                    pe.wait_ge(o_lo, 8 if n >= 14 else 4)
                    out_unit(U_WO1, OUT_LO_FIRST, n - 12)
                elif step == "X":
                    pe.wait_ge(rows_loaded, 16 * 7)
                    for b in range(LB):
                        pe.transpose(ub[:, 0, 16 * b:16 * b + N_ROWS], rows[:, b * P:(b + 1) * P], ident[0:N_ROWS, 0:N_ROWS])
                    pe.transpose(ub[:, 0, 64:64 + KB], c_rows[:, :], ident[0:KB, 0:KB]).then_inc(cols_T, 1)
                elif step == "T":
                    pe.wait_ge(chunk_a, T0["qkv1"] + 1)
                    pe.wait_ge(chunk_v, T0["qkv1"] + 1)
                    chunk_T(T0["qkv1"], C0["qkv1"])
                    chunks = n + 1
                elif step == "S":
                    if n == 0:
                        pe.wait_ge(cols_done, 2)
                    pe.wait_ge(cT_a, C0["qkv1"] + (4 if n >= HEADS // 2 else 2))
                    pe.wait_ge(cT_v, C0["qkv1"] + (4 if n >= HEADS // 2 else 2))
                    if n >= 2:
                        pe.wait_ge(s_max, n - 1)
                    scores(n, qkT[:, n, :], qkT[:, HEADS + n, :]).then_inc(s_ready, 1)
                elif step == "W":
                    pe.wait_ge(s_norm, 2 * n + 2)
                    pe.wait_ge(cT_a, C0["qkv1"] + chunks)
                    pe.wait_ge(cT_v, C0["qkv1"] + chunks)
                    if n >= 2:
                        pe.wait_ge(pT_copied, n - 1)
                    weights_T(n, prob[:, n % 4, :]).then_inc(pT_ready, 1)
                    weights = n + 1
                elif step == "V":
                    pe.wait_ge(v_a, 2)
                    pe.wait_ge(v_v, 2)
                    pe.wait_ge(pT_copied, HEADS if n >= 6 else n + 1)
                    if n >= 4:
                        pe.wait_ge(s_max, HEADS)
                    f = slice(n * DH, (n + 1) * DH)
                    weighted(o_bank[n][:, 0:TOK], probT[:, n, :], vtok[:, 0, f], vtok[:, 1, f]).then_inc(o_ready, 1)

            def clear_acc():
                for n in range(4):
                    pe.matmul(acc[:, n, :], zeros[:, 0:P], zeros[:, :], start=True, stop=False)

            ub_banks = ub[:, 0, :], ub[:, 1, :]
            tp_banks = tp[:, 0, :], tp[:, 1, :]

            def first_hidden(u):
                first_unit_T(u, tp_banks)
                project_T(u + 1, 1, tp_banks)

            def hidden(u, i, per):
                for h in range(2):
                    project_T(u + h, h, ub_banks, i, per)

            pe.wait_ge(consts, 3)
            keep_warm(16)
            first_hidden(U_MLP)
            clear_acc()
            with pe.Fori(0, NJ_MLP - 1) as i:
                u = U_MLP + 2
                hidden(u, i, 4)
                pe.wait_ge(hT_lo_done, plus(1, i, 1))
                down(u + 2, 0, i, 4)
                down(u + 3, 1, i, 4)
                pe.wait_ge(act_h, plus(2, i, 1))
            def ada_sums(layer, n0, n1):
                for n in range(n0, n1):
                    c, m = ADA_ORDER[layer][n], 12 * layer + n
                    if m >= 2:
                        pe.wait_ge(ada_out, m - 1)
                    pe.matmul(ub[:, n % 2, :], ones[:, :], mod[:, c * CH:(c + 1) * CH], start=True,
                              stop=True).then_inc(ada_sum, 1)

            pe.wait_ge(ada_used, 22)
            ada_sums(0, 0, 4)
            pe.wait_ge(hT_lo_done, NJ_MLP)
            down(U_WIN - 2, 0)
            down(U_WIN - 1, 1, final=NJ_MLP)
            pe.wait_ge(ada_used, 24)
            ada_sums(0, 4, 12)
            first_unit(U_WIN, (acc[:, 0, :], acc[:, 1, :]), 12)
            for step, n in LRU_STEPS:
                if step == "U" and 0 < n < 10:
                    c = n // 2
                    if c == 2:
                        pe.wait_ge(cT_a, C0["win"] + 1)
                        pe.wait_ge(cT_v, C0["win"] + 1)
                    if c == 3:
                        pe.wait_ge(lru_gelu, 1)
                    if c == 4:
                        pe.wait_ge(lru_i, 1)
                    if c == 0:
                        project(U_WIN + n, n % 2, lambda t: acc[:, t, :])
                    else:
                        project_T(U_WIN + n, n % 2, ub_banks if c == 4 else [acc[:, 2 * (c % 2) + p, :] for p in range(2)])
                elif step == "U" and n >= 10:
                    if n == 10:
                        pe.wait_ge(lru_u, 2)
                    y = 1 if n < 12 else 2
                    if n % 2 == 0:
                        pe.wait_ge(y_hi, y)
                    out_unit(U_WOUT0, OUT_HI_FIRST, n - 10, (hT_hi, hT_lo) if n < 12 else None,
                             lo_count=y if n % 2 == 0 else 0)
                elif step == "T":
                    pe.wait_ge(chunk_a, T0["win"] + 1)
                    pe.wait_ge(chunk_v, T0["win"] + 1)
                    chunk_T(T0["win"], C0["win"])
                elif step == "G":
                    pe.wait_ge(small_loaded, 16 * 8)
                    pe.wait_ge(lru_xr, 1)
                    if n == 1:
                        pe.wait_ge(lru_r, 1)
                    for b in range(LB):
                        last = pe.matmul(ub[:, b // 2, (b % 2) * TOK:(b % 2 + 1) * TOK], rg_w[:, n, b, :],
                                         xr[:, b, :], start=True, stop=True)
                    last.then_inc(lru_gate, 1)
            pe.wait_ge(ada_used, 32)
            ada_sums(1, 0, 4)

            def swiglu(layer):
                u, j0 = SG_U[layer], H0[layer]
                first_hidden(u)
                clear_acc()
                pe.wait_ge(ada_out, (16, 24)[layer])

                def one(v, j, i=None):
                    hidden(v, i, 6)
                    pe.wait_ge(hT_lo_done, plus(j0 + j, i, 2))
                    down(v + 2, 0, i, 6)
                    pe.wait_ge(h_ready, plus(j0 + j + 1, i, 2))

                with pe.Fori(0, 4) as i:
                    for q in range(2):
                        one(u + 2 + 3 * q, 1 + q, i)
                for q in range(2):
                    one(u + 2 + 3 * (8 + q), 9 + q)
                if layer == 0:
                    pe.wait_ge(ada_used, 48)
                    ada_sums(1, 4, 6)
                pe.wait_ge(hT_hi_done, j0 + NJ_SG)
                down(u + 3 * NJ_SG - 1, 1, final=j0 + NJ_SG)

            swiglu(0)
            ada_sums(1, 6, 10)
            first_unit(U_QKV2, (acc[:, 0, :], acc[:, 1, :]), 22)
            weights = chunks = 0
            for step, n in STICK_STEPS:
                if step == "U" and 0 < n < 12:
                    c = n // 2
                    if c >= 2 and n % 2 == 0:
                        pe.wait_ge(chunk_v, T0["qkv2"] + min(c, 4) - 1)
                    if n == 10:
                        pe.wait_ge(cT_a, C0["qkv2"] + 4)
                        pe.wait_ge(cT_v, C0["qkv2"] + 4)
                    project(U_QKV2 + n, n % 2, lambda t: acc[:, 2 * (c % 2) + t, :])
                elif step == "U" and n >= 12:
                    pe.wait_ge(so_lo, 16 if n >= 14 else 8)
                    out_unit(U_WOUT1, OUT_LO_FIRST, n - 12)
                elif step == "T":
                    pe.wait_ge(chunk_v, T0["qkv2"] + n + 1)
                    if weights and n < 3:
                        pe.wait_ge(wT_copied, weights)
                    chunk_T(T0["qkv2"] + n, C0["qkv2"] + n)
                    chunks = min(n + 1, 3)
                elif step == "S":
                    pe.wait_ge(cT_a, C0["qkv2"] + (4 if n >= SB_HEADS // 2 else 2))
                    pe.wait_ge(cT_v, C0["qkv2"] + (4 if n >= SB_HEADS // 2 else 2))
                    if n >= 2:
                        pe.wait_ge(z_masked, n - 1)
                    q = slice(SB_DH * (n % 2), SB_DH * (n % 2 + 1))
                    scores(n, qkT[q, n // 2, :], qkT[q, KB + n // 2, :]).then_inc(z_ready, 1)
                elif step == "W":
                    pe.wait_ge(z_w, n + 1)
                    pe.wait_ge(cT_a, C0["qkv2"] + chunks)
                    pe.wait_ge(cT_v, C0["qkv2"] + chunks)
                    if n >= 2:
                        pe.wait_ge(wT_copied, n - 1)
                    weights_T(n, stick_z[:, n % 4, :]).then_inc(wT_ready, 1)
                    weights = n + 1
                elif step == "V":
                    pe.wait_ge(v_a, 4)
                    pe.wait_ge(v_v, 4)
                    pe.wait_ge(wT_copied, SB_HEADS if n >= 12 else n + 1)
                    if n >= 8:
                        pe.wait_ge(z_masked, SB_HEADS)
                    f = slice(n // 2 * P, (n // 2 + 1) * P)
                    weighted(o_bank[n // 2][:, TOK * (n % 2):TOK * (n % 2 + 1)], stick_wT[:, n, :], vtok[:, 0, f],
                             vtok[:, 1, f]).then_inc(so_ready, 1)
            ada_sums(1, 10, 12)
            pe.wait_ge(ada_out, 24)
            keep_warm(12)
            swiglu(1)


_INPUTS = [
    "x", "norm_mix_pre", "norm_mix_post", "norm_ffn_pre", "norm_ffn_post", "w_up", "w_down", "attn_w_qkv", "attn_w_o",
    "c_2", "l0_ada_w_2", "l0_ada_b_2", "l0_mix_norm_2", "l0_w_in_2", "l0_conv_a_w_2", "l0_conv_b_w_2",
    "l0_conv_b_b_2", "l0_rg_a_w_2", "l0_rg_a_b_2", "l0_rg_x_w_2", "l0_rg_x_b_2", "l0_rg_lambda_2", "l0_w_out_2",
    "l0_ffn_norm_2", "l0_ffn_w_gate_2", "l0_ffn_w_up_2", "l0_ffn_w_down_2", "l1_ada_w_2", "l1_ada_b_2",
    "l1_mix_norm_2", "l1_w_qkv_2", "l1_q_norm_2", "l1_k_norm_2", "l1_w_out_2", "l1_ffn_norm_2",
    "l1_ffn_w_gate_2", "l1_ffn_w_up_2", "l1_ffn_w_down_2",
]


def kernel(**inputs):
    import numpy as np
    import concourse.bacc as bacc
    from concourse.bass_utils import run_bass_kernel_spmd

    nc = bacc.Bacc("TRN2", target_bir_lowering=False, num_devices=1)
    arrays, args = {}, {}
    for name in _INPUTS:
        arr = np.ascontiguousarray(inputs[name])
        arrays[f"in_{name}"] = arr
        args[name] = nc.dram_tensor(f"in_{name}", arr.shape, mybir.dt.from_np(arr.dtype), kind="ExternalInput").ap()
    out = nc.dram_tensor("out", (1, TOK, D), F32, kind="ExternalOutput").ap()
    block_program(nc, args, out)
    return run_bass_kernel_spmd(nc, [arrays], core_ids=[0]).results[0]["out"]
```
